# Optimizing a Trainium2 kernel written in Bass

```python
import math
import jax, jax.numpy as jnp
from jax import lax
import numpy as np

D_MODEL = 1024
BATCH = 1
SEQ = 256
DEPTH = 2

MEM_LEN = 256
HEAD_DIM = 64
EPS = 1e-6
A_WIDTH = D_MODEL // 2
A_HEADS = A_WIDTH // HEAD_DIM
MOBA_BLOCK = 256
MOBA_TOPK = 3
MOBA_QCHUNK = 64
B_HEADS = 4
B_VW = D_MODEL // 4
B_DV = B_VW // B_HEADS
B_DK = B_DV // 2
B_KW = B_HEADS * B_DK
GATE_RANK = 16
GATE_TEMP = 16.0
GLA_CHUNK = 64
M_WIDTH = D_MODEL // 4
M_HEADS = 4
M_DH = M_WIDTH // M_HEADS

IN_SPLITS = (A_WIDTH, A_WIDTH, A_WIDTH, A_WIDTH,
             B_KW, B_KW, B_VW, B_VW, GATE_RANK,
             M_WIDTH, M_WIDTH)
IN_PROJ = sum(IN_SPLITS)


def rms_norm(t, g):
    tf = t.astype(jnp.float32)
    y = tf * lax.rsqrt(jnp.mean(tf * tf, axis=-1, keepdims=True) + EPS)
    return (y * g.astype(jnp.float32)).astype(t.dtype)

def split_heads(t, n):
    b, s, w = t.shape
    return t.reshape(b, s, n, w // n).transpose(0, 2, 1, 3)

def merge_heads(t):
    b, h, s, d = t.shape
    return t.transpose(0, 2, 1, 3).reshape(b, s, h * d)

def alibi_slopes(n_heads):
    return jnp.asarray([2.0 ** (-8.0 * (i + 1) / n_heads) for i in range(n_heads)], jnp.float32)

def moba_attention(q, k, v):
    bsz, nh, s, d = q.shape
    nb = -(-s // MOBA_BLOCK)
    sp = nb * MOBA_BLOCK
    pad = ((0, 0), (0, 0), (0, sp - s), (0, 0))
    q, k, v = jnp.pad(q, pad), jnp.pad(k, pad), jnp.pad(v, pad)
    kb = k.reshape(bsz, nh, nb, MOBA_BLOCK, d)
    vb = v.reshape(bsz, nh, nb, MOBA_BLOCK, d)
    kmean = jnp.mean(kb.astype(jnp.float32), axis=3)
    slopes = alibi_slopes(nh)
    scale = d ** -0.5
    nsel = min(MOBA_TOPK, nb)
    n_qc = sp // MOBA_QCHUNK
    qc = q.reshape(bsz, nh, n_qc, MOBA_QCHUNK, d).transpose(2, 0, 1, 3, 4)
    blk_ar = jnp.arange(MOBA_BLOCK, dtype=jnp.int32)
    gather = jax.vmap(jax.vmap(lambda tb, ib: tb[ib]))

    def one_chunk(args):
        qi, c = args
        t0 = c * MOBA_QCHUNK
        qblk = t0 // MOBA_BLOCK
        pos_q = t0 + jnp.arange(MOBA_QCHUNK, dtype=jnp.int32)
        gate = jnp.einsum('bhqd,bhnd->bhqn', qi.astype(jnp.float32), kmean)
        past = jnp.arange(nb, dtype=jnp.int32) < qblk
        gate = jnp.where(past, gate, -jnp.inf)
        _, idx = lax.top_k(gate, nsel)
        valid = idx < qblk
        k_sel = gather(kb, idx)
        v_sel = gather(vb, idx)
        s_past = jnp.einsum('bhqd,bhqjsd->bhqjs', qi, k_sel,
                            preferred_element_type=jnp.float32) * scale
        pos_k_past = idx[..., None] * MOBA_BLOCK + blk_ar
        dist_past = (pos_q[None, None, :, None, None] - pos_k_past).astype(jnp.float32)
        s_past = s_past - slopes[None, :, None, None, None] * dist_past
        s_past = jnp.where(valid[..., None], s_past, -jnp.inf)
        k_own = lax.dynamic_slice_in_dim(kb, qblk, 1, axis=2)[:, :, 0]
        v_own = lax.dynamic_slice_in_dim(vb, qblk, 1, axis=2)[:, :, 0]
        pos_k_own = qblk * MOBA_BLOCK + blk_ar
        dist_own = (pos_q[:, None] - pos_k_own[None, :]).astype(jnp.float32)
        s_own = jnp.einsum('bhqd,bhsd->bhqs', qi, k_own,
                           preferred_element_type=jnp.float32) * scale
        s_own = s_own - slopes[None, :, None, None] * dist_own
        s_own = jnp.where(dist_own >= 0, s_own, -jnp.inf)
        logits = jnp.concatenate([s_past.reshape(bsz, nh, MOBA_QCHUNK, nsel * MOBA_BLOCK), s_own], -1)
        p = jax.nn.softmax(logits, axis=-1).astype(v.dtype)
        p_past = p[..., :nsel * MOBA_BLOCK].reshape(bsz, nh, MOBA_QCHUNK, nsel, MOBA_BLOCK)
        p_own = p[..., nsel * MOBA_BLOCK:]
        return (jnp.einsum('bhqjs,bhqjsd->bhqd', p_past, v_sel)
                + jnp.einsum('bhqs,bhsd->bhqd', p_own, v_own))

    out = lax.map(one_chunk, (qc, jnp.arange(n_qc, dtype=jnp.int32)))
    out = out.transpose(1, 2, 0, 3, 4).reshape(bsz, nh, sp, d)
    return out[:, :, :s]

def gla_attention(q, k, v, log_a):
    bsz, nh, s, dk = q.shape
    dv = v.shape[-1]
    nc = s // GLA_CHUNK

    def to_chunks(t):
        return t.astype(jnp.float32).reshape(bsz, nh, nc, GLA_CHUNK, t.shape[-1]).transpose(2, 0, 1, 3, 4)

    mask = jnp.tril(jnp.ones((GLA_CHUNK, GLA_CHUNK), dtype=bool))

    def step(state, inp):
        qc, kc, vc, gc = inp
        b = jnp.cumsum(gc, axis=-2)
        o_inter = jnp.einsum('bhcd,bhde->bhce', qc * jnp.exp(b), state)
        diff = b[:, :, :, None, :] - b[:, :, None, :, :]
        decay = jnp.exp(jnp.where(mask[None, None, :, :, None], diff, -jnp.inf))
        att = jnp.einsum('bhid,bhjd,bhijd->bhij', qc, kc, decay)
        o_intra = jnp.einsum('bhij,bhje->bhie', att, vc)
        b_last = b[:, :, -1:, :]
        new_state = (jnp.exp(b_last[:, :, 0, :, None]) * state
                     + jnp.einsum('bhcd,bhce->bhde', kc * jnp.exp(b_last - b), vc))
        return new_state, o_inter + o_intra

    state0 = jnp.zeros((bsz, nh, dk, dv), jnp.float32)
    _, out = lax.scan(step, state0, (to_chunks(q), to_chunks(k), to_chunks(v), to_chunks(log_a)))
    out = out.transpose(1, 2, 0, 3, 4).reshape(bsz, nh, s, dv)
    return out.astype(v.dtype)

def mem_attention(q, mk, mv):
    scale = q.shape[-1] ** -0.5
    logits = jnp.einsum('bhqd,bhmd->bhqm', q, mk, preferred_element_type=jnp.float32) * scale
    p = jax.nn.softmax(logits, axis=-1).astype(mv.dtype)
    return jnp.einsum('bhqm,bhmd->bhqd', p, mv)

def first_inputs(seed: int = 0) -> dict:
    key = jax.random.key(seed)
    ks = jax.random.split(key, 16)
    f32 = jnp.float32

    def gain(k, shape):
        return 1.0 + 0.02 * jax.random.normal(k, shape, f32)

    return {
        "x": jax.random.normal(ks[0], (BATCH, SEQ, D_MODEL), f32),
        "mem": jax.random.normal(ks[1], (BATCH, MEM_LEN, D_MODEL), f32),
        "g_pre": gain(ks[2], (DEPTH, D_MODEL)),
        "w_in": jax.random.normal(ks[3], (DEPTH, D_MODEL, IN_PROJ), f32) * D_MODEL ** -0.5,
        "g_q_moba": gain(ks[4], (DEPTH, HEAD_DIM)),
        "g_k_moba": gain(ks[5], (DEPTH, HEAD_DIM)),
        "w_gate_up": jax.random.normal(ks[6], (DEPTH, GATE_RANK, B_KW), f32) * GATE_RANK ** -0.5,
        "b_gate_up": 0.1 * jax.random.normal(ks[7], (DEPTH, B_KW), f32),
        "g_gla_out": gain(ks[8], (DEPTH, B_DV)),
        "g_mem": gain(ks[9], (DEPTH, D_MODEL)),
        "w_mem_kv": jax.random.normal(ks[10], (DEPTH, D_MODEL, 2 * M_WIDTH), f32) * D_MODEL ** -0.5,
        "g_q_mem": gain(ks[11], (DEPTH, M_DH)),
        "g_k_mem": gain(ks[12], (DEPTH, M_DH)),
        "w_out": jax.random.normal(ks[13], (DEPTH, D_MODEL, D_MODEL), f32) * (D_MODEL * 2 * DEPTH) ** -0.5,
    }

def first_block(x, mem, g_pre, w_in, g_q_moba, g_k_moba, w_gate_up, b_gate_up, g_gla_out,
              g_mem, w_mem_kv, g_q_mem, g_k_mem, w_out):
    split_idx = [int(i) for i in np.cumsum(IN_SPLITS)[:-1]]
    for l in range(DEPTH):
        h = rms_norm(x, g_pre[l])
        u = h @ w_in[l]
        (qa, ka, va, ga, qb, kb, vb, gb, rb, qm, gm) = jnp.split(u, split_idx, axis=-1)

        qa_h = rms_norm(split_heads(qa, A_HEADS), g_q_moba[l])
        ka_h = rms_norm(split_heads(ka, A_HEADS), g_k_moba[l])
        oa = merge_heads(moba_attention(qa_h, ka_h, split_heads(va, A_HEADS))) * jax.nn.silu(ga)

        z = rb @ w_gate_up[l] + b_gate_up[l]
        log_a = jax.nn.log_sigmoid(z.astype(jnp.float32)) / GATE_TEMP
        qb_h = split_heads(qb, B_HEADS) * (B_DK ** -0.5)
        ob = gla_attention(qb_h, split_heads(kb, B_HEADS), split_heads(vb, B_HEADS),
                           split_heads(log_a, B_HEADS))
        ob = merge_heads(rms_norm(ob, g_gla_out[l])) * jax.nn.silu(gb)

        mkv = rms_norm(mem, g_mem[l]) @ w_mem_kv[l]
        mk, mv = jnp.split(mkv, 2, axis=-1)
        qm_h = rms_norm(split_heads(qm, M_HEADS), g_q_mem[l])
        mk_h = rms_norm(split_heads(mk, M_HEADS), g_k_mem[l])
        om = merge_heads(mem_attention(qm_h, mk_h, split_heads(mv, M_HEADS))) * jax.nn.silu(gm)

        x = x + jnp.concatenate([oa, ob, om], axis=-1) @ w_out[l]
    return x


CHUNK = 64
N_MIXERS = 2
D_FF = 256 * ((8 * D_MODEL // 3 + 255) // 256)
RMS_EPS = 1e-6
L2_EPS = 1e-6
SC_WIDTH = 3
GDN_HEAD_DIM = 128
GDN_K_HEADS = D_MODEL // 128
GDN_V_HEADS = 2 * GDN_K_HEADS
GDN_KEY_DIM = GDN_K_HEADS * GDN_HEAD_DIM
GDN_VAL_DIM = GDN_V_HEADS * GDN_HEAD_DIM
GDN_CONV_WIDTH = 4
GDN_CONV_DIM = 2 * GDN_KEY_DIM + GDN_VAL_DIM
GDN_IN_DIM = GDN_CONV_DIM + GDN_VAL_DIM + 2 * GDN_V_HEADS
N_SC_LAYERS = (DEPTH + 1) // 2
N_GDN_LAYERS = DEPTH // 2
N_NORMS = 6


def rms_norm_2(x, g):
    xf = x.astype(jnp.float32)
    y = xf * lax.rsqrt(jnp.mean(xf * xf, axis=-1, keepdims=True) + RMS_EPS)
    return (y * g.astype(jnp.float32)).astype(x.dtype)

def causal_depthwise_conv(x, w):
    k, c = w.shape
    return lax.conv_general_dilated(
        x, w[:, None, :].astype(x.dtype), window_strides=(1,), padding=[(k - 1, 0)],
        dimension_numbers=("NWC", "WIO", "NWC"), feature_group_count=c)

def swiglu(x, w_gate_up, w_down):
    gate, up = jnp.split(x @ w_gate_up, 2, axis=-1)
    return (jax.nn.silu(gate) * up) @ w_down

def short_conv_mixer(x, w_in, conv_w, w_out):
    b, c, v = jnp.split(x @ w_in, 3, axis=-1)
    y = b * causal_depthwise_conv(c * v, conv_w)
    return y @ w_out

def l2norm(x):
    return x * lax.rsqrt(jnp.sum(x * x, axis=-1, keepdims=True) + L2_EPS)

def chunk_gated_delta_rule(q, k, v, g, beta):
    bsz, nh, t, dk = q.shape
    dv = v.shape[-1]
    n = t // CHUNK
    q = q * (dk ** -0.5)

    def rs(a):
        return a.reshape(bsz, nh, n, CHUNK, *a.shape[3:])

    q, k, v, g, beta = rs(q), rs(k), rs(v), rs(g), rs(beta)
    g = jnp.cumsum(g, axis=-1)
    k_beta = k * beta[..., None]
    v_beta = v * beta[..., None]
    idx = jnp.arange(CHUNK)
    causal = idx[:, None] >= idx[None, :]
    strict = idx[:, None] > idx[None, :]
    decay = jnp.exp(jnp.where(causal, g[..., :, None] - g[..., None, :], -jnp.inf))
    a = jnp.where(strict, jnp.einsum("bhncd,bhnsd->bhncs", k_beta, k) * decay, 0.0)
    eye = jnp.eye(CHUNK, dtype=q.dtype)
    t_inv = lax.linalg.triangular_solve(eye + a, jnp.broadcast_to(eye, a.shape),
                                        left_side=True, lower=True)
    u = jnp.einsum("bhncs,bhnse->bhnce", t_inv, v_beta)
    w = jnp.einsum("bhncs,bhnsd->bhncd", t_inv, k_beta * jnp.exp(g)[..., None])
    qk = jnp.where(causal, jnp.einsum("bhncd,bhnsd->bhncs", q, k) * decay, 0.0)
    q_g = q * jnp.exp(g)[..., None]
    g_last = g[..., -1]
    k_tail = k * jnp.exp(g_last[..., None] - g)[..., None]

    def step(state, inp):
        q_g_n, qk_n, u_n, w_n, k_tail_n, gl_n = inp
        v_new = u_n - jnp.einsum("bhcd,bhde->bhce", w_n, state)
        o = jnp.einsum("bhcd,bhde->bhce", q_g_n, state) + jnp.einsum("bhcs,bhse->bhce", qk_n, v_new)
        state = state * jnp.exp(gl_n)[..., None, None] + jnp.einsum("bhcd,bhce->bhde", k_tail_n, v_new)
        return state, o

    xs = tuple(jnp.moveaxis(a_, 2, 0) for a_ in (q_g, qk, u, w, k_tail, g_last))
    s0 = jnp.zeros((bsz, nh, dk, dv), dtype=q.dtype)
    _, o = lax.scan(step, s0, xs)
    return jnp.moveaxis(o, 0, 2).reshape(bsz, nh, t, dv)

def gated_deltanet_mixer(x, w_in, conv_w, a_log, dt_bias, norm_w, w_out):
    bsz, t, _ = x.shape
    proj = x @ w_in
    qkv, z, b, a = jnp.split(proj, [GDN_CONV_DIM, GDN_CONV_DIM + GDN_VAL_DIM,
                                    GDN_CONV_DIM + GDN_VAL_DIM + GDN_V_HEADS], axis=-1)
    qkv = jax.nn.silu(causal_depthwise_conv(qkv, conv_w))
    q, k, v = jnp.split(qkv.astype(jnp.float32), [GDN_KEY_DIM, 2 * GDN_KEY_DIM], axis=-1)
    rep = GDN_V_HEADS // GDN_K_HEADS
    q = jnp.repeat(l2norm(q.reshape(bsz, t, GDN_K_HEADS, GDN_HEAD_DIM)), rep, axis=2)
    k = jnp.repeat(l2norm(k.reshape(bsz, t, GDN_K_HEADS, GDN_HEAD_DIM)), rep, axis=2)
    v = v.reshape(bsz, t, GDN_V_HEADS, GDN_HEAD_DIM)
    beta = jax.nn.sigmoid(b.astype(jnp.float32))
    g = -jnp.exp(a_log.astype(jnp.float32)) * jax.nn.softplus(
        a.astype(jnp.float32) + dt_bias.astype(jnp.float32))
    o = chunk_gated_delta_rule(q.transpose(0, 2, 1, 3), k.transpose(0, 2, 1, 3),
                               v.transpose(0, 2, 1, 3), g.transpose(0, 2, 1),
                               beta.transpose(0, 2, 1))
    o = o.transpose(0, 2, 1, 3)
    o = o * lax.rsqrt(jnp.mean(o * o, axis=-1, keepdims=True) + RMS_EPS) * norm_w.astype(jnp.float32)
    o = o * jax.nn.silu(z.astype(jnp.float32).reshape(bsz, t, GDN_V_HEADS, GDN_HEAD_DIM))
    return o.reshape(bsz, t, GDN_VAL_DIM).astype(x.dtype) @ w_out

def second_inputs(seed: int = 0) -> dict:
    key = jax.random.key(seed)
    ks = jax.random.split(key, 16)
    f32 = jnp.float32
    d = D_MODEL
    x = jax.random.normal(ks[0], (BATCH, SEQ, d), f32)
    norm_g = 1.0 + 0.02 * jax.random.normal(ks[1], (DEPTH, N_NORMS, d), f32)
    ffn_w_gate_up = jax.random.normal(ks[2], (DEPTH, 2, d, 2 * D_FF), f32) * d ** -0.5
    ffn_w_down = jax.random.normal(ks[3], (DEPTH, 2, D_FF, d), f32) * D_FF ** -0.5
    sc_w_in = jax.random.normal(ks[4], (N_SC_LAYERS, d, 3 * d), f32) * d ** -0.5
    sc_conv_w = jax.random.normal(ks[5], (N_SC_LAYERS, SC_WIDTH, d), f32) * SC_WIDTH ** -0.5
    sc_w_out = jax.random.normal(ks[6], (N_SC_LAYERS, d, d), f32) * d ** -0.5
    gdn_w_in = jax.random.normal(ks[7], (N_GDN_LAYERS, d, GDN_IN_DIM), f32) * d ** -0.5
    gdn_conv_w = jax.random.normal(ks[8], (N_GDN_LAYERS, GDN_CONV_WIDTH, GDN_CONV_DIM), f32) * GDN_CONV_WIDTH ** -0.5
    gdn_a_log = jnp.log(jax.random.uniform(ks[9], (N_GDN_LAYERS, GDN_V_HEADS), f32, 1.0, 16.0))
    gdn_dt_bias = 1.0 + 0.1 * jax.random.normal(ks[10], (N_GDN_LAYERS, GDN_V_HEADS), f32)
    gdn_norm_w = 1.0 + 0.02 * jax.random.normal(ks[11], (N_GDN_LAYERS, GDN_HEAD_DIM), f32)
    gdn_w_out = jax.random.normal(ks[12], (N_GDN_LAYERS, GDN_VAL_DIM, d), f32) * GDN_VAL_DIM ** -0.5
    return {"x": x, "norm_g": norm_g, "ffn_w_gate_up": ffn_w_gate_up, "ffn_w_down": ffn_w_down,
            "sc_w_in": sc_w_in, "sc_conv_w": sc_conv_w, "sc_w_out": sc_w_out,
            "gdn_w_in": gdn_w_in, "gdn_conv_w": gdn_conv_w, "gdn_a_log": gdn_a_log,
            "gdn_dt_bias": gdn_dt_bias, "gdn_norm_w": gdn_norm_w, "gdn_w_out": gdn_w_out}

def second_block(x, norm_g, ffn_w_gate_up, ffn_w_down, sc_w_in, sc_conv_w, sc_w_out,
              gdn_w_in, gdn_conv_w, gdn_a_log, gdn_dt_bias, gdn_norm_w, gdn_w_out):
    h = x
    for i in range(DEPTH):
        g = norm_g[i]
        ff = swiglu(rms_norm_2(h, g[0]), ffn_w_gate_up[i, 0], ffn_w_down[i, 0])
        h = h + 0.5 * rms_norm_2(ff, g[1])
        m_in = rms_norm_2(h, g[2])
        j = i // N_MIXERS
        if i % N_MIXERS == 0:
            mix = short_conv_mixer(m_in, sc_w_in[j], sc_conv_w[j], sc_w_out[j])
        else:
            mix = gated_deltanet_mixer(m_in, gdn_w_in[j], gdn_conv_w[j], gdn_a_log[j],
                                       gdn_dt_bias[j], gdn_norm_w[j], gdn_w_out[j])
        h = h + rms_norm_2(mix, g[3])
        ff = swiglu(rms_norm_2(h, g[4]), ffn_w_gate_up[i, 1], ffn_w_down[i, 1])
        h = h + 0.5 * rms_norm_2(ff, g[5])
    return h


def setup_inputs(seed=0):
    out = dict(first_inputs(seed))
    for name, value in second_inputs(seed + 1).items():
        if name != "x":
            out[name + "_2"] = value
    return out


def reference(
    x, mem, g_pre, w_in, g_q_moba, g_k_moba, w_gate_up, b_gate_up, g_gla_out, g_mem, w_mem_kv,
    g_q_mem, g_k_mem, w_out, norm_g_2, ffn_w_gate_up_2, ffn_w_down_2, sc_w_in_2, sc_conv_w_2,
    sc_w_out_2, gdn_w_in_2, gdn_conv_w_2, gdn_a_log_2, gdn_dt_bias_2, gdn_norm_w_2, gdn_w_out_2,
):
    x = first_block(
        x, mem, g_pre, w_in, g_q_moba, g_k_moba, w_gate_up, b_gate_up, g_gla_out, g_mem,
        w_mem_kv, g_q_mem, g_k_mem, w_out,
    )
    return second_block(
        x, norm_g_2, ffn_w_gate_up_2, ffn_w_down_2, sc_w_in_2, sc_conv_w_2, sc_w_out_2,
        gdn_w_in_2, gdn_conv_w_2, gdn_a_log_2, gdn_dt_bias_2, gdn_norm_w_2, gdn_w_out_2,
    )


_drawn_inputs = setup_inputs


def setup_inputs(seed=0):
    import zlib

    import numpy as np

    out = dict(_drawn_inputs(seed))
    spreads = {}
    factors = {'g_q_moba': 8.0,
     'g_k_moba': 8.0,
     'b_gate_up': 2.892,
     'g_gla_out': 5.729,
     'g_mem': 8.0,
     'g_q_mem': 8.0,
     'g_k_mem': 8.0,
     'gdn_dt_bias_2': 64.0,
     'gdn_norm_w_2': 35.909,
     'gdn_a_log_2': 8.0}
    for name, (base, spread) in spreads.items():
        noise = np.random.default_rng([zlib.crc32(name.encode()), seed]).standard_normal(out[name].shape)
        drawn = base * np.exp(spread * noise) if base else spread * noise
        out[name] = __import__('jax').numpy.asarray(drawn.astype(out[name].dtype))
    for name, factor in factors.items():
        out[name] = (out[name] * factor).astype(out[name].dtype)
    return out
```

```python
import numpy as np
import concourse.bass as bass
from concourse import mybir
from contextlib import ExitStack

F32 = mybir.dt.float32
F32R = mybir.dt.float32r
BF16 = mybir.dt.bfloat16
U8 = mybir.dt.uint8
ACT = mybir.ActivationFunctionType
ALU = mybir.AluOpType
AX = mybir.AxisListType

P = 128
T = 256
TT = T // P
D = 1024
KT = D // P
EPS = 1e-6
RING = 3
SLOT = 2048
LEAD = 2


class Chain:

    def __init__(self, eng, sem):
        self.eng, self.sem, self.n, self.it, self.per = eng, sem, 0, None, 0

    def mark(self, ins):
        self.n += 1
        ins.then_inc(self.sem, 1)

    def sync(self):
        self.eng.wait_ge(self.sem, self.n if self.it is None else self.it * self.per + self.n)

    def __call__(self, ins):
        self.mark(ins)
        self.sync()

    def enter(self, it, per):
        self.it, self.per, self.start = it, per, self.n

    def leave(self, trips):
        assert self.n - self.start == self.per, (self.n - self.start, self.per)
        self.n = self.start + trips * self.per
        self.it = None


class Signal:

    def __init__(self, sem, base):
        self.sem, self.base = sem, base

    def __call__(self, n):
        return self.sem, self.base + n


class Net:

    def __init__(self, nc, ctx, dram):
        self.nc, self.dram = nc, dram
        self.ctx, self.prefix, self.shared = ctx, "", {}
        self.raw = self.sb("raw", [P, RING, SLOT])
        self.w_hi = self.sb("w_hi", [P, RING, SLOT], F32R)
        self.w_lo = self.sb("w_lo", [P, RING, SLOT], F32R)
        self.x = self.sb("x", [P, TT, D])
        self.x_hi = self.sb("x_hi", [P, KT, T], F32R)
        self.x_lo = self.sb("x_lo", [P, KT, T], F32R)
        self.ident = self.sb("ident", [P, P])
        self.zeros = self.sb("zeros", [P, 512], BF16)
        self.level_f = self.sb("level_f", [P, len(LEVELS), P])
        self.level_u8 = self.sb("level_u8", [P, len(LEVELS), P], U8)
        self.diag_u8 = self.sb("diag_u8", [P, T], U8)
        self.neg_dist = self.sb("neg_dist", [P, P + T])
        self.rows = self.sb("rows", [P, 2, P])
        self.cols = self.sb("cols", [P, 2, P])
        self.row_loads, self.next_row = [], [0, 0]
        self.brow = self.sb("brow", [P, D])
        self.ss = self.sb("ss", [P, TT])
        self.r = self.sb("r", [P, TT])
        self.nr = self.sb("nr", [P, TT])
        self.ss4 = self.sb("ss4", [P, TT, 2])
        self.post_ss = self.sb("post_ss", [P, TT])
        self.post_r = self.sb("post_r", [P, TT])
        self.scratch = self.sb("scratch", [P, D], BF16)
        self.tmp = self.sb("tmp", [P, 2, 512])
        self.A = [self.ps(f"A{i}") for i in range(4)]
        self.G = [self.ps(f"G{i}") for i in range(2)]
        self.M = [self.ps(f"M{i}") for i in range(2)]
        self.raw_full = [self.sem(f"raw_full{i}") for i in range(RING)]
        self.w_hi_ready = self.sem("w_hi_ready")
        self.w_lo_ready = self.sem("w_lo_ready")
        self.unit_used = self.sem("unit_used")
        self.act_chain = self.sem("act_chain")
        self.dve_chain = self.sem("dve_chain")
        self.params = self.sem("params")
        self.rows_clear = self.sem("rows_clear")
        self.rows_turned = self.sem("rows_turned")
        self.cols_ready = self.sem("cols_ready")
        self.consts = self.sem("consts")
        self.x_in = Signal(self.sem("x_in"), 0)
        self.out_done = self.sem("out_done")
        self.sizes = []

    def columns(self, ap, width=P, side=0):
        n, row = ap.shape[0], self.next_row[side]
        for at in range(0, P, width):
            self.row_loads.append((self.rows[row:row + n, side, at:at + width], ap))
        self.next_row[side] += n
        assert self.next_row[side] <= P
        return self.cols[:, side, row:row + n]

    def sb(self, name, shape, dt=F32):
        return self.ctx.enter_context(self.nc.sbuf_tensor(self.prefix + name, shape, dt))

    def ps(self, name):
        return self.ctx.enter_context(self.nc.psum_tensor(name, [P, 512], F32))

    def shared_sem(self, name, total=0):
        if name not in self.shared:
            self.shared[name] = [self.sem(name), 0]
        sem, base = self.shared[name]
        self.shared[name][1] += total
        return Signal(sem, base)

    def sem(self, name):
        return self.ctx.enter_context(self.nc.semaphore(name))


class Walk:
    STEP = 2 * RING

    def __init__(self, net, eng, chain_sem=None):
        self.net, self.eng, self.u, self.it = net, eng, 0, None
        self.chain = Chain(eng, chain_sem) if chain_sem is not None else None

    def at(self, n):
        return n if self.it is None else self.it * self.STEP + n

    def enter(self, it, per=0):
        self.it = it
        if self.chain:
            self.chain.enter(it, per)

    def leave(self, trips):
        self.it = None
        self.u += (trips - 1) * self.STEP
        if self.chain:
            self.chain.leave(trips)

    def load(self, dst_dims, src):
        u, net = self.u, self.net
        if u >= RING or self.it is not None:
            self.eng.wait_ge(net.w_lo_ready, self.at(u - RING + 1))
        k, m = dst_dims[0], dst_dims[-1]
        for piece in range(2):
            if len(dst_dims) == 2:
                assert k % 2 == 0
                dst = net.raw[:, u % RING, piece * k * m // 2:(piece + 1) * k * m // 2]
                dst = dst.rearrange("p (k n) -> p k n", k=k // 2)
                part = src[:, piece * k // 2:(piece + 1) * k // 2, :]
            else:
                dst = net.raw[:, u % RING, 0:k * 2 * m].rearrange("p (k g n) -> p k g n", k=k, g=2)[:, :, piece, :]
                part = src[:, :, piece, :]
            self.eng.dma_start(dst, part).then_inc(net.raw_full[u % RING], 16)
        self.u += 1

    def split_hi(self, half=None):
        net, v, act = self.net, self.u, self.eng
        self.u += half != 0
        if v >= len(net.sizes):
            return
        n = net.sizes[v]
        part = slice(n // 2 if half == 1 else 0, n // 2 if half == 0 else n)
        full = 32 * (v // RING + 1)
        act.wait_ge(net.raw_full[v % RING], full if self.it is None else self.it * 64 + full)
        if v >= RING:
            act.wait_ge(net.unit_used, self.at(v - RING + 1))
        ins = act.activation(net.w_hi[:, v % RING, part], net.raw[:, v % RING, part], ACT.Copy)
        if half != 0:
            ins.then_inc(net.w_hi_ready, 1)

    def split_lo(self, half=None):
        net, v, dve = self.net, self.u, self.eng
        self.u += half != 0
        if v >= len(net.sizes):
            return
        n = net.sizes[v]
        part = slice(n // 2 if half == 1 else 0, n // 2 if half == 0 else n)
        dve.wait_ge(net.w_hi_ready, self.at(v + 1))
        if v >= RING:
            dve.wait_ge(net.unit_used, self.at(v - RING + 1))
        ins = dve.tensor_tensor(net.w_lo[:, v % RING, part], net.raw[:, v % RING, part],
                                net.w_hi[:, v % RING, part].bitcast(F32), ALU.subtract)
        if half != 0:
            ins.then_inc(net.w_lo_ready, 1)

    def unit(self, x_hi, x_lo, k0, nk, width, banks, start, stop, pieces=1, quarter=None):
        net, u, pe = self.net, self.u, self.eng
        n = nk * pieces * width
        assert self.it is not None or net.sizes[u] == n, (u, net.sizes[u], n)
        hi = net.w_hi[:, u % RING, 0:n].rearrange("p (k c n) -> p k c n", k=nk, c=pieces)
        lo = net.w_lo[:, u % RING, 0:n].rearrange("p (k c n) -> p k c n", k=nk, c=pieces)
        if not quarter:
            pe.wait_ge(net.w_lo_ready, self.at(u + 1))
        for tt in range(TT) if quarter is None else [quarter // 2]:
            for k in range(nk) if quarter is None else range(quarter % 2 * nk // 2, (quarter % 2 + 1) * nk // 2):
                first, last = start and k == 0, stop and k == nk - 1
                xh = x_hi[:, k0 + k, tt * P:(tt + 1) * P]
                xl = x_lo[:, k0 + k, tt * P:(tt + 1) * P]
                for c in range(pieces):
                    out = banks[tt][c][:, 0:width]
                    pe.matmul(out, xh, hi[:, k, c, :], start=first, stop=False)
                for c in range(pieces):
                    pe.matmul(banks[tt][c][:, 0:width], xh, lo[:, k, c, :], start=False, stop=False)
                for c in range(pieces):
                    mm = pe.matmul(banks[tt][c][:, 0:width], xl, hi[:, k, c, :], start=False, stop=last)
        if quarter in (None, 3):
            mm.then_inc(net.unit_used, 1)
            self.u += 1



class Pre:
    def __init__(self, net, name, g, x_ready, x_step, x=None, x_hi=None, x_lo=None):
        self.net, self.g = net, g
        self.x_ready, self.x_step = x_ready, x_step
        self.turned = net.shared_sem("pre_turned", 4)
        self.hi = net.shared_sem("pre_x_hi", KT)
        self.lo = net.shared_sem("pre_x_lo", KT)
        self.r_ready = net.shared_sem("pre_r", 0 if g is None else 1)
        self.x = net.x if x is None else x
        self.x_hi = net.x_hi if x_hi is None else x_hi
        self.x_lo = net.x_lo if x_lo is None else x_lo
        self.banks = [net.G[0], net.G[1], net.M[0], net.M[1]]

    def pe(self, pe):
        for grp in range(4):
            if self.x_step:
                pe.wait_ge(*self.x_ready(self.x_step * (grp // 2 + 1)))
            for kk in range(2):
                k = 2 * grp + kk
                for tt in range(TT):
                    mm = pe.transpose(self.banks[grp][:, kk * T + tt * P:kk * T + (tt + 1) * P],
                                      self.x[:, tt, k * P:(k + 1) * P], self.net.ident[:, :])
            mm.then_inc(self.turned.sem, 1)

    def act(self, w):
        act, net = w.eng, self.net
        for k in range(KT):
            if k % 2 == 0:
                act.wait_ge(*self.turned(k // 2 + 1))
            act.activation(self.x_hi[:, k, :], self.banks[k // 2][:, (k % 2) * T:(k % 2 + 1) * T],
                           ACT.Copy, scale=1.0 if self.g is None else self.g[:, k:k + 1])\
               .then_inc(self.hi.sem, 1)

    def act_r(self, w, r=None):
        act, net = w.eng, self.net
        for tt in range(TT):
            w.chain(act.activation(net.scratch[:, :], self.x[:, tt, :], ACT.Square,
                                   accum_out=net.ss[:, tt:tt + 1]))
        w.chain(act.activation(net.ss[:, :], net.ss[:, :], ACT.Ln, scale=1.0 / D, bias=EPS))
        if r is not None:
            act.activation(r[:, :], net.ss[:, :], ACT.Exp, scale=-0.5).then_inc(self.r_ready.sem, 1)
            act.wait_ge(*self.r_ready(1))
            return
        w.chain(act.activation(net.r[:, :], net.ss[:, :], ACT.Exp, scale=-0.5))
        act.activation(net.nr[:, :], net.r[:, :], ACT.Copy, scale=-1.0).then_inc(self.r_ready.sem, 1)

    def dve(self, w):
        dve, net = w.eng, self.net
        for k in range(KT):
            if k % 2 == 0:
                dve.wait_ge(*self.hi(k + 2))
            dve.scalar_tensor_tensor(out=self.x_lo[:, k, :],
                                     in0=self.banks[k // 2][:, (k % 2) * T:(k % 2 + 1) * T],
                                     scalar=1.0 if self.g is None else self.g[:, k:k + 1],
                                     in1=self.x_hi[:, k, :].bitcast(F32),
                                     op0=ALU.mult, op1=ALU.subtract).then_inc(self.lo.sem, 1)



class Post:
    def __init__(self, net, name, g_row, scale, brow_free):
        self.net, self.g_row, self.scale, self.brow_free = net, g_row, scale, brow_free
        self.loaded = net.shared_sem("post_brow", 16)
        self.squared = net.shared_sem("post_squares", 1)
        self.summed = net.shared_sem("post_sums", 1)
        self.r_ready = net.shared_sem("post_r", 1)
        self.x_ready = net.shared_sem("post_x", 2)

    def pool(self, pool):
        if self.brow_free is not None:
            pool.wait_ge(*self.brow_free(2))
        pool.dma_start(self.net.brow[:, :], self.g_row.partition_broadcast(P)).then_inc(self.loaded.sem, 16)

    def act(self, w):
        act, net = w.eng, self.net
        act.wait_ge(net.unit_used, w.at(w.u - LEAD))
        for tt in range(TT):
            for c in range(2):
                ins = act.activation(net.scratch[:, c * 512:(c + 1) * 512], net.A[2 * tt + c][:, :],
                                     ACT.Square, accum_out=net.ss4[:, tt, c:c + 1])
                if tt == 0 or c == 0:
                    w.chain.mark(ins)
            if tt == 0:
                w.chain.sync()
        ins.then_inc(self.squared.sem, 1)
        act.wait_ge(*self.summed(1))
        w.chain(act.activation(net.post_ss[:, :], net.post_ss[:, :], ACT.Ln, scale=1.0 / D, bias=EPS))
        act.activation(net.post_r[:, :], net.post_ss[:, :], ACT.Exp, scale=-0.5).then_inc(self.r_ready.sem, 1)

    def dve(self, w):
        dve, net = w.eng, self.net
        dve.wait_ge(*self.squared(1))
        dve.tensor_tensor(net.post_ss[:, :], net.ss4[:, :, 0], net.ss4[:, :, 1], ALU.add)\
           .then_inc(self.summed.sem, 1)
        dve.wait_ge(*self.r_ready(1))
        dve.wait_ge(*self.loaded(16))
        for c in range(2):
            for tt in range(TT):
                cols = slice(c * 512, (c + 1) * 512)
                w.chain(dve.scalar_tensor_tensor(out=net.tmp[:, tt, :], in0=net.A[2 * tt + c][:, :],
                                                 scalar=net.post_r[:, tt:tt + 1], in1=net.brow[:, cols],
                                                 op0=ALU.mult, op1=ALU.mult))
                ins = dve.scalar_tensor_tensor(out=net.x[:, tt, cols], in0=net.tmp[:, tt, :],
                                               scalar=self.scale, in1=net.x[:, tt, cols],
                                               op0=ALU.mult, op1=ALU.add)
                if tt == 1:
                    ins.then_inc(self.x_ready.sem, 1)
                else:
                    w.chain.mark(ins)



class Ffn:
    def __init__(self, net, name, w_gu, w_dn, pre_g, post_row, x_ready, x_step, brow_free, last):
        self.net, self.w_gu, self.w_dn = net, w_gu, w_dn
        self.steps = w_dn.shape[0] // 256
        self.loops = (self.steps - 1) // 2 - last
        self.after = range(1 + 2 * self.loops, self.steps)
        self.pre = Pre(net, name, pre_g, x_ready, x_step)
        self.post = Post(net, name, post_row, 0.5, brow_free)
        self.x_ready = self.post.x_ready
        self.clamped = net.shared_sem("ffn_gate", self.steps)
        self.gated = net.shared_sem("ffn_sigmoid", self.steps)
        self.hidden = net.shared_sem("ffn_hidden", self.steps)
        self.h_turned = net.shared_sem("ffn_h_turned", self.steps)
        self.h_hi = net.shared_sem("ffn_h_hi", self.steps)
        self.h_lo = net.shared_sem("ffn_h_lo", self.steps)
        net.sizes += [4 * 512] * (3 * self.steps)

    def tensors(self, net):
        self.z = net.sb("ffn_z", [P, TT, 256])
        self.e = net.sb("ffn_e", [P, TT, 256])
        self.gs = net.sb("ffn_gs", [P, TT, 256])
        self.h = net.sb("ffn_h", [P, TT, 256])
        self.hT_hi = net.sb("ffn_hT_hi", [P, 2, T], F32R)
        self.hT_lo = net.sb("ffn_hT_lo", [P, 2, T], F32R)

    def pool(self, pool):
        self.post.pool(pool)

    def sp(self, w):
        half = self.w_gu.shape[1] // 2

        def gate_up(j):
            for kh in range(2):
                src = self.w_gu[kh * 512:(kh + 1) * 512, :].rearrange("(k p) (g n) -> p k g n", p=P, g=2)
                w.load([4, 2, 256], src[:, :, :, bass.ds(j * 256, 256)])

        def down(j):
            src = self.w_dn[bass.ds(j * 256, 256), :].rearrange("(k p) n -> p k n", p=P)
            w.load([2, D], src)

        gate_up(0)
        with w.eng.Fori(0, self.loops) as it:
            w.enter(it)
            for i in range(2):
                gate_up(it * 2 + (1 + i))
                down(it * 2 + i)
            w.leave(self.loops)
        for j in self.after:
            gate_up(j)
            down(j - 1)
        down(self.steps - 1)

    def gate_up(self, w, j, k_waits=False):
        net, pe = self.net, w.eng
        for kh in range(2):
            if k_waits:
                pe.wait_ge(*self.pre.lo(4 * (kh + 1)))
            elif kh == 0:
                pe.wait_ge(*self.hidden(j))
            w.unit(net.x_hi, net.x_lo, 4 * kh, 4, 512, [[net.G[0]], [net.G[1]]], kh == 0, kh == 1)

    def turn(self, w, j):
        net, pe = self.net, w.eng
        pe.wait_ge(*self.hidden(j + 1))
        if not isinstance(j, int) or j:
            pe.wait_ge(*self.h_lo(j))
        for kk in range(2):
            for tt in range(TT):
                mm = pe.transpose(net.M[0][:, kk * T + tt * P:kk * T + (tt + 1) * P],
                                  self.h[:, tt, kk * P:(kk + 1) * P], net.ident[:, :])
        mm.then_inc(self.h_turned.sem, 1)

    def down(self, w, j, last=False):
        net = self.net
        w.eng.wait_ge(*self.h_lo(j + 1))
        w.unit(self.hT_hi, self.hT_lo, 0, 2, 512, [net.A[0:2], net.A[2:4]], False, last, pieces=2)

    def pe(self, w):
        net, pe = self.net, w.eng
        self.pre.pe(pe)
        for bank in net.A:
            pe.matmul(bank[:, :], net.zeros[:, 0:P], net.zeros[:, :], start=True, stop=False)
        self.gate_up(w, 0, True)
        self.turn(w, 0)
        with pe.Fori(0, self.loops) as it:
            w.enter(it)
            for i in range(2):
                j = it * 2 + (1 + i)
                self.gate_up(w, j)
                self.down(w, it * 2 + i)
                self.turn(w, j)
            w.leave(self.loops)
        for j in self.after:
            self.gate_up(w, j)
            self.down(w, j - 1)
            self.turn(w, j)
        self.down(w, self.steps - 1, True)

    def sigmoid(self, w, j):
        act = w.eng
        act.wait_ge(*self.clamped(j + 1))
        w.chain(act.activation(self.e[:, :, :], self.z[:, :, :], ACT.Exp, scale=-1.0))
        w.chain(act.activation(self.e[:, :, :], self.e[:, :, :], ACT.Ln, bias=1.0))
        act.activation(self.e[:, :, :], self.e[:, :, :], ACT.Exp, scale=-1.0).then_inc(self.gated.sem, 1)

    def hid_hi(self, w, j):
        act = w.eng
        act.wait_ge(*self.h_turned(j + 1))
        act.activation(self.hT_hi[:, :, :], self.net.M[0][:, :], ACT.Copy).then_inc(self.h_hi.sem, 1)

    def act(self, w):
        act = w.eng
        self.pre.act(w)
        w.split_hi()
        self.pre.act_r(w)
        w.split_hi()
        act.wait_ge(*self.pre.r_ready(1))
        self.sigmoid(w, 0)
        with act.Fori(0, self.loops) as it:
            w.enter(it, per=4)
            for i in range(2):
                w.split_hi()
                self.hid_hi(w, it * 2 + i)
                w.split_hi()
                self.sigmoid(w, it * 2 + (1 + i))
                w.split_hi()
            w.leave(self.loops)
        for j in self.after:
            w.split_hi()
            self.hid_hi(w, j - 1)
            w.split_hi()
            self.sigmoid(w, j)
            w.split_hi()
        self.hid_hi(w, self.steps - 1)
        w.split_hi()
        self.post.act(w)

    def make_hidden(self, w, j):
        net, dve = self.net, w.eng
        dve.wait_ge(net.unit_used, w.at(w.u - LEAD))
        for tt in range(TT):
            ins = dve.tensor_scalar(self.z[:, tt, :], net.G[tt][:, 0:256], net.r[:, tt:tt + 1], CLAMP,
                                    ALU.mult, ALU.max)
        ins.then_inc(self.clamped.sem, 1)
        dve.wait_ge(*self.gated(j + 1))
        w.chain(dve.tensor_tensor(self.gs[:, :, :], self.z[:, :, :], self.e[:, :, :], ALU.mult))
        for tt in range(TT):
            ins = dve.scalar_tensor_tensor(out=self.h[:, tt, :], in0=net.G[tt][:, 256:512],
                                           scalar=net.r[:, tt:tt + 1], in1=self.gs[:, tt, :],
                                           op0=ALU.mult, op1=ALU.mult)
        ins.then_inc(self.hidden.sem, 1)

    def hid_lo(self, w, j):
        dve = w.eng
        dve.wait_ge(*self.h_hi(j + 1))
        dve.tensor_tensor(self.hT_lo[:, :, :], self.net.M[0][:, :], self.hT_hi[:, :, :].bitcast(F32),
                          ALU.subtract).then_inc(self.h_lo.sem, 1)

    def dve(self, w):
        dve = w.eng
        self.pre.dve(w)
        w.split_lo()
        w.split_lo()
        dve.wait_ge(*self.pre.r_ready(1))
        self.make_hidden(w, 0)
        with dve.Fori(0, self.loops) as it:
            w.enter(it, per=2)
            for i in range(2):
                w.split_lo()
                self.hid_lo(w, it * 2 + i)
                w.split_lo()
                self.make_hidden(w, it * 2 + (1 + i))
                w.split_lo()
            w.leave(self.loops)
        for j in self.after:
            w.split_lo()
            self.hid_lo(w, j - 1)
            w.split_lo()
            self.make_hidden(w, j)
            w.split_lo()
        self.hid_lo(w, self.steps - 1)
        w.split_lo()
        self.post.dve(w)



HD = 64
HEADS_A, HEADS_M, HEADS_B = 8, 4, 4
DK_B = 32
RANK = 16
LEVELS = [64, 32, 16, 8, 4, 2, 1]
CLAMP = -43.0

CHUNKS = {"b": (2048, 512), "gb": (2560, 256), "rb": (2816, 16), "m": (2832, 512), "qa": (0, 512), "ka": (512, 512),
          "va": (1024, 512), "ga": (1536, 512)}


class Block:

    def __init__(self, net, name, l, dram, gain, x_ready, x_step):
        self.net, self.l, self.x_before, self.name = net, l, (x_ready if l else None), name
        self.w_in, self.w_mem, self.w_out = dram["w_in"][l], dram["w_mem_kv"][l], dram["w_out"][l]
        self.mem_dram = dram["mem"][0].rearrange("(t p) d -> p t d", p=P)
        self.w_gate_up = dram["w_gate_up"][l]
        self.g_gla_row = dram["g_gla_out"][l:l + 1, :]
        self.mem_g = gain(dram["g_mem"][l])
        self.x_g = gain(dram["g_pre"][l])
        self.x_from = (x_ready, x_step)
        self.head_g = {y: net.columns(dram[f"g_{k}"][l:l + 1, :], HD)
                       for y, k in (("qa", "q_moba"), ("ka", "k_moba"), ("qm", "q_mem"), ("mk", "k_mem"))}
        self.b_gate = net.columns(dram["b_gate_up"][l:l + 1, :])
        steps = "mempre unit:mem:0 unit:mem:1 xpre evac:mem norm1:mk " \
                "unit:b:0 norm2:mk unit:b:1 evac:b turn:mk " \
                "unit:rb:0 evac:rb unit:gb:0 evac:gb turn:qkb " \
                "unit:m:0 turn:rb unit:m:1 evac:m z norm1:qm decay " \
                "unit:qa:0 norm2:qm spread unit:qa:1 evac:qa turn:qm norm1:qa gate1:b gate1:m " \
                "unit:ka:0 norm2:qa level:0 level:1 gate2:b gate2:m unit:ka:1 evac:ka turn:qa0 turn:qa1 " \
                "glav:0 level:2 norm1:ka " \
                "unit:va:0 norm2:ka glav:1 level:3 glav:2 score:8 unit:va:1 evac:va glav:3 gcopy " \
                "turn:ka0 turn:ka1 norm1:gla score:9 pturn:8 " \
                "unit:ga:0 norm2:gla score:10 pv:8 pturn:9 score:11 pv:9 gfin score:0 " \
                "unit:ga:1 evac:ga pturn:10 score:1 pv:10 pturn:11 gate1:a score:2 pv:11 join:1 gate2:a " \
                "pturn:0 score:3 pv:0 pturn:1 score:4 pv:1 pturn:2 score:5 pv:2 pturn:3 score:6 pv:3 join:2 " \
                "pturn:4 score:7 pv:4 pturn:5 pv:5 pturn:6 pv:6 pturn:7 pv:7 join:3 " \
                "catpre out:0 out:1"
        self.steps = [tuple(x.split(":")) for x in steps.split()]
        self.norms = [x[1] for x in self.steps if x[0] == "norm1"]
        self.evacs = [x[1] for x in self.steps if x[0] == "evac"]
        self.gates = [x[1] for x in self.steps if x[0] == "gate1"]
        self.items = [int(x[1]) for x in self.steps if x[0] == "score"]
        self.misc = [x for x in self.steps if x[0] in ("turn", "z", "pturn")]
        self.g_uses = []
        for x in self.steps:
            if x[0] == "level":
                self.g_uses += [("level", x[1], part) for part in range(3)]
            elif x[0] == "score":
                self.g_uses.append(x)
        s = lambda n, total: net.shared_sem(f"block_{n}", total)
        self.mem_loaded, self.small_loaded = s("mem_loaded", 16), s("small_loaded", 32)
        self.evacuated = s("evacuated", 2 * len(self.evacs))
        self.sumsq = s("sumsq", len(self.norms))
        self.rhead = s("rhead", len(self.norms))
        self.normed = s("normed", len(self.norms))
        self.misc_done = s("misc_done", len(self.misc))
        self.misc_free = s("misc_free", len(self.misc))
        self.score_done = s("score_done", len(self.g_uses))
        self.levels_in = s("levels_in", 3 * HEADS_B)
        self.maxed = s("maxed", len(self.items))
        self.probs = s("probs", len(self.items))
        self.soft = s("soft", 1)
        self.b_diff = s("b_diff", 1)
        self.b_exp = s("b_exp", 1)
        self.b_qk = s("b_qk", 1)
        self.pv_done = s("pv_done", 4)
        self.o_free = s("o_free", 4)
        self.clamped = s("clamped", len(self.gates))
        self.sigm = s("sigm", len(self.gates))
        self.cat_ready = s("cat_ready", 1)
        self.x_ready = s("x", 2)
        self.u0 = len(net.sizes)
        for x in self.steps:
            if x[0] == "unit":
                net.sizes.append(KT * CHUNKS[x[1]][1] if x[1] in ("gb", "rb") else 4 * 512)
            elif x == ("out", "0"):
                self.u_out = len(net.sizes)
                net.sizes += [4 * 512] * 4

    def tensors(self, net):
        self.y = {c: net.sb(f"y_{c}", [P, TT, w]) for c, w in
                  (("mem", 512), ("b", 512), ("gb", 256), ("rb", 16), ("m", 512), ("qa", 512),
                   ("ka", 512), ("va", 512))}
        self.y["ga"] = self.y["qa"]
        self.gate = net.sb("gate", [P, TT, D])
        self.cat = net.sb("cat", [P, TT, D])
        self.qaT, self.kaT = net.sb("qaT", [P, 4, T]), net.sb("kaT", [P, 4, T])
        self.qmT, self.kmT = net.sb("qmT", [P, 2, T]), net.sb("kmT", [P, 2, T])
        self.qbT, self.kbT = net.sb("qbT", [P, T]), net.sb("kbT", [P, T])
        self.rbT = net.sb("rbT", [RANK, T])
        self.w_gate = net.sb("w_gate", [RANK, P])
        self.g_gla = net.sb("g_gla", [P, HD])
        self.zb, self.soft_t = net.sb("zb", [P, T]), net.sb("soft_t", [P, T])
        self.decay = net.sb("decay", [P, T])
        self.ones = net.sb("ones_row", [P, T])
        self.att = net.sb("att", [P, 2, 3, P])
        self.Pb = net.sb("Pb", [P, 3, 512])
        self.PT = net.sb("PT", [P, 2, 512])
        self.ssh = net.sb("ssh", [P, 5, TT * 8])
        self.r_mem = net.sb("r_mem", [P, TT])
        self.mx, self.nm = net.sb("mx", [P, 12, 2]), net.sb("nm", [P, 12, 2])
        self.rs, self.rr = net.sb("rs", [P, 2, 12]), net.sb("rr", [P, 2, 12])
        with ExitStack() as alias:
            keep, net.ctx = net.ctx, alias
            self.mem_hi = net.sb("mem_hi", [P, KT, T], F32R)
            self.mem_lo = net.sb("mem_lo", [P, KT, T], F32R)
            net.ctx = keep
        self.QE = net.sb("QE", [P, 8, T])
        self.KE = net.sb("KE", [P, 8, T])
        self.src = {"mk": (self.y["mem"][:, :, 0:256], 4), "qm": (self.y["m"][:, :, 0:256], 4),
                    "qa": (self.y["qa"][:, :, :], 8), "ka": (self.y["ka"][:, :, :], 8),
                    "gla": (self.cat[:, :, 512:768], 4)}
        self.gate_src = {"b": (self.y["gb"][:, :, :], self.gate[:, :, 512:768]),
                         "m": (self.y["m"][:, :, 256:512], self.gate[:, :, 768:1024]),
                         "a": (self.y["ga"][:, :, :], self.gate[:, :, 0:512])}
        n = self.name
        self.mempre = Pre(net, f"{n}_mem", self.mem_g, self.mem_loaded, 0, self.cat, self.mem_hi, self.mem_lo)
        self.xpre = Pre(net, n, self.x_g, *self.x_from)
        self.catpre = Pre(net, f"{n}_cat", None, self.cat_ready, 0, self.cat)

    def misc_no(self, step):
        return self.misc.index(step)

    def g_no(self, use):
        return self.g_uses.index(use)

    def item_no(self, n):
        return self.items.index(n)

    def pool(self, pool):
        net = self.net
        if self.x_before is not None:
            pool.wait_ge(*self.prev.catpre.turned(4))
        pool.dma_start(self.cat[:, :, :], self.mem_dram).then_inc(self.mem_loaded.sem, 16)
        if self.x_before is not None:
            pool.wait_ge(*self.prev.cat_ready(1))
        pool.dma_start(self.w_gate[:, :], self.w_gate_up).then_inc(self.small_loaded.sem, 16)
        pool.dma_start(self.g_gla[:, :], self.g_gla_row.partition_broadcast(P)).then_inc(self.small_loaded.sem, 16)

    def sp(self, w):
        def cols(m, rows, at, width):
            return m[rows[0]:rows[1], at:at + width].rearrange("(k p) n -> p k n", p=P)
        for step in self.steps:
            if step[0] == "unit":
                h = int(step[2])
                if step[1] == "mem":
                    w.load([4, 512], cols(self.w_mem, (512 * h, 512 * h + 512), 0, 512))
                elif step[1] in ("gb", "rb"):
                    at, width = CHUNKS[step[1]]
                    w.load([KT, width], cols(self.w_in, (0, D), at, width))
                else:
                    w.load([4, 512], cols(self.w_in, (512 * h, 512 * h + 512), *CHUNKS[step[1]]))
            elif step[0] == "out":
                for h in range(2):
                    w.load([4, 512], cols(self.w_out, (512 * h, 512 * h + 512), 512 * int(step[1]), 512))

    def pe(self, w):
        net, pe = self.net, w.eng
        ident = net.ident

        def take_misc(step):
            n = self.misc_no(step)
            if n >= 2:
                pe.wait_ge(*self.misc_free(n - 1))
            return net.M[n % 2]

        def take_g(use):
            n = self.g_no(use)
            if n >= 2:
                before = self.g_uses[n - 2]
                if before[0] == "level":
                    pe.wait_ge(*self.levels_in(self.level_no(before)))
                elif int(before[1]) >= HEADS_A:
                    pe.wait_ge(*self.probs(self.item_no(int(before[1])) + 1))
                else:
                    pe.wait_ge(*self.maxed(self.item_no(int(before[1])) + 1))
            return net.G[n % 2]

        for step in self.steps:
            kind = step[0]
            if kind == "mempre":
                if self.x_before is not None:
                    pe.wait_ge(*self.prev.catpre.lo(KT))
                pe.wait_ge(*self.mem_loaded(16))
                self.mempre.pe(pe)
            elif kind == "xpre":
                pe.wait_ge(*self.mempre.lo(KT))
                self.xpre.pe(pe)
            elif kind == "unit":
                c, h = step[1], int(step[2])
                i = 2 * self.evacs.index(c)
                if h == 0:
                    if i >= 2:
                        pe.wait_ge(*self.evacuated(i - 1))
                    elif self.x_before is not None:
                        pe.wait_ge(*self.x_before(1))
                banks = [[net.A[i % 3]], [net.A[(i + 1) % 3]]]
                if c == "mem":
                    if h == 0:
                        pe.wait_ge(*self.mempre.lo(KT))
                    w.unit(self.mem_hi, self.mem_lo, 4 * h, 4, 512, banks, h == 0, h == 1)
                elif c in ("gb", "rb"):
                    w.unit(net.x_hi, net.x_lo, 0, KT, CHUNKS[c][1], banks, True, True)
                else:
                    if c == "b" and h == 0:
                        pe.wait_ge(*self.xpre.lo(KT))
                    w.unit(net.x_hi, net.x_lo, 4 * h, 4, 512, banks, h == 0, h == 1)
            elif kind == "turn":
                y = step[1]
                bank = take_misc(step)
                if y == "qkb":
                    pe.wait_ge(*self.evacuated(2 * self.evacs.index("b") + 2))
                    parts = [self.y["b"][:, :, 0:P], self.y["b"][:, :, P:2 * P]]
                elif y == "rb":
                    pe.wait_ge(*self.evacuated(2 * self.evacs.index("rb") + 2))
                    parts = [self.y["rb"][:, :, :]]
                else:
                    src = self.src[y[0:2]][0]
                    pe.wait_ge(*self.normed(self.norms.index(y[0:2]) + 1))
                    first = 2 * int(y[2]) if len(y) == 3 else 0
                    parts = [src[:, :, (first + q) * P:(first + q + 1) * P] for q in range(2)]
                for q, part in enumerate(parts):
                    rows = part.shape[2]
                    for tt in range(TT):
                        mm = pe.transpose(bank[0:rows, q * T + tt * P:q * T + (tt + 1) * P],
                                          part[:, tt, :], ident[:, :])
                mm.then_inc(self.misc_done.sem, 1)
            elif kind == "z":
                bank = take_misc(step)
                pe.wait_ge(*self.misc_free(self.misc_no(("turn", "rb")) + 1))
                pe.wait_ge(*self.small_loaded(32))
                pe.matmul(bank[:, 0:T], self.w_gate[:, :], self.rbT[:, :], start=True, stop=True)\
                  .then_inc(self.misc_done.sem, 1)
            elif kind == "level":
                h = int(step[1])
                rows = slice(DK_B * h, DK_B * (h + 1))
                pe.wait_ge(*self.b_qk(1))
                for part in range(3):
                    bank = take_g(("level", step[1], part))
                    if part < 2:
                        for n, lev in enumerate((range(0, 4), range(4, 7))[part]):
                            s = LEVELS[lev]
                            for t in range(TT):
                                right = self.QE[rows, 1 + lev, t * P:(t + 1) * P]\
                                    .rearrange("p (b h r) -> p b h r", h=2, r=s)[:, :, 1, :]
                                mm = pe.matmul(bank[:, n * P + t * 64:n * P + (t + 1) * 64],
                                               self.KE[rows, 1 + lev, t * P:(t + 1) * P], right,
                                               start=True, stop=True, tile_position=(DK_B * h, 0))
                        if part == 1:
                            mm = pe.matmul(bank[:, 3 * P:4 * P], self.KE[rows, 0, 0:P],
                                           self.QE[rows, 0, P:2 * P], start=True, stop=True,
                                           tile_position=(DK_B * h, 0))
                    else:
                        for t in range(TT):
                            tok = slice(t * P, (t + 1) * P)
                            mm = pe.matmul(bank[:, tok], self.kbT[rows, tok], self.qbT[rows, tok],
                                           start=True, stop=True, tile_position=(DK_B * h, 0))
                    mm.then_inc(self.score_done.sem, 1)
            elif kind == "glav":
                h = int(step[1])
                pe.wait_ge(*self.levels_in(3 * (h + 1)))
                v = self.y["b"]
                cols = slice(256 + HD * h, 256 + HD * (h + 1))
                a = self.att[:, h % 2]
                O = net.A[3]
                pe.matmul(O[:, HD * h:HD * (h + 1)], a[:, 0, :], v[:, 0, cols], start=True, stop=True)
                o1 = O[:, T + HD * h:T + HD * (h + 1)]
                pe.matmul(o1, a[:, 2, :], v[:, 0, cols], start=True, stop=False)
                mm = pe.matmul(o1, a[:, 1, :], v[:, 1, cols], start=False, stop=True)
                if h == 3:
                    mm.then_inc(self.pv_done.sem, 1)
            elif kind == "score":
                n = int(step[1])
                bank = take_g(step)
                if n < HEADS_A:
                    pe.wait_ge(*self.misc_free(self.misc_no(("turn", "qa1")) + 1))
                    pe.wait_ge(*self.misc_free(self.misc_no(("turn", "ka1")) + 1))
                    rows, pair = slice(HD * (n % 2), HD * (n % 2 + 1)), n // 2
                    q, k = self.qaT[rows, pair, :], self.kaT[rows, pair, :]
                    spans = [(0, P), (P, T)]
                else:
                    pe.wait_ge(*self.misc_free(self.misc_no(("turn", "qm")) + 1))
                    h = n - HEADS_A
                    rows, pair = slice(HD * (h % 2), HD * (h % 2 + 1)), h // 2
                    q, k = self.qmT[rows, pair, :], self.kmT[rows, pair, :]
                    spans = [(0, T), (T, T)]
                for tt, (at, keys) in enumerate(spans):
                    mm = pe.matmul(bank[:, at:at + keys], q[:, tt * P:(tt + 1) * P], k[:, 0:keys],
                                   start=True, stop=True, tile_position=(rows.start, 0))
                mm.then_inc(self.score_done.sem, 1)
            elif kind == "pturn":
                n = int(step[1])
                bank = take_misc(step)
                i = self.item_no(n)
                pe.wait_ge(*self.probs(i + 1))
                for b in range(3 if n < HEADS_A else 4):
                    mm = pe.transpose(bank[:, b * P:(b + 1) * P], self.Pb[:, i % 3, b * P:(b + 1) * P],
                                      ident[:, :])
                mm.then_inc(self.misc_done.sem, 1)
            elif kind == "pv":
                n = int(step[1])
                i = self.item_no(n)
                pe.wait_ge(*self.misc_free(self.misc_no(("pturn", step[1])) + 1))
                g = i // 4 + 1
                if i % 4 == 0:
                    pe.wait_ge(*self.o_free(g))
                pt = self.PT[:, i % 2, :]
                O = net.A[3]
                at = HD * (i % 4)
                if n < HEADS_A:
                    pe.wait_ge(*self.evacuated(2 * self.evacs.index("va") + 2))
                    v, cols = self.y["va"], slice(HD * n, HD * (n + 1))
                    blocks = [[0], [1, 2]]
                else:
                    v, cols = self.y["mem"], slice(256 + HD * (n - HEADS_A), 256 + HD * (n - HEADS_A + 1))
                    blocks = [[0, 1], [2, 3]]
                for tt in range(TT):
                    for kt, b in enumerate(blocks[tt]):
                        mm = pe.matmul(O[:, tt * T + at:tt * T + at + HD], pt[:, b * P:(b + 1) * P],
                                       v[:, kt, cols], start=(kt == 0), stop=(b == blocks[tt][-1]))
                if i % 4 == 3:
                    mm.then_inc(self.pv_done.sem, 1)
            elif kind == "catpre":
                pe.wait_ge(*self.misc_free(len(self.misc)))
                pe.wait_ge(*self.probs(len(self.items)))
                pe.wait_ge(*self.cat_ready(1))
                self.catpre.pe(pe)
            elif kind == "out":
                c = int(step[1])
                if c == 0:
                    pe.wait_ge(*self.evacuated(2 * len(self.evacs)))
                    pe.wait_ge(*self.catpre.lo(KT))
                for h in range(2):
                    w.unit(net.x_hi, net.x_lo, 4 * h, 4, 512, [[net.A[2 * c]], [net.A[2 * c + 1]]],
                           h == 0, h == 1)

    def level_no(self, use):
        return [u for u in self.g_uses if u[0] == "level"].index(use) + 1

    def act(self, w):
        net, act = self.net, w.eng
        for step in self.steps:
            kind = step[0]
            if kind == "mempre":
                self.mempre.act(w)
                self.mempre.act_r(w, self.r_mem)
            elif kind == "xpre":
                self.xpre.act(w)
                self.xpre.act_r(w)
            elif kind == "unit":
                w.split_hi()
            elif kind == "out":
                w.split_hi()
                w.split_hi()
            elif kind == "evac":
                c = step[1]
                i = 2 * self.evacs.index(c)
                act.wait_ge(net.unit_used, self.unit_end(c))
                if c == "mem":
                    act.wait_ge(*self.mempre.r_ready(1))
                elif c == "b":
                    act.wait_ge(*self.xpre.r_ready(1))
                width = self.y[c].shape[2]
                r = self.r_mem if c == "mem" else net.r
                for tt in range(TT):
                    act.activation(self.y[c][:, tt, :], net.A[(i + tt) % 3][:, 0:width], ACT.Copy,
                                   scale=r[:, tt:tt + 1]).then_inc(self.evacuated.sem, 1)
            elif kind == "norm1":
                i = self.norms.index(step[1])
                n = TT * self.src[step[1]][1]
                act.wait_ge(*self.sumsq(i + 1))
                w.chain(act.activation(self.ssh[:, i, 0:n], self.ssh[:, i, 0:n], ACT.Ln,
                                       scale=1.0 / HD, bias=EPS))
                act.activation(self.ssh[:, i, 0:n], self.ssh[:, i, 0:n], ACT.Exp, scale=-0.5)\
                   .then_inc(self.rhead.sem, 1)
            elif kind in ("turn", "z", "pturn"):
                m = self.misc_no(step)
                bank = net.M[m % 2]
                act.wait_ge(*self.misc_done(m + 1))
                if kind == "pturn":
                    n = int(step[1])
                    width = (3 if n < HEADS_A else 4) * P
                    ins = act.activation(self.PT[:, self.item_no(n) % 2, 0:width], bank[:, 0:width], ACT.Copy)
                elif kind == "z":
                    ins = act.activation(self.zb[:, :], bank[:, 0:T], ACT.Identity, bias=self.b_gate)
                elif step[1] == "qkb":
                    w.chain.mark(act.activation(self.qbT[:, :], bank[:, 0:T], ACT.Copy, scale=DK_B ** -0.5))
                    ins = act.activation(self.kbT[:, :], bank[:, T:2 * T], ACT.Copy)
                elif step[1] == "rb":
                    ins = act.activation(self.rbT[:, :], bank[0:RANK, 0:T], ACT.Copy)
                else:
                    y = step[1]
                    dst = {"qa": self.qaT, "ka": self.kaT, "qm": self.qmT, "mk": self.kmT}[y[0:2]]
                    first = 2 * int(y[2]) if len(y) == 3 else 0
                    ins = act.activation(dst[:, first:first + 2, :], bank[:, :], ACT.Copy,
                                         scale=self.head_g[y[0:2]])
                ins.then_inc(self.misc_free.sem, 1)
            elif kind == "decay":
                act.wait_ge(*self.misc_free(self.misc_no(("z",)) + 1))
                w.chain(act.activation(self.soft_t[:, :], self.zb[:, :], ACT.Abs))
                w.chain(act.activation(self.soft_t[:, :], self.soft_t[:, :], ACT.Exp, scale=-1.0))
                act.activation(self.soft_t[:, :], self.soft_t[:, :], ACT.Ln, bias=1.0).then_inc(self.soft.sem, 1)
            elif kind == "spread":
                act.wait_ge(*self.b_diff(1))
                w.chain(act.activation(self.KE[:, :, :], self.KE[:, :, :], ACT.Abs))
                act.activation(self.KE[:, :, :], self.KE[:, :, :], ACT.Exp, scale=-1.0 / 16.0)\
                   .then_inc(self.b_exp.sem, 1)
            elif kind == "gate1":
                i = self.gates.index(step[1])
                g = self.gate_src[step[1]][1]
                act.wait_ge(*self.clamped(i + 1))
                w.chain(act.activation(g, g, ACT.Exp, scale=-1.0))
                w.chain(act.activation(g, g, ACT.Ln, bias=1.0))
                act.activation(g, g, ACT.Exp, scale=-1.0).then_inc(self.sigm.sem, 1)
            elif kind == "score":
                n = int(step[1])
                i = self.item_no(n)
                act.wait_ge(*self.maxed(i + 1))
                for tt in range(TT):
                    if n < HEADS_A:
                        span = slice(0, P) if tt == 0 else slice(P, P + T)
                        src = self.Pb[:, i % 3, span]
                    else:
                        span = slice(tt * T, (tt + 1) * T)
                        src = net.G[self.g_no(step) % 2][:, span]
                    ins = act.activation(self.Pb[:, i % 3, span], src, ACT.Exp, scale=HD ** -0.5,
                                         bias=self.nm[:, i, tt:tt + 1], accum_out=self.rs[:, tt, i:i + 1])
                    if tt == 0:
                        w.chain.mark(ins)
                ins.then_inc(self.probs.sem, 1)
            elif kind == "catpre":
                self.catpre.act(w)

    def unit_end(self, c):
        n = self.u0
        for step in self.steps:
            if step[0] == "unit":
                n += 1
                if step[1] == c and (step[2] == "1" or c in ("gb", "rb")):
                    return n

    def dve(self, w):
        net, dve = self.net, w.eng
        w.chain.mark(dve.memset(self.ones[:, :], 1.0))
        w.chain(dve.memset(self.att[:, :, :, :], 0.0))
        for step in self.steps:
            kind = step[0]
            if kind == "mempre":
                self.mempre.dve(w)
            elif kind == "xpre":
                self.xpre.dve(w)
            elif kind == "unit":
                w.split_lo()
            elif kind == "norm1":
                y = step[1]
                i = self.norms.index(y)
                src, heads = self.src[y]
                n = TT * heads
                if y != "gla":
                    c = {"mk": "mem", "qm": "m"}.get(y, y)
                    dve.wait_ge(*self.evacuated(2 * self.evacs.index(c) + 2))
                else:
                    w.chain.sync()
                sq = net.tmp[:, :, 0:heads * HD]
                w.chain(dve.tensor_tensor(sq, src, src, ALU.mult))
                dve.tensor_reduce(self.ssh[:, i, 0:n].rearrange("p (t h) -> p t h", t=TT),
                                  sq.rearrange("p t (h d) -> p t h d", d=HD), AX.X, ALU.add)\
                   .then_inc(self.sumsq.sem, 1)
            elif kind == "norm2":
                y = step[1]
                i = self.norms.index(y)
                src, heads = self.src[y]
                dve.wait_ge(*self.rhead(i + 1))
                for tt in range(TT):
                    s = src[:, tt, :].rearrange("p (h d) -> p h d", d=HD)
                    r = self.ssh[:, i, tt * heads:(tt + 1) * heads].unsqueeze(2).to_broadcast([P, heads, HD])
                    ins = dve.tensor_tensor(s, s, r, ALU.mult)
                    if tt == 0:
                        w.chain.mark(ins)
                ins.then_inc(self.normed.sem, 1)
            elif kind == "decay":
                dve.wait_ge(net.consts, net.masks_at)
                dve.wait_ge(*self.soft(1))
                w.chain(dve.scalar_tensor_tensor(out=self.soft_t[:, :], in0=self.zb[:, :], scalar=0.0,
                                                 in1=self.soft_t[:, :], op0=ALU.min, op1=ALU.subtract))
                w.chain(dve.tensor_tensor_scan(self.decay[:, :], self.ones[:, :], self.soft_t[:, :], 0.0,
                                               ALU.mult, ALU.add))
                for lev, s in enumerate([P] + LEVELS):
                    b = self.decay[:, :].rearrange("p (n s) -> p n s", s=2 * s)
                    mid = b[:, :, s - 1:s].to_broadcast([P, T // (2 * s), 2 * s])
                    ins = dve.tensor_tensor(self.KE[:, lev, :].rearrange("p (n s) -> p n s", s=2 * s),
                                            b, mid, ALU.subtract)
                    if lev < len(LEVELS):
                        w.chain.mark(ins)
                ins.then_inc(self.b_diff.sem, 1)
            elif kind == "spread":
                dve.wait_ge(*self.b_exp(1))
                all_levels = [P, 8, T]
                w.chain(dve.tensor_tensor(self.QE[:, :, :], self.KE[:, :, :],
                                          self.qbT[:, :].unsqueeze(1).to_broadcast(all_levels), ALU.mult))
                dve.tensor_tensor(self.KE[:, :, :], self.KE[:, :, :],
                                  self.kbT[:, :].unsqueeze(1).to_broadcast(all_levels), ALU.mult)\
                   .then_inc(self.b_qk.sem, 1)
            elif kind == "gate1":
                y, g = self.gate_src[step[1]]
                c = {"b": "gb", "m": "m", "a": "ga"}[step[1]]
                dve.wait_ge(*self.evacuated(2 * self.evacs.index(c) + 2))
                dve.tensor_scalar(g, y, CLAMP, None, ALU.max).then_inc(self.clamped.sem, 1)
            elif kind == "gate2":
                y, g = self.gate_src[step[1]]
                dve.wait_ge(*self.sigm(self.gates.index(step[1]) + 1))
                w.chain(dve.tensor_tensor(g, g, y, ALU.mult))
            elif kind == "level":
                a = self.att[:, int(step[1]) % 2, 0:2, :].rearrange("p t i -> p (t i)")
                for part in range(3):
                    n = self.g_no(("level", step[1], part))
                    bank = net.G[n % 2]
                    dve.wait_ge(*self.score_done(n + 1))
                    if part < 2:
                        for k, lev in enumerate((range(0, 4), range(4, 7))[part]):
                            s = LEVELS[lev]
                            right = a.rearrange("p (b h r) -> p b h r", h=2, r=s)[:, :, 1, :]
                            ins = dve.copy_predicated(
                                right, net.level_u8[:, lev, :].rearrange("p (b r) -> p b r", r=s),
                                bank[:, k * P:(k + 1) * P].rearrange("p (b r) -> p b r", r=s))
                            if lev < 6 and not (part == 0 and k == 3):
                                w.chain(ins)
                        if part == 1:
                            w.chain(ins)
                            ins = dve.tensor_copy(self.att[:, int(step[1]) % 2, 2, :], bank[:, 3 * P:4 * P])
                    else:
                        ins = dve.copy_predicated(a, net.diag_u8[:, :], bank[:, 0:T])
                    ins.then_inc(self.levels_in.sem, 1)
                    dve.wait_ge(*self.levels_in(self.level_no(("level", step[1], part))))
            elif kind == "gcopy":
                dve.wait_ge(*self.pv_done(1))
                dve.tensor_copy(self.cat[:, :, 512:768], net.A[3][:, :].rearrange("p (t n) -> p t n", t=TT))\
                   .then_inc(self.o_free.sem, 1)
                dve.wait_ge(*self.o_free(1))
            elif kind == "gfin":
                dve.wait_ge(*self.normed(self.norms.index("gla") + 1))
                for tt in range(TT):
                    o = self.cat[:, tt, 512:768].rearrange("p (h d) -> p h d", d=HD)
                    w.chain.mark(dve.tensor_tensor(
                        o, o, self.g_gla[:, :].unsqueeze(1).to_broadcast([P, HEADS_B, HD]), ALU.mult))
                w.chain.sync()
                w.chain(dve.tensor_tensor(self.cat[:, :, 512:768], self.cat[:, :, 512:768],
                                          self.gate[:, :, 512:768], ALU.mult))
            elif kind == "score":
                n = int(step[1])
                i = self.item_no(n)
                g = self.g_no(step)
                bank = net.G[g % 2]
                dve.wait_ge(*self.score_done(g + 1))
                if n < HEADS_A:
                    logits = self.Pb[:, i % 3, 0:P + T]
                    slope = 2.0 ** (-8.0 * (n + 1) / HEADS_A)
                    w.chain(dve.scalar_tensor_tensor(out=logits, in0=net.neg_dist[:, :],
                                                     scalar=slope * HD ** 0.5, in1=bank[:, 0:P + T],
                                                     op0=ALU.mult, op1=ALU.add))
                    for tt, span in enumerate((slice(0, P), slice(P, P + T))):
                        w.chain.mark(dve.tensor_reduce(self.mx[:, i, tt:tt + 1], logits[:, span], AX.X, ALU.max))
                else:
                    w.chain.mark(dve.tensor_reduce(self.mx[:, i, :],
                                                   bank[:, :].rearrange("p (t n) -> p t n", t=TT), AX.X, ALU.max))
                w.chain.sync()
                dve.tensor_scalar(self.nm[:, i, :], self.mx[:, i, :], -(HD ** -0.5), None, ALU.mult)\
                   .then_inc(self.maxed.sem, 1)
            elif kind == "join":
                g = int(step[1])
                i0 = 4 * (g - 1)
                n0 = self.items[i0]
                at = HD * n0 if n0 < HEADS_A else 768
                dve.wait_ge(*self.pv_done(g + 1))
                dve.wait_ge(*self.probs(i0 + 4))
                w.chain(dve.reciprocal(self.rr[:, :, i0:i0 + 4], self.rs[:, :, i0:i0 + 4]))
                for tt in range(TT):
                    ins = dve.tensor_tensor(
                        self.cat[:, tt, at:at + 4 * HD].rearrange("p (h d) -> p h d", d=HD),
                        net.A[3][:, tt * T:(tt + 1) * T].rearrange("p (h d) -> p h d", d=HD),
                        self.rr[:, tt, i0:i0 + 4].unsqueeze(2).to_broadcast([P, 4, HD]), ALU.mult)
                    if tt == 0:
                        w.chain.mark(ins)
                ins.then_inc(self.o_free.sem, 1)
                dve.wait_ge(*self.o_free(g + 1))
                ins = dve.tensor_tensor(self.cat[:, :, at:at + 4 * HD], self.cat[:, :, at:at + 4 * HD],
                                        self.gate[:, :, at:at + 4 * HD], ALU.mult)
                if g == 3:
                    ins.then_inc(self.cat_ready.sem, 1)
                else:
                    w.chain.mark(ins)
            elif kind == "catpre":
                self.catpre.dve(w)
            elif kind == "out":
                c = int(step[1])
                w.split_lo()
                w.split_lo()
                dve.wait_ge(net.unit_used, self.u_out + 2 * (c + 1))
                for tt in range(TT):
                    cols = net.x[:, tt, c * 512:(c + 1) * 512]
                    ins = dve.tensor_tensor(cols, net.A[2 * c + tt][:, :], cols, ALU.add)
                    if tt == 0:
                        w.chain.mark(ins)
                ins.then_inc(self.x_ready.sem, 1)



class Conv:
    def __init__(self, net, name, dram, gain, x_ready, x_step, brow_free):
        self.net = net
        s = lambda n: net.shared_sem(f"{name}_{n}")
        self.w_in, self.w_out = dram["sc_w_in_2"][0], dram["sc_w_out_2"][0]
        g = dram["norm_g_2"][0]
        self.pre = Pre(net, name, gain(g[2]), x_ready, x_step)
        self.post = Post(net, name, g[3], 1.0, brow_free)
        self.x_ready = self.post.x_ready
        taps = dram["sc_conv_w_2"][0]
        self.width = taps.shape[0]
        self.taps = net.columns(taps.rearrange("j (k p) -> (j k) p", p=P))
        self.c_out, self.cv, self.b_out = s("c_out"), s("cv"), s("b_out")
        self.cv_turned, self.b_turned = s("cv_turned"), s("b_turned")
        self.tapped = s("tapped")
        self.y, self.y_hi_ready, self.y_lo_ready = s("y"), s("y_hi"), s("y_lo")
        self.u0 = len(net.sizes)
        net.sizes += [4 * 512] * 16
        steps = "unit:c:0:0 unit:c:0:1 c:0 unit:v:0:0 unit:v:0:1 cv:0 unit:b:0:0 turncv:0 unit:b:0:1 b:0 " \
                "unit:c:1:0 turnb:0 mul:0 unit:c:1:1 c:1 unit:v:1:0 unit:v:1:1 cv:1 unit:b:1:0 turncv:1 " \
                "unit:b:1:1 b:1 turnb:1 mul:1 out"
        self.steps = [tuple(x.split(":")) for x in steps.split()]
        self.chunks = [("c", 0), ("v", 0), ("b", 0), ("c", 1), ("v", 1), ("b", 1)]

    def tensors(self, net):
        self.c = net.sb("sc_c", [P, TT, 512])
        self.b = net.sb("sc_b", [P, TT, 512])
        self.cvs = net.sb("sc_cv", [P, TT, 512])
        self.t = net.sb("sc_t", [P, 4, T])
        self.y_hi = net.sb("sc_y_hi", [P, KT, T], F32R)
        self.y_lo = net.sb("sc_y_lo", [P, KT, T], F32R)

    def pool(self, pool):
        self.post.pool(pool)

    def sp(self, w):
        for what, half in self.chunks:
            at = {"b": 0, "c": D, "v": 2 * D}[what] + 512 * half
            for h in range(2):
                w.load([4, 512], self.w_in[512 * h:512 * h + 512, at:at + 512].rearrange("(k p) n -> p k n", p=P))
        for h in range(4):
            w.load([2, D], self.w_out[256 * h:256 * h + 256, :].rearrange("(k p) n -> p k n", p=P))

    def banks(self, n):
        A = self.net.A
        return (A[0], A[1]) if n % 2 == 0 else (A[2], A[3])

    def pe(self, w):
        net, pe = self.net, w.eng
        self.pre.pe(pe)
        for step in self.steps:
            kind = step[0]
            if kind == "unit":
                n = self.chunks.index((step[1], int(step[2])))
                h = int(step[3])
                if n == 0:
                    pe.wait_ge(*self.pre.lo(4 * (h + 1)))
                elif n >= 2 and h == 0:
                    what, half = self.chunks[n - 2]
                    sem, per = {"c": (self.c_out, 1), "v": (self.cv, 1), "b": (self.b_out, 1)}[what]
                    pe.wait_ge(*sem(half + 1))
                b0, b1 = self.banks(n)
                w.unit(net.x_hi, net.x_lo, 4 * h, 4, 512, [[b0], [b1]], h == 0, h == 1)
            elif kind in ("turncv", "turnb"):
                half = int(step[1])
                src, banks, sem, ready = (self.cvs, net.G, self.cv_turned, self.cv) if kind == "turncv" \
                    else (self.b, net.M, self.b_turned, self.b_out)
                pe.wait_ge(*ready(half + 1))
                if half:
                    pe.wait_ge(*self.y(2))
                else:
                    pe.wait_ge(*self.pre.lo(KT))
                for pair in range(2):
                    for kk in range(2):
                        for tt in range(TT):
                            k = 2 * pair + kk
                            mm = pe.transpose(banks[pair][:, kk * T + tt * P:kk * T + (tt + 1) * P],
                                              src[:, tt, k * P:(k + 1) * P], net.ident[:, :])
                    mm.then_inc(sem.sem, 1)
            elif kind == "out":
                pe.wait_ge(*self.cv(2))
                pe.wait_ge(*self.b_out(2))
                for h in range(4):
                    pe.wait_ge(*self.y_lo_ready(h + 1))
                    w.unit(self.y_hi, self.y_lo, 2 * h, 2, 512, [net.A[0:2], net.A[2:4]], h == 0, h == 3,
                           pieces=2)

    def act(self, w):
        net, act = self.net, w.eng
        self.pre.act(w)
        self.pre.act_r(w)
        act.wait_ge(*self.pre.r_ready(1))
        for step in self.steps:
            kind = step[0]
            if kind == "unit":
                w.split_hi()
            elif kind in ("c", "b"):
                half = int(step[1])
                n = self.chunks.index((kind, half))
                act.wait_ge(net.unit_used, self.u0 + 2 * (n + 1))
                if kind == "c" and half:
                    act.wait_ge(*self.cv(1))
                if kind == "b" and half:
                    act.wait_ge(*self.b_turned(2))
                for tt in range(TT):
                    ins = act.activation((self.c if kind == "c" else self.b)[:, tt, :],
                                         self.banks(n)[tt][:, :], ACT.Copy, scale=net.r[:, tt:tt + 1])
                ins.then_inc((self.c_out if kind == "c" else self.b_out).sem, 1)
            elif kind == "turncv":
                half = int(step[1])
                for pair in range(2):
                    act.wait_ge(*self.cv_turned(2 * half + pair + 1))
                    if half:
                        act.wait_ge(*self.y_lo_ready(pair + 1))
                    for kk in range(2):
                        k = 4 * half + 2 * pair + kk
                        at = (self.width - 1) * KT + k
                        ins = act.activation(self.t[:, 2 * pair + kk, :],
                                             net.G[pair][:, kk * T:(kk + 1) * T], ACT.Copy,
                                             scale=self.taps[:, at:at + 1])
                    ins.then_inc(self.tapped.sem, 1)
            elif kind == "mul":
                half = int(step[1])
                for pair in range(2):
                    n = 2 * half + pair
                    act.wait_ge(*self.y(n + 1))
                    act.activation(self.y_hi[:, 2 * n:2 * n + 2, :], self.t[:, 2 * pair:2 * pair + 2, :],
                                   ACT.Copy).then_inc(self.y_hi_ready.sem, 1)
            elif kind == "out":
                for _ in range(4):
                    w.split_hi()
        self.post.act(w)

    def dve(self, w):
        net, dve = self.net, w.eng
        self.pre.dve(w)
        for step in self.steps:
            kind = step[0]
            if kind == "unit":
                w.split_lo()
            elif kind == "cv":
                half = int(step[1])
                n = self.chunks.index(("v", half))
                dve.wait_ge(net.unit_used, self.u0 + 2 * (n + 1))
                dve.wait_ge(*self.c_out(half + 1))
                if half:
                    dve.wait_ge(*self.cv_turned(2))
                for tt in range(TT):
                    ins = dve.scalar_tensor_tensor(out=self.cvs[:, tt, :], in0=self.banks(n)[tt][:, :],
                                                   scalar=net.r[:, tt:tt + 1], in1=self.c[:, tt, :],
                                                   op0=ALU.mult, op1=ALU.mult)
                    if tt == 0:
                        w.chain.mark(ins)
                ins.then_inc(self.cv.sem, 1)
            elif kind == "turncv":
                half = int(step[1])
                for pair in range(2):
                    dve.wait_ge(*self.tapped(2 * half + pair + 1))
                    for back in range(1, self.width):
                        for kk in range(2):
                            k = 4 * half + 2 * pair + kk
                            at = (self.width - 1 - back) * KT + k
                            row = self.t[:, 2 * pair + kk, back:T]
                            w.chain.mark(dve.scalar_tensor_tensor(
                                out=row, in0=net.G[pair][:, kk * T:(kk + 1) * T - back],
                                scalar=self.taps[:, at:at + 1], in1=row, op0=ALU.mult, op1=ALU.add))
                        w.chain.sync()
            elif kind == "mul":
                half = int(step[1])
                for pair in range(2):
                    n = 2 * half + pair
                    t = self.t[:, 2 * pair:2 * pair + 2, :].rearrange("p k t -> p (k t)")
                    dve.wait_ge(*self.b_turned(n + 1))
                    dve.tensor_tensor(t, t, net.M[pair][:, :], ALU.mult).then_inc(self.y.sem, 1)
                for pair in range(2):
                    n = 2 * half + pair
                    dve.wait_ge(*self.y_hi_ready(n + 1))
                    dve.tensor_tensor(self.y_lo[:, 2 * n:2 * n + 2, :], self.t[:, 2 * pair:2 * pair + 2, :],
                                      self.y_hi[:, 2 * n:2 * n + 2, :].bitcast(F32), ALU.subtract)\
                       .then_inc(self.y_lo_ready.sem, 1)
            elif kind == "out":
                for _ in range(4):
                    w.split_lo()
        self.post.dve(w)



GH, GV = 8, 16
NQ = 4


class Gdn:

    def __init__(self, net, name, dram, gain, x_ready, x_step, brow_free):
        self.net, self.name = net, name
        s = lambda n: net.shared_sem(f"{name}_{n}")
        self.w_in, self.w_out = dram["gdn_w_in_2"][0], dram["gdn_w_out_2"][0]
        g = dram["norm_g_2"][1]
        self.pre = Pre(net, name, gain(g[2]), x_ready, x_step)
        self.post = Post(net, name, g[3], 1.0, brow_free)
        self.x_ready = self.post.x_ready
        taps = dram["gdn_conv_w_2"][0]
        self.width, self.ctiles = taps.shape[0], taps.shape[1] // P
        self.taps = net.columns(taps.rearrange("j (k p) -> (j k) p", p=P), side=1)
        self.rows_dram = (dram["gdn_a_log_2"], dram["gdn_dt_bias_2"], dram["gdn_norm_w_2"])
        self.small_loaded = s("small_loaded")
        self.evacuated = s("evacuated")
        self.ba = {x: s(f"ba_{x}") for x in ("act", "dve", "pe")}
        self.ones_set = s("ones_set")
        self.a3_pe = s("a3_written")
        self.a3_act = s("a3_read_act")
        self.a3_dve = s("a3_read_dve")
        self.tapped = s("tapped")
        self.clamped, self.sigm = s("clamped"), s("sigm")
        self.silued = s("silued")
        self.squared = s("squared")
        self.rsq = s("rsq")
        self.l2 = s("l2")
        self.c_pe = [s(f"core_pe{i}") for i in range(2)]
        self.c_act = [s(f"core_act{i}") for i in range(2)]
        self.c_dve = [s(f"core_dve{i}") for i in range(2)]
        self.c_pool = [s(f"core_pool{i}") for i in range(2)]
        self.o_sq, self.o_r, self.o_ready = s("o_sq"), s("o_r"), s("o_ready")
        self.z_clamped, self.z_sigm = s("z_clamped"), s("z_sigm")
        self.o_turned, self.o_hi_ready, self.o_lo_ready = s("o_turned"), s("o_hi"), s("o_lo")
        self.u0 = len(net.sizes)
        self.chunks = ["ba", "q0", "k0", "v0", "v1", "q1", "k1", "v2", "v3", "z0", "z1", "z2", "z3"]
        for c in self.chunks:
            net.sizes += [KT * 32] if c == "ba" else [4 * 512] * 2
        net.sizes += [4 * 512] * 8
        self.steps = [tuple(x.split(":")) for x in self.schedule()]
        self.evacs = [x[1] for x in self.steps if x[0] == "evac"]
        self.silus = [x[1] for x in self.steps if x[0] == "silu" and x[2] == "0"]
        self.norms = [x for x in self.steps if x[0] == "norm"]
        self.l2s = [x[1] for x in self.steps if x[0] == "l2"]
        self.a3 = [x for x in self.steps if x[0] in ("conv", "norm", "kn", "vt", "ba")]
        self.a3 = [x for x in self.a3 if x[0] != "ba" or x[1] in "12"]

    def schedule(self):
        steps, cores = [], [[], [[]] * 3]
        conv = [c for c in self.chunks if c[0] in "qkv"]
        z = [c for c in self.chunks if c[0] == "z"]

        def add_core(i):
            pieces = ["k0", "", "k1"] + [f"{ab}{lev}" for lev in range(5, -1, -1) for ab in "xt"] + \
                     [f"p{n}" for n in range(5)]
            for one in range(2):
                cores[one] += [[f"core:{2 * i + one}:{piece}"] if piece else [] for piece in pieces]

        def core():
            for one in range(2):
                if cores[one]:
                    steps.extend(cores[one].pop(0))

        def quarter(unit, extras):
            steps.append(unit)
            if extras and extras[0].startswith("evac"):
                steps.append(extras.pop(0))
            if any(cores[0] + cores[1]):
                core()
            steps.extend(extras)

        for q in range(NQ):
            quarter(f"unit:ba:0:{q}", ["evac:ba"] if q == 3 else [])
        started_by = ["k0", "v1", "v2", "v3"]
        for n, c in enumerate(self.chunks[1:]):
            slots = [[] for _ in range(2 * NQ)]
            one = conv[n - 1] if 1 <= n <= len(conv) else None
            two = conv[n - 2] if 2 <= n <= len(conv) + 1 else None
            if n == 0:
                slots[3], slots[7] = ["ba:0", "ba:1"], ["ba:2", "ba:3"]
            if two:
                slots[0] = [f"silu:{two}:2"]
                if two[0] == "v":
                    slots[1], slots[2] = [f"vt:{two}:0"], [f"vt:{two}:1"]
                else:
                    slots[1:4] = [f"l2:{two}"], [f"norm:{two}:0"], [f"norm:{two}:1"]
                    slots[4] += [f"kn:{two}"] if two[0] == "k" else []
            if one:
                slots[4] += [f"conv:{one}:0"]
                slots[5] += [f"conv:{one}:1"]
                slots[6] += [f"silu:{one}:0"]
                slots[7] += [f"silu:{one}:1"]
            if c in z[2:]:
                slots[0] += [f"z2:{z[z.index(c) - 2]}:2"]
            if c in z[1:]:
                i = z.index(c) - 1
                slots[3:8] = [f"z1:z{i}:0"], [f"z1:z{i}:1"], [f"z1:z{i}:2"], [f"z2:z{i}:0"], [f"z2:z{i}:1"]
            slots[7].insert(0, f"evac:{c}")
            for slot, extras in enumerate(slots):
                quarter(f"unit:{c}:{slot // NQ}:{slot % NQ}", extras)
                if two in started_by and slot == 4:
                    add_core(started_by.index(two))
        steps.append("z2:z2:2")
        steps += [f"ot:{n}" for n in range(4)]
        last_z = ["z1:z3:0", "z1:z3:1", "z1:z3:2"]
        last_o = ["z2:z3:0", "z2:z3:1", "z2:z3:2"]
        for slot in range(4 * NQ):
            quarter(f"out:{slot // NQ}:{slot % NQ}", [last_z.pop(0)] if last_z else [])
            if not any(cores[0] + cores[1]) and not last_z and last_o:
                steps.append(last_o.pop(0))
        while any(cores[0] + cores[1]):
            core()
        steps += last_o
        steps += [f"ot:{n}" for n in range(4, 8)]
        for slot in range(4 * NQ):
            quarter(f"out:{4 + slot // NQ}:{slot % NQ}", [])
        return steps

    def tensors(self, net):
        self.v = net.sb("gd_v", [P, TT, GV * P])
        self.u = net.sb("gd_u", [P, 2, TT, 512])
        self.t = net.sb("gd_t", [P, 4, T])
        self.sg = net.sb("gd_sg", [P, 4, T])
        self.yba = net.sb("gd_ba", [P, TT, 32])
        self.a_row, self.dt_row = net.sb("gd_a", [P, GV]), net.sb("gd_dt", [P, GV])
        self.n_row = net.sb("gd_n", [P, P])
        self.beta, self.g = net.sb("gd_beta", [P, TT, GV]), net.sb("gd_g", [P, TT, GV])
        self.tb = net.sb("gd_tb", [P, TT, GV])
        self.G, self.eG, self.neG = (net.sb(f"gd_{n}", [P, TT, GV]) for n in ("G", "eG", "neG"))
        self.tail = net.sb("gd_tail", [P, GV])
        self.GT = net.sb("gd_GT", [GV, T])
        self.ones = net.sb("gd_ones", [P, P])
        self.tri = net.sb("gd_tri", [P, P])
        self.strict = net.sb("gd_strict", [P, P])
        self.before = net.sb("gd_before", [P, P])
        self.ss16 = net.sb("gd_ss", [P, TT * 4])
        with ExitStack() as alias:
            keep, net.ctx = net.ctx, alias
            self.qT, self.kT = net.sb("gd_qT", [P, GH, T]), net.sb("gd_kT", [P, GH, T])
            self.kn = net.sb("gd_kn", [P, GH, P])
            self.E, self.MT, self.Tm, self.U, self.X, self.QK = (
                [net.sb(f"gd_{n}{i}", [P, 4, P]) for i in range(2)] for n in ("E", "MT", "T", "U", "X", "QK"))
            net.ctx = keep
        self.o_hi = [net.x_hi, net.sb("gd_o_hi", [P, GV // 2, T], F32R)]
        self.o_lo = [net.x_lo, net.sb("gd_o_lo", [P, GV // 2, T], F32R)]
        self.ot_banks = [net.A[(2 * len(self.evacs)) % 3], net.A[3], net.G[0], net.G[1]]
        self.ML = self.E
        self.vn = self.X
        self.S = self.MT
        self.qs = self.Tm

    def pool(self, pool):
        net = self.net
        self.post.pool(pool)
        for dst, src in zip((self.a_row, self.dt_row, self.n_row), self.rows_dram):
            pool.dma_start(dst[:, :], src.partition_broadcast(P) if len(src.shape) == 1
                           else src[0].partition_broadcast(P)).then_inc(self.small_loaded.sem, 16)
        for step in self.steps:
            if step[0] != "core" or step[2] not in ("k1", "x5", "x4", "x3", "x2", "x1"):
                continue
            g, x = int(step[1]), step[2]
            i = g % 2
            if x == "k1":
                lev = 5
                pool.wait_ge(*self.C("dve", g)(3))
            else:
                lev = int(x[1]) - 1
                pool.wait_ge(*self.C("pe", g)(3 + 2 * (4 - lev)))
            pool.tensor_tensor(self.ML[i][:, :, :], self.MT[i][:, :, :],
                               net.level_f[:, lev, :].unsqueeze(1).to_broadcast([P, 4, P]), ALU.mult)\
                .then_inc(self.c_pool[i].sem, 1)

    def C(self, engine, g):
        sem, per = {"pe": (self.c_pe, 19), "act": (self.c_act, 12), "dve": (self.c_dve, 13),
                    "pool": (self.c_pool, 6)}[engine]
        return lambda n: sem[g % 2](per * (g // 2) + n)

    def sp(self, w):
        starts = {"q": 0, "k": D, "v": 2 * D, "z": 4 * D}
        for c in self.chunks:
            if c == "ba":
                w.load([KT, 32], self.w_in[:, 6 * D:6 * D + 32].rearrange("(k p) n -> p k n", p=P))
                continue
            at = starts[c[0]] + 512 * int(c[1])
            for h in range(2):
                w.load([4, 512], self.w_in[512 * h:512 * h + 512, at:at + 512].rearrange("(k p) n -> p k n", p=P))
        for h in range(8):
            w.load([2, D], self.w_out[256 * h:256 * h + 256, :].rearrange("(k p) n -> p k n", p=P))

    def a3_take(self, eng, step):
        n = self.a3.index(step)
        if n:
            kinds = ["dve" if x[0] == "conv" else "act" for x in self.a3[:n]]
            sem = self.a3_dve if kinds[-1] == "dve" else self.a3_act
            eng.wait_ge(*sem(kinds.count(kinds[-1])))
        return self.net.A[3]

    def a3_ready(self, eng, step):
        eng.wait_ge(*self.a3_pe(self.a3.index(step) + 1))

    def pe(self, w):
        net, pe = self.net, w.eng
        ident = net.ident
        self.pre.pe(pe)
        for step in self.steps:
            kind = step[0]
            if kind == "unit":
                c, h, q = step[1], int(step[2]), int(step[3])
                n = self.evacs.index(c)
                i = 2 * n
                if q % 2 == 0 and h == 0 and i + q // 2 > 2:
                    pe.wait_ge(*self.evacuated(i + q // 2 - 2))
                if n == 0 and q == 0:
                    pe.wait_ge(*self.pre.lo(KT))
                banks = [[net.A[i % 3]], [net.A[(i + 1) % 3]]]
                if c == "ba":
                    w.unit(net.x_hi, net.x_lo, 0, KT, 32, banks, True, True, quarter=q)
                else:
                    w.unit(net.x_hi, net.x_lo, 4 * h, 4, 512, banks, h == 0, h == 1, quarter=q)
            elif kind == "ba":
                if step[1] == "1":
                    bank = self.a3_take(pe, step)
                    pe.wait_ge(*self.ba["dve"](2))
                    pe.wait_ge(*self.ones_set(2))
                    for t in range(TT):
                        mm = pe.matmul(bank[:, t * GV:(t + 1) * GV], self.tri[:, :], self.g[:, t, :],
                                       start=True, stop=True)
                    mm.then_inc(self.a3_pe.sem, 1)
                elif step[1] == "2":
                    bank = self.a3_take(pe, step)
                    for t in range(TT):
                        pe.transpose(bank[0:GV, t * P:(t + 1) * P], self.G[:, t, :], ident[:, :])
                    pe.matmul(bank[:, T:T + GV], ident[:, P - 1:P].to_broadcast([P, P]), self.G[:, 0, :],
                              start=True, stop=True).then_inc(self.a3_pe.sem, 1)
            elif kind == "conv":
                c, part = step[1], int(step[2])
                bank = self.a3_take(pe, step)
                pe.wait_ge(*self.evacuated(2 * self.evacs.index(c) + 2))
                u = self.u[:, self.evacs.index(c) % 2]
                for kk in range(2):
                    for tt in range(TT):
                        k = 2 * part + kk
                        mm = pe.transpose(bank[:, kk * T + tt * P:kk * T + (tt + 1) * P],
                                          u[:, tt, k * P:(k + 1) * P], ident[:, :])
                mm.then_inc(self.a3_pe.sem, 1)
            elif kind == "norm":
                c, part = step[1], int(step[2])
                bank = self.a3_take(pe, step)
                pe.wait_ge(*self.squared(self.l2s.index(c) + 1))
                pe.matmul(bank[:, :], self.ones[:, :],
                          self.sg[:, 2 * part:2 * part + 2, :].rearrange("p k t -> p (k t)"),
                          start=True, stop=True).then_inc(self.a3_pe.sem, 1)
            elif kind == "kn":
                c = step[1]
                bank = self.a3_take(pe, step)
                pe.wait_ge(*self.l2(self.norms.index(("norm", c, "1")) + 1))
                for k in range(4):
                    mm = pe.transpose(bank[:, k * P:(k + 1) * P], self.kT[:, 4 * int(c[1]) + k, 0:P],
                                      ident[:, :])
                mm.then_inc(self.a3_pe.sem, 1)
            elif kind == "vt":
                c, t = step[1], int(step[2])
                bank = self.a3_take(pe, step)
                pe.wait_ge(*self.silued(self.silus.index(c) + 1))
                for k in range(4):
                    mm = pe.transpose(bank[:, k * P:(k + 1) * P], self.t[:, k, t * P:(t + 1) * P], ident[:, :])
                mm.then_inc(self.a3_pe.sem, 1)
            elif kind == "core":
                self.core_pe(pe, int(step[1]), step[2])
            elif kind == "ot":
                n = int(step[1])
                bank = self.ot_banks[n % 2 + 2 * (n >= 4)]
                pe.wait_ge(*self.o_ready(n // 2 + 1))
                if n == 0:
                    pe.wait_ge(*self.evacuated(2 * len(self.evacs) - 2))
                    pe.wait_ge(*self.a3_act(self.act_reads(self.a3[-1])))
                if n == 4:
                    pe.wait_ge(*self.o_ready(4))
                if n >= 2:
                    pe.wait_ge(*self.o_lo_ready(n - 1))
                for kk in range(2):
                    for tt in range(TT):
                        k = 2 * n + kk
                        mm = pe.transpose(bank[:, kk * T + tt * P:kk * T + (tt + 1) * P],
                                          self.v[:, tt, k * P:(k + 1) * P], ident[:, :])
                mm.then_inc(self.o_turned.sem, 1)
            elif kind == "out":
                h, q = int(step[1]), int(step[2])
                if q == 0:
                    pe.wait_ge(*self.o_lo_ready(h + 1 if h else 4))
                    if h == 0:
                        pe.wait_ge(*self.evacuated(2 * len(self.evacs)))
                w.unit(self.o_hi[h // 4], self.o_lo[h // 4], 2 * (h % 4), 2, 512, [net.A[0:2], net.A[2:4]],
                       h == 0, h == 7, pieces=2, quarter=q)

    def core_pe(self, pe, g, x):
        net = self.net
        i = g % 2
        bg, bm = net.G[i], net.M[i]
        act, dve, pool = (self.C(n, g) for n in ("act", "dve", "pool"))
        tile = lambda t: slice(t * P, (t + 1) * P)
        four = [(j, t, 2 * j + t) for j in range(2) for t in range(TT)]
        kT, qT = self.kT[:, g, :], self.qT[:, g, :]
        if x == "k0":
            pe.wait_ge(*self.l2(self.norms.index(("norm", f"k{g // 4}", "1")) + 1))
            if g == 0 or g == 1:
                pe.wait_ge(*self.ba["act"](3))
            if g >= 2:
                prev_act, prev_dve = self.C("act", g - 2), self.C("dve", g - 2)
                pe.wait_ge(*prev_act(12))
                pe.wait_ge(*prev_dve(13))
            for t in range(TT):
                pe.matmul(bg[:, tile(t)], kT[:, tile(t)], kT[:, tile(t)], start=True, stop=True)
                pe.matmul(bg[:, tile(2 + t)], kT[:, tile(t)], qT[:, tile(t)], start=True, stop=True)
            for j, t, n in four:
                h = 2 * g + j
                mm = pe.matmul(bm[:, tile(n)], net.ident[0:GV, h:h + 1].to_broadcast([GV, P]),
                               self.GT[:, tile(t)], start=True, stop=True)
        elif x == "k1":
            pe.wait_ge(*dve(4))
            for n in range(4):
                mm = pe.transpose(bm[:, tile(n)], self.U[i][:, n, :], net.ident[:, :])
        elif x[0] == "x":
            lev = int(x[1])
            pe.wait_ge(*pool(1 + 5 - lev))
            if lev == 5:
                pe.wait_ge(*act(2))
            else:
                pe.wait_ge(*dve(5 + 4 - lev))
            for n in range(4):
                mm = pe.matmul(bg[:, n * P:(n + 1) * P], self.ML[i][:, n, :], self.Tm[i][:, n, :],
                               start=True, stop=True)
        elif x[0] == "t":
            lev = int(x[1])
            s = LEVELS[lev]
            pe.wait_ge(*act(3 + 5 - lev))
            for n in range(4):
                if lev:
                    left = self.X[i][:, n, :].rearrange("p (b h r) -> p b h r", h=2, r=s)[:, :, 0, :]
                    pe.matmul(bm[:, n * 64:(n + 1) * 64], self.U[i][:, n, :], left, start=True, stop=True)
                right = self.U[i][:, n, :].rearrange("p (b h r) -> p b h r", h=2, r=s)[:, :, 1, :]
                mm = pe.matmul(bm[:, T + n * 64:T + (n + 1) * 64], self.X[i][:, n, :], right,
                               start=True, stop=True)
        elif x == "p0":
            pe.wait_ge(*dve(10))
            pe.wait_ge(*self.a3_act(self.vt_read(g)))
            for j in range(2):
                h = 2 * g + j
                mm = pe.matmul(bg[:, tile(j)], self.U[i][:, 2 * j, :], self.v[:, 0, h * P:(h + 1) * P],
                               start=True, stop=True)
        elif x == "p1":
            pe.wait_ge(*act(9))
            pe.wait_ge(*dve(11))
            for j in range(2):
                pe.matmul(bm[:, tile(j)], self.QK[i][:, 2 * j, :], self.vn[i][:, j, :], start=True, stop=True)
                mm = pe.matmul(bm[:, tile(2 + j)], self.kn[:, g, :], self.S[i][:, 2 + j, :],
                               start=True, stop=True)
        elif x == "p2":
            pe.wait_ge(*act(10))
            S = self.S[i][:, 0:2, :].rearrange("p j e -> p (j e)")
            pe.matmul(bg[:, 0:T], kT[:, tile(1)], S, start=True, stop=True)
            mm = pe.matmul(bg[:, T:2 * T], qT[:, tile(1)], S, start=True, stop=True)
        elif x == "p3":
            pe.wait_ge(*dve(12))
            for j in range(2):
                mm = pe.matmul(bm[:, tile(j)], self.U[i][:, 2 * j + 1, :], self.S[i][:, 2 + j, :],
                               start=True, stop=True)
        elif x == "p4":
            pe.wait_ge(*act(12))
            for j in range(2):
                mm = pe.matmul(bm[:, tile(2 + j)], self.QK[i][:, 2 * j + 1, :], self.vn[i][:, 2 + j, :],
                               start=True, stop=True)
        mm.then_inc(self.c_pe[i].sem, 1)

    def vt_read(self, g):
        step = ("vt", f"v{g // 2}", "1")
        n = self.a3.index(step)
        return len([x for x in self.a3[:n + 1] if x[0] != "conv"])

    def act(self, w):
        net, act = self.net, w.eng
        self.pre.act(w)
        self.pre.act_r(w)
        act.wait_ge(*self.pre.r_ready(1))
        for step in self.steps:
            kind = step[0]
            if kind in ("unit", "out"):
                if int(step[-1]) < 2:
                    w.split_hi(int(step[-1]))
            elif kind == "evac":
                c = step[1]
                n = self.evacs.index(c)
                act.wait_ge(net.unit_used, self.u0 + 2 * n + 1)
                if c == "ba":
                    dst = self.yba
                else:
                    dst = self.u[:, n % 2]
                    if c[0] == "z" and int(c[1]) >= 2:
                        act.wait_ge(*self.o_ready(int(c[1]) - 1))
                for tt in range(TT):
                    act.activation(dst[:, tt, :], net.A[(2 * n + tt) % 3][:, 0:dst.shape[2]], ACT.Copy,
                                   scale=net.r[:, tt:tt + 1]).then_inc(self.evacuated.sem, 1)
            elif kind == "ba":
                sem = self.ba["act"]
                if step[1] == "0":
                    act.wait_ge(*self.ba["dve"](1))
                    act.wait_ge(*self.small_loaded(48))
                    w.chain(act.activation(self.beta[:, :, :], self.beta[:, :, :], ACT.Exp, scale=-1.0))
                    w.chain(act.activation(self.beta[:, :, :], self.beta[:, :, :], ACT.Ln, bias=1.0))
                    w.chain(act.activation(self.beta[:, :, :], self.beta[:, :, :], ACT.Exp, scale=-1.0))
                    w.chain(act.activation(self.tb[:, :, :], self.g[:, :, :], ACT.Abs))
                    w.chain(act.activation(self.tb[:, :, :], self.tb[:, :, :], ACT.Exp, scale=-1.0))
                    w.chain.mark(act.activation(self.tb[:, :, :], self.tb[:, :, :], ACT.Ln, bias=1.0))
                    act.activation(self.a_row[:, :], self.a_row[:, :], ACT.Exp).then_inc(sem.sem, 1)
                elif step[1] == "1":
                    self.a3_ready(act, step)
                    act.activation(self.G[:, :, :], net.A[3][:, 0:TT * GV].rearrange("p (t h) -> p t h", t=TT),
                                   ACT.Copy).then_inc(self.a3_act.sem, 1)
                    act.wait_ge(*self.a3_act(1))
                    w.chain(act.activation(self.eG[:, :, :], self.G[:, :, :], ACT.Exp))
                    act.activation(self.neG[:, :, :], self.eG[:, :, :], ACT.Copy, scale=-1.0).then_inc(sem.sem, 1)
                elif step[1] == "2":
                    self.a3_ready(act, step)
                    w.chain.mark(act.activation(self.GT[:, :], net.A[3][0:GV, 0:T], ACT.Copy))
                    act.activation(self.tail[:, :], net.A[3][:, T:T + GV], ACT.Copy).then_inc(self.a3_act.sem, 1)
                elif step[1] == "3":
                    act.wait_ge(*self.ba["dve"](3))
                    act.activation(self.tail[:, :], self.tail[:, :], ACT.Exp).then_inc(sem.sem, 1)
            elif kind == "conv":
                c, part = step[1], int(step[2])
                self.a3_ready(act, step)
                n = self.silus.index(c)
                if n and part == 0:
                    before = self.silus[n - 1]
                    if before[0] == "v":
                        act.wait_ge(*self.a3_act(self.act_reads(("vt", before, "1"))))
                    else:
                        act.wait_ge(*self.l2(self.norms.index(("norm", before, "1")) + 1))
                for kk in range(2):
                    at = (self.width - 1) * self.ctiles + self.ctile(c) + 2 * part + kk
                    ins = act.activation(self.t[:, 2 * part + kk, :], net.A[3][:, kk * T:(kk + 1) * T],
                                         ACT.Copy, scale=self.taps[:, at:at + 1])
                ins.then_inc(self.tapped.sem, 1)
            elif kind == "silu":
                if step[2] == "0":
                    act.wait_ge(*self.clamped(self.silus.index(step[1]) + 1))
                    w.chain(act.activation(self.sg[:, :, :], self.sg[:, :, :], ACT.Exp, scale=-1.0))
                    w.chain.mark(act.activation(self.sg[:, :, :], self.sg[:, :, :], ACT.Ln, bias=1.0))
                elif step[2] == "1":
                    w.chain.sync()
                    act.activation(self.sg[:, :, :], self.sg[:, :, :], ACT.Exp, scale=-1.0)\
                       .then_inc(self.sigm.sem, 1)
            elif kind == "l2":
                act.wait_ge(*self.silued(self.silus.index(step[1]) + 1))
                act.activation(self.sg[:, :, :], self.t[:, :, :], ACT.Square).then_inc(self.squared.sem, 1)
            elif kind == "norm":
                self.a3_ready(act, step)
                half = self.sg[:, 2 * int(step[2]):2 * int(step[2]) + 2, :].rearrange("p k t -> p (k t)")
                act.activation(half, net.A[3][:, :], ACT.Ln, bias=EPS).then_inc(self.a3_act.sem, 1)
                act.wait_ge(*self.a3_act(self.act_reads(step)))
                act.activation(half, half, ACT.Exp, scale=-0.5).then_inc(self.rsq.sem, 1)
            elif kind == "kn":
                self.a3_ready(act, step)
                first = 4 * int(step[1][1])
                act.activation(self.kn[:, first:first + 4, :], net.A[3][:, :], ACT.Copy).then_inc(self.a3_act.sem, 1)
            elif kind == "vt":
                self.a3_ready(act, step)
                first = 512 * int(step[1][1])
                act.activation(self.v[:, int(step[2]), first:first + 512], net.A[3][:, :], ACT.Copy)\
                   .then_inc(self.a3_act.sem, 1)
            elif kind == "core":
                self.core_act(w, int(step[1]), step[2])
            elif kind == "z1":
                i = int(step[1][1])
                z = self.sg[:, :, :].rearrange("p (t k) n -> p t (k n)", t=TT)
                if step[2] == "0":
                    act.wait_ge(*self.z_clamped(i + 1))
                    w.chain(act.activation(z, z, ACT.Exp, scale=-1.0))
                    w.chain.mark(act.activation(z, z, ACT.Ln, bias=1.0))
                elif step[2] == "1":
                    w.chain.sync()
                    act.activation(z, z, ACT.Exp, scale=-1.0).then_inc(self.z_sigm.sem, 1)
            elif kind == "z2" and step[2] == "0":
                i = int(step[1][1])
                act.wait_ge(*self.o_sq(i + 1))
                w.chain(act.activation(self.ss16[:, :], self.ss16[:, :], ACT.Ln, scale=1.0 / P, bias=EPS))
                act.activation(self.ss16[:, :], self.ss16[:, :], ACT.Exp, scale=-0.5).then_inc(self.o_r.sem, 1)
            elif kind == "ot":
                n = int(step[1])
                act.wait_ge(*self.o_turned(n + 1))
                at = 2 * (n % 4)
                act.activation(self.o_hi[n // 4][:, at:at + 2, :], self.ot_banks[n % 2 + 2 * (n >= 4)][:, :], ACT.Copy)\
                   .then_inc(self.o_hi_ready.sem, 1)
        self.post.act(w)

    def act_reads(self, step):
        n = self.a3.index(step)
        return len([x for x in self.a3[:n + 1] if x[0] != "conv"])

    def ctile(self, c):
        return {"q": 0, "k": GH, "v": 2 * GH}[c[0]] + 4 * int(c[1])

    def core_act(self, w, g, x):
        net, act = self.net, w.eng
        i = g % 2
        bg, bm = net.G[i], net.M[i]
        pe, dve = self.C("pe", g), self.C("dve", g)
        own = self.C("act", g)
        heads = slice(2 * g * P, (2 * g + 2) * P)
        tile = lambda t: slice(t * P, (t + 1) * P)
        if x == "k0":
            act.wait_ge(*dve(1))
            ins = act.activation(self.E[i][:, :, :], self.E[i][:, :, :], ACT.Exp)
        elif x == "k1":
            act.wait_ge(*pe(2))
            ins = act.activation(self.Tm[i][:, :, :], bm[:, :], ACT.Copy)
        elif x[0] == "x":
            act.wait_ge(*pe(3 + 2 * (5 - int(x[1]))))
            ins = act.activation(self.X[i][:, :, :], bg[:, :], ACT.Copy)
        elif x == "p0":
            act.wait_ge(*pe(15))
            for j in range(2):
                h = 2 * g + j
                ins = act.activation(self.vn[i][:, j, :], bg[:, tile(j)], ACT.Copy,
                                     scale=self.beta[:, 0, h:h + 1])
        elif x == "p1":
            act.wait_ge(*pe(16))
            w.chain.mark(act.activation(self.v[:, 0, heads], bm[:, 0:T], ACT.Copy))
            ins = act.activation(self.S[i][:, 0:2, :], bm[:, T:2 * T], ACT.Copy)
        elif x == "p2":
            act.wait_ge(*pe(17))
            act.wait_ge(*dve(12))
            for j in range(2):
                h = 2 * g + j
                ins = act.activation(self.qs[i][:, j, :], bg[:, tile(2 + j)], ACT.Copy,
                                     scale=self.eG[:, 1, h:h + 1])
        elif x == "p3":
            act.wait_ge(*pe(18))
            for j in range(2):
                h = 2 * g + j
                ins = act.activation(self.vn[i][:, 2 + j, :], bm[:, tile(j)], ACT.Copy,
                                     scale=self.beta[:, 1, h:h + 1])
        else:
            return
        ins.then_inc(self.c_act[i].sem, 1)

    def dve(self, w):
        net, dve = self.net, w.eng
        w.chain(dve.memset(self.ones[:, :], 1.0))
        dve.wait_ge(net.consts, net.masks_at)
        dve.tensor_reduce(self.strict[:, :], net.level_f[:, :, :].rearrange("p l c -> p c l"), AX.X, ALU.add)\
           .then_inc(self.ones_set.sem, 1)
        dve.wait_ge(*self.ones_set(1))
        dve.tensor_tensor(self.tri[:, :], self.strict[:, :], net.ident[:, :], ALU.add).then_inc(self.ones_set.sem, 1)
        dve.wait_ge(*self.ones_set(2))
        w.chain(dve.tensor_scalar(self.before[:, :], self.tri[:, :], 1.0, 1e30, ALU.subtract, ALU.mult))
        self.pre.dve(w)
        for step in self.steps:
            kind = step[0]
            if kind in ("unit", "out"):
                if int(step[-1]) >= 2:
                    w.split_lo(int(step[-1]) - 2)
            elif kind == "ba":
                sem = self.ba["dve"]
                if step[1] == "0":
                    dve.wait_ge(*self.evacuated(2))
                    dve.wait_ge(*self.small_loaded(48))
                    w.chain.mark(dve.tensor_scalar(self.beta[:, :, :], self.yba[:, :, 0:GV], CLAMP, None, ALU.max))
                    dve.tensor_tensor(self.g[:, :, :], self.yba[:, :, GV:2 * GV],
                                      self.dt_row[:, :].unsqueeze(1).to_broadcast([P, TT, GV]), ALU.add)\
                       .then_inc(sem.sem, 1)
                    dve.wait_ge(*self.ba["act"](1))
                    w.chain(dve.scalar_tensor_tensor(out=self.tb[:, :, :], in0=self.g[:, :, :], scalar=0.0,
                                                     in1=self.tb[:, :, :], op0=ALU.max, op1=ALU.add))
                    for t in range(TT):
                        ins = dve.scalar_tensor_tensor(out=self.g[:, t, :], in0=self.tb[:, t, :], scalar=-1.0,
                                                       in1=self.a_row[:, :], op0=ALU.mult, op1=ALU.mult)
                        if t == 0:
                            w.chain.mark(ins)
                    ins.then_inc(sem.sem, 1)
                elif step[1] == "2":
                    dve.wait_ge(*self.a3_act(self.act_reads(step)))
                    dve.tensor_tensor(self.tail[:, :], self.tail[:, :], self.G[:, 0, :], ALU.subtract)\
                       .then_inc(sem.sem, 1)
            elif kind == "conv":
                c, part = step[1], int(step[2])
                n = 2 * self.silus.index(c) + part
                dve.wait_ge(*self.tapped(n + 1))
                for back in range(1, self.width):
                    for kk in range(2):
                        at = (self.width - 1 - back) * self.ctiles + self.ctile(c) + 2 * part + kk
                        row = self.t[:, 2 * part + kk, back:T]
                        ins = dve.scalar_tensor_tensor(out=row, in0=net.A[3][:, kk * T:(kk + 1) * T - back],
                                                       scalar=self.taps[:, at:at + 1], in1=row,
                                                       op0=ALU.mult, op1=ALU.add)
                        if back == self.width - 1 and kk == 1:
                            ins.then_inc(self.a3_dve.sem, 1)
                        else:
                            w.chain.mark(ins)
                    if back < self.width - 1:
                        w.chain.sync()
                dve.wait_ge(*self.a3_dve(n + 1))
            elif kind == "silu":
                n = self.silus.index(step[1])
                if step[2] == "0":
                    if n and self.silus[n - 1][0] != "v":
                        dve.wait_ge(*self.l2(self.norms.index(("norm", self.silus[n - 1], "1")) + 1))
                    dve.tensor_scalar(self.sg[:, :, :], self.t[:, :, :], CLAMP, None, ALU.max)\
                       .then_inc(self.clamped.sem, 1)
                elif step[2] == "2":
                    dve.wait_ge(*self.sigm(n + 1))
                    dve.tensor_tensor(self.t[:, :, :], self.t[:, :, :], self.sg[:, :, :], ALU.mult)\
                       .then_inc(self.silued.sem, 1)
            elif kind == "norm":
                c, part = step[1], int(step[2])
                dve.wait_ge(*self.rsq(self.norms.index(step) + 1))
                half = slice(2 * part, 2 * part + 2)
                first = 4 * int(c[1]) + 2 * part
                dst = (self.qT if c[0] == "q" else self.kT)[:, first:first + 2, :].rearrange("p k t -> p (k t)")
                dve.scalar_tensor_tensor(out=dst, in0=self.t[:, half, :].rearrange("p k t -> p (k t)"),
                                         scalar=P ** -0.5 if c[0] == "q" else 1.0,
                                         in1=self.sg[:, half, :].rearrange("p k t -> p (k t)"),
                                         op0=ALU.mult, op1=ALU.mult).then_inc(self.l2.sem, 1)
            elif kind == "core":
                self.core_dve(w, int(step[1]), step[2])
            elif kind == "z1":
                i = int(step[1][1])
                n = self.evacs.index(step[1])
                z = self.sg[:, :, :].rearrange("p (t k) n -> p t (k n)", t=TT)
                u = self.u[:, n % 2]
                if step[2] == "0":
                    dve.wait_ge(*self.evacuated(2 * n + 2))
                    dve.wait_ge(*self.silued(len(self.silus)))
                    dve.tensor_scalar(z, u, CLAMP, None, ALU.max).then_inc(self.z_clamped.sem, 1)
                elif step[2] == "2":
                    dve.wait_ge(*self.z_sigm(i + 1))
                    w.chain.mark(dve.tensor_tensor(u, u, z, ALU.mult))
            elif kind == "z2":
                i = int(step[1][1])
                n = self.evacs.index(step[1])
                u = self.u[:, n % 2]
                o = self.v[:, :, 512 * i:512 * (i + 1)]
                w.chain.sync()
                if step[2] == "0":
                    dve.wait_ge(*self.C("act", 2 * i + 1)(12))
                    dve.wait_ge(*self.C("dve", 2 * i)(13))
                    dve.wait_ge(*self.C("dve", 2 * i + 1)(13))
                    w.chain(dve.tensor_tensor(net.tmp[:, :, :], o, o, ALU.mult))
                    dve.tensor_reduce(self.ss16[:, :].rearrange("p (t h) -> p t h", t=TT),
                                      net.tmp[:, :, :].rearrange("p t (h e) -> p t h e", e=P), AX.X, ALU.add)\
                       .then_inc(self.o_sq.sem, 1)
                elif step[2] == "1":
                    for tt in range(TT):
                        z = u[:, tt, :].rearrange("p (h e) -> p h e", e=P)
                        w.chain.mark(dve.tensor_tensor(z, z, self.n_row[:, :].unsqueeze(1)
                                                       .to_broadcast([P, 4, P]), ALU.mult))
                    dve.wait_ge(*self.o_r(i + 1))
                    for tt in range(TT):
                        oh = o[:, tt, :].rearrange("p (h e) -> p h e", e=P)
                        r = self.ss16[:, 4 * tt:4 * tt + 4].unsqueeze(2).to_broadcast([P, 4, P])
                        w.chain.mark(dve.tensor_tensor(oh, oh, r, ALU.mult))
                else:
                    dve.tensor_tensor(o, o, u, ALU.mult).then_inc(self.o_ready.sem, 1)
            elif kind == "ot":
                n = int(step[1])
                dve.wait_ge(*self.o_hi_ready(n + 1))
                at = slice(2 * (n % 4), 2 * (n % 4) + 2)
                dve.tensor_tensor(self.o_lo[n // 4][:, at, :], self.ot_banks[n % 2 + 2 * (n >= 4)][:, :],
                                  self.o_hi[n // 4][:, at, :].bitcast(F32), ALU.subtract)\
                   .then_inc(self.o_lo_ready.sem, 1)
        self.post.dve(w)

    def core_dve(self, w, g, x):
        net, dve = self.net, w.eng
        i = g % 2
        bg, bm = net.G[i], net.M[i]
        pe, act, pool, own = (self.C(n, g) for n in ("pe", "act", "pool", "dve"))
        sem = self.c_dve[i]
        tile = lambda t: slice(t * P, (t + 1) * P)
        four = [(2 * g + j, t, 2 * j + t) for j in range(2) for t in range(TT)]
        if x == "k0":
            dve.wait_ge(*pe(1))
            if g >= 2:
                dve.wait_ge(*self.C("pool", g - 2)(6))
                dve.wait_ge(*self.C("pe", g - 2)(19))
            for h, t, n in four:
                ins = dve.scalar_tensor_tensor(out=self.E[i][:, n, :], in0=bm[:, tile(n)],
                                               scalar=self.G[:, t, h:h + 1], in1=self.before[:, :],
                                               op0=ALU.subtract, op1=ALU.min)
            ins.then_inc(sem.sem, 1)
            dve.wait_ge(*act(1))
            for h, t, n in four:
                ins = dve.scalar_tensor_tensor(out=self.MT[i][:, n, :], in0=bg[:, tile(t)],
                                               scalar=self.beta[:, t, h:h + 1], in1=self.E[i][:, n, :],
                                               op0=ALU.mult, op1=ALU.mult)
                if n < 3:
                    w.chain.mark(ins)
            ins.then_inc(sem.sem, 1)
            for j in range(2):
                ins = dve.tensor_tensor(self.QK[i][:, 2 * j:2 * j + 2, :], self.E[i][:, 2 * j:2 * j + 2, :],
                                        bg[:, T:2 * T].rearrange("p (t c) -> p t c", t=TT), ALU.mult)
                if j == 0:
                    w.chain.mark(ins)
            ins.then_inc(sem.sem, 1)
        elif x == "k1":
            dve.wait_ge(*own(2))
            w.chain(dve.tensor_tensor(self.U[i][:, :, :], self.MT[i][:, :, :],
                                      net.level_f[:, 6, :].unsqueeze(1).to_broadcast([P, 4, P]), ALU.mult))
            dve.tensor_tensor(self.U[i][:, :, :], net.ident[:, :].unsqueeze(1).to_broadcast([P, 4, P]),
                              self.U[i][:, :, :], ALU.subtract).then_inc(sem.sem, 1)
        elif x[0] == "t":
            lev = int(x[1])
            s = LEVELS[lev]
            dve.wait_ge(*pe(4 + 2 * (5 - lev)))

            def take(m, right, at):
                half = m[:, :, :].rearrange("p n c -> p (n c)")\
                    .rearrange("p (b h r) -> p b h r", h=2, r=s)[:, :, right, :]
                part = bm[:, at:at + T].rearrange("p (b r) -> p b r", r=s)
                return dve.tensor_tensor(half, half, part, ALU.subtract)
            dve.wait_ge(*own(4 + 5 - lev))
            if lev:
                w.chain.mark(take(self.Tm[i], 0, 0))
            take(self.U[i], 1, T).then_inc(sem.sem, 1)
        elif x == "p0":
            dve.wait_ge(*act(9))
            for j in range(2):
                h = 2 * g + j
                ins = dve.tensor_scalar(self.S[i][:, 2 + j, :], self.vn[i][:, j, :], self.tail[:, h:h + 1],
                                        None, ALU.mult)
                if j == 0:
                    w.chain.mark(ins)
            ins.then_inc(sem.sem, 1)
        elif x == "p2":
            dve.wait_ge(*pe(17))
            for j in range(2):
                h = 2 * g + j
                ins = dve.scalar_tensor_tensor(out=self.S[i][:, 2 + j, :], in0=bg[:, tile(j)],
                                               scalar=self.neG[:, 1, h:h + 1],
                                               in1=self.v[:, 1, h * P:(h + 1) * P], op0=ALU.mult, op1=ALU.add)
                if j == 0:
                    w.chain.mark(ins)
            ins.then_inc(sem.sem, 1)
        elif x == "p4":
            dve.wait_ge(*pe(19))
            dve.wait_ge(*act(11))
            dve.tensor_tensor(self.v[:, 1, 2 * g * P:(2 * g + 2) * P],
                              self.qs[i][:, 0:2, :].rearrange("p j e -> p (j e)"), bm[:, T:2 * T], ALU.add)\
               .then_inc(sem.sem, 1)


def program(nc, dram, out, only=None):
    with ExitStack() as ctx:
        net = Net(nc, ctx, dram)
        x_in, out_t = dram["x"][0].rearrange("(t p) d -> p t d", p=P), out[0].rearrange("(t p) d -> p t d", p=P)
        phases, ready, step, brow_free = [], net.x_in, 16, None

        def gain(ap):
            return net.columns(ap.rearrange("(k p) -> k p", p=P))

        plan = only or ["block0", "block1", "ffn00", "conv", "ffn01", "ffn10", "gdn", "ffn11"]
        for what in plan:
            phase_ctx = ExitStack()
            if what.startswith("ffn"):
                i, s = int(what[3]), int(what[4])
                g = dram["norm_g_2"][i]
                ph = Ffn(net, what, dram["ffn_w_gate_up_2"][i, s], dram["ffn_w_down_2"][i, s],
                         gain(g[4 * s]), g[4 * s + 1], ready, step, brow_free, what == plan[-1])
                brow_free = ph.x_ready
            elif what.startswith("block"):
                ph = Block(net, what, int(what[5]), dram, gain, ready, step)
                ph.prev = phases[-1] if phases else None
                if not phases:
                    ph.x_before = None
            elif what == "conv":
                ph = Conv(net, what, dram, gain, ready, step, brow_free)
                brow_free = ph.x_ready
            else:
                ph = Gdn(net, what, dram, gain, ready, step, brow_free)
                brow_free = ph.x_ready
            with phase_ctx:
                net.ctx, net.prefix = phase_ctx, f"{what}_"
                ph.tensors(net)
            net.ctx = ctx
            ready, step = ph.x_ready, 1
            phases.append(ph)

        block = ctx.enter_context(nc.Block())

        @block.sync
        def _(sp):
            w = Walk(net, sp)
            sp.dma_start(net.x[:, :, 0:512], x_in[:, :, 0:512]).then_inc(net.x_in.sem, 16)
            sp.wait_ge(*net.x_in(16))
            sp.dma_start(net.x[:, :, 512:D], x_in[:, :, 512:D]).then_inc(net.x_in.sem, 16)
            for ph in phases:
                ph.sp(w)
            for c in range(2):
                sp.wait_ge(*ready(c + 1))
                sp.dma_start(out_t[:, :, c * 512:(c + 1) * 512], net.x[:, :, c * 512:(c + 1) * 512])\
                  .then_inc(net.out_done, 16)
            sp.wait_ge(net.out_done, 32)

        @block.gpsimd
        def _(pool):
            c = Chain(pool, net.consts)
            c(pool.memset(net.ident[:, :], 0.0))
            c(pool.affine_select(out=net.ident[:, :], in_=net.ident[:, :], compare_op=ALU.not_equal,
                                 fill=1.0, base=0, pattern=[[-1, P]], channel_multiplier=1))
            c(pool.memset(net.zeros[:, :], 0.0))
            c(pool.memset(net.level_f[:, :, :], 0.0))
            for lev, s in enumerate(LEVELS):
                right = net.level_f[:, lev, :].rearrange("p (b h r) -> p b h r", h=2, r=s)[:, :, 1, :]
                c(pool.memset(right, 1.0))
                c(pool.affine_select(out=right, in_=right, compare_op=ALU.is_ge, fill=0.0, base=0,
                                     pattern=[[-2 * s, P // (2 * s)], [0, s]], channel_multiplier=1))
                c(pool.affine_select(out=right, in_=right, compare_op=ALU.is_ge, fill=0.0, base=s - 1,
                                     pattern=[[2 * s, P // (2 * s)], [0, s]], channel_multiplier=-1))
                for t in range(TT):
                    c.mark(pool.tensor_copy(
                        net.level_u8[:, lev, t * 64:(t + 1) * 64].rearrange("p (b r) -> p b r", r=s), right))
            for t in range(TT):
                c.mark(pool.tensor_copy(net.diag_u8[:, t * P:(t + 1) * P], net.ident[:, :]))
            c.mark(pool.iota(net.neg_dist[:, 0:P], [[1, P]], base=0, channel_multiplier=-1,
                             allow_small_or_imprecise_dtypes=True))
            c(pool.iota(net.neg_dist[:, P:P + T], [[1, T]], base=-P, channel_multiplier=-1,
                        allow_small_or_imprecise_dtypes=True))
            c.mark(pool.affine_select(out=net.neg_dist[:, 0:P], in_=net.neg_dist[:, 0:P],
                                      compare_op=ALU.is_ge, fill=-1e30, base=0, pattern=[[-1, P]],
                                      channel_multiplier=1))
            c(pool.affine_select(out=net.neg_dist[:, P:P + T], in_=net.neg_dist[:, P:P + T],
                                 compare_op=ALU.is_ge, fill=-1e30, base=P, pattern=[[-1, T]],
                                 channel_multiplier=1))
            net.masks_at = c.n
            for ph in phases:
                ph.pool(pool)

        @block.scalar
        def _(act):
            w = Walk(net, act, net.act_chain)
            act.wait_ge(net.rows_clear, 1)
            for dst, src in net.row_loads:
                act.dma_start(dst, src).then_inc(net.params, 16)
            act.preload_act_table_set("natural_log_exp_and_others")
            for _ in range(LEAD):
                w.split_hi()
            act.wait_ge(net.rows_turned, 1)
            act.activation(net.cols[:, :, :], net.M[1][:, 0:2 * P], ACT.Copy).then_inc(net.cols_ready, 1)
            act.wait_ge(net.cols_ready, 1)
            for ph in phases:
                ph.act(w)

        @block.vector
        def _(dve):
            w = Walk(net, dve, net.dve_chain)
            dve.memset(net.rows[:, :, :], 0.0).then_inc(net.rows_clear, 1)
            for _ in range(LEAD):
                w.split_lo()
            dve.wait_ge(net.cols_ready, 1)
            for ph in phases:
                ph.dve(w)

        @block.tensor
        def _(pe):
            w = Walk(net, pe)
            pe.wait_ge(net.consts, 3)
            pe.wait_ge(net.rows_clear, 1)
            pe.wait_ge(net.params, 16 * len(net.row_loads))
            for side in range(2):
                mm = pe.transpose(net.M[1][:, side * P:(side + 1) * P], net.rows[:, side, :], net.ident[:, :])
            mm.then_inc(net.rows_turned, 1)
            pe.wait_ge(net.cols_ready, 1)
            for ph in phases:
                ph.pe(w)


INPUTS = ["x", "mem", "g_pre", "w_in", "g_q_moba", "g_k_moba", "w_gate_up", "b_gate_up", "g_gla_out",
          "g_mem", "w_mem_kv", "g_q_mem", "g_k_mem", "w_out", "norm_g_2", "ffn_w_gate_up_2",
          "ffn_w_down_2", "sc_w_in_2", "sc_conv_w_2", "sc_w_out_2", "gdn_w_in_2", "gdn_conv_w_2",
          "gdn_a_log_2", "gdn_dt_bias_2", "gdn_norm_w_2", "gdn_w_out_2"]


def kernel(**inputs):
    import concourse.bacc as bacc
    from concourse.bass_utils import run_bass_kernel_spmd

    nc = bacc.Bacc("TRN2", target_bir_lowering=False, num_devices=1)
    arrays, dram = {}, {}
    for name in INPUTS:
        arrays[f"in_{name}"] = np.ascontiguousarray(inputs[name])
        dram[name] = nc.dram_tensor(f"in_{name}", arrays[f"in_{name}"].shape, F32, kind="ExternalInput").ap()
    out = nc.dram_tensor("out", (1, T, D), F32, kind="ExternalOutput").ap()
    program(nc, dram, out)
    return run_bass_kernel_spmd(nc, [arrays], core_ids=[0]).results[0]["out"]
```

```python
import numpy as np
import concourse.bass as bass
from concourse import mybir
from contextlib import ExitStack

F32 = mybir.dt.float32
F32R = mybir.dt.float32r
BF16 = mybir.dt.bfloat16
U8 = mybir.dt.uint8
ACT = mybir.ActivationFunctionType
ALU = mybir.AluOpType
AX = mybir.AxisListType

P = 128
T = 256
TT = T // P
D = 1024
KT = D // P
EPS = 1e-6
RING = 3
SLOT = 2048
LEAD = 2


class Chain:

    def __init__(self, eng, sem):
        self.eng, self.sem, self.n, self.it, self.per = eng, sem, 0, None, 0

    def mark(self, ins):
        self.n += 1
        ins.then_inc(self.sem, 1)

    def sync(self):
        self.eng.wait_ge(self.sem, self.n if self.it is None else self.it * self.per + self.n)

    def __call__(self, ins):
        self.mark(ins)
        self.sync()

    def enter(self, it, per):
        self.it, self.per, self.start = it, per, self.n

    def leave(self, trips):
        assert self.n - self.start == self.per, (self.n - self.start, self.per)
        self.n = self.start + trips * self.per
        self.it = None


class Signal:

    def __init__(self, sem, base):
        self.sem, self.base = sem, base

    def __call__(self, n):
        return self.sem, self.base + n


class Net:

    def __init__(self, nc, ctx, dram):
        self.nc, self.dram = nc, dram
        self.ctx, self.prefix, self.shared = ctx, "", {}
        self.raw = self.sb("raw", [P, RING, SLOT])
        self.w_hi = self.sb("w_hi", [P, RING, SLOT], F32R)
        self.w_lo = self.sb("w_lo", [P, RING, SLOT], F32R)
        self.x = self.sb("x", [P, TT, D])
        self.x_hi = self.sb("x_hi", [P, KT, T], F32R)
        self.x_lo = self.sb("x_lo", [P, KT, T], F32R)
        self.ident = self.sb("ident", [P, P])
        self.zeros = self.sb("zeros", [P, 512], BF16)
        self.level_f = self.sb("level_f", [P, len(LEVELS), P])
        self.level_u8 = self.sb("level_u8", [P, len(LEVELS), P], U8)
        self.diag_u8 = self.sb("diag_u8", [P, T], U8)
        self.neg_dist = self.sb("neg_dist", [P, P + T])
        self.rows = self.sb("rows", [P, 2, P])
        self.cols = self.sb("cols", [P, 2, P])
        self.row_loads, self.next_row = [], [0, 0]
        self.brow = self.sb("brow", [P, D])
        self.ss = self.sb("ss", [P, TT])
        self.r = self.sb("r", [P, TT])
        self.nr = self.sb("nr", [P, TT])
        self.ss4 = self.sb("ss4", [P, TT, 2])
        self.post_ss = self.sb("post_ss", [P, TT])
        self.post_r = self.sb("post_r", [P, TT])
        self.scratch = self.sb("scratch", [P, D], BF16)
        self.tmp = self.sb("tmp", [P, 2, 512])
        self.A = [self.ps(f"A{i}") for i in range(4)]
        self.G = [self.ps(f"G{i}") for i in range(2)]
        self.M = [self.ps(f"M{i}") for i in range(2)]
        self.raw_full = [self.sem(f"raw_full{i}") for i in range(RING)]
        self.w_hi_ready = self.sem("w_hi_ready")
        self.w_lo_ready = self.sem("w_lo_ready")
        self.unit_used = self.sem("unit_used")
        self.act_chain = self.sem("act_chain")
        self.dve_chain = self.sem("dve_chain")
        self.params = self.sem("params")
        self.rows_clear = self.sem("rows_clear")
        self.rows_turned = self.sem("rows_turned")
        self.cols_ready = self.sem("cols_ready")
        self.consts = self.sem("consts")
        self.x_in = Signal(self.sem("x_in"), 0)
        self.out_done = self.sem("out_done")
        self.booked = {}
        self.sizes = []

    def columns(self, ap, width=P, side=0):
        n, row = ap.shape[0], self.next_row[side]
        for at in range(0, P, width):
            self.row_loads.append((self.rows[row:row + n, side, at:at + width], ap))
        self.next_row[side] += n
        assert self.next_row[side] <= P
        return self.cols[:, side, row:row + n]

    def vectors(self, name, l, width=P):
        if name not in self.booked:
            m = self.dram[name]
            self.booked[name] = self.columns(m.rearrange("l (k p) -> (l k) p", p=width), width)
        n = self.booked[name].shape[1] // self.dram[name].shape[0]
        return self.booked[name][:, l * n:(l + 1) * n]

    def sb(self, name, shape, dt=F32):
        return self.ctx.enter_context(self.nc.sbuf_tensor(self.prefix + name, shape, dt))

    def ps(self, name):
        return self.ctx.enter_context(self.nc.psum_tensor(name, [P, 512], F32))

    def shared_sem(self, name, total=0):
        if name not in self.shared:
            self.shared[name] = [self.sem(name), 0]
        sem, base = self.shared[name]
        self.shared[name][1] += total
        return Signal(sem, base)

    def sem(self, name):
        return self.ctx.enter_context(self.nc.semaphore(name))


class Walk:
    STEP = 2 * RING

    def __init__(self, net, eng, chain_sem=None):
        self.net, self.eng, self.u, self.it = net, eng, 0, None
        self.chain = Chain(eng, chain_sem) if chain_sem is not None else None

    def at(self, n):
        return n if self.it is None else self.it * self.STEP + n

    def enter(self, it, per=0):
        self.it = it
        if self.chain:
            self.chain.enter(it, per)

    def leave(self, trips):
        self.it = None
        self.u += (trips - 1) * self.STEP
        if self.chain:
            self.chain.leave(trips)

    def load(self, dst_dims, src):
        u, net = self.u, self.net
        if u >= RING or self.it is not None:
            self.eng.wait_ge(net.w_lo_ready, self.at(u - RING + 1))
        k, m = dst_dims[0], dst_dims[-1]
        for piece in range(2):
            if len(dst_dims) == 2:
                assert k % 2 == 0
                dst = net.raw[:, u % RING, piece * k * m // 2:(piece + 1) * k * m // 2]
                dst = dst.rearrange("p (k n) -> p k n", k=k // 2)
                part = src[:, piece * k // 2:(piece + 1) * k // 2, :]
            else:
                dst = net.raw[:, u % RING, 0:k * 2 * m].rearrange("p (k g n) -> p k g n", k=k, g=2)[:, :, piece, :]
                part = src[:, :, piece, :]
            self.eng.dma_start(dst, part).then_inc(net.raw_full[u % RING], 16)
        self.u += 1

    def split_hi(self, half=None):
        net, v, act = self.net, self.u, self.eng
        self.u += half != 0
        if v >= len(net.sizes):
            return
        n = net.sizes[v]
        part = slice(n // 2 if half == 1 else 0, n // 2 if half == 0 else n)
        full = 32 * (v // RING + 1)
        act.wait_ge(net.raw_full[v % RING], full if self.it is None else self.it * 64 + full)
        if v >= RING:
            act.wait_ge(net.unit_used, self.at(v - RING + 1))
        ins = act.activation(net.w_hi[:, v % RING, part], net.raw[:, v % RING, part], ACT.Copy)
        if half != 0:
            ins.then_inc(net.w_hi_ready, 1)

    def split_lo(self, half=None):
        net, v, dve = self.net, self.u, self.eng
        self.u += half != 0
        if v >= len(net.sizes):
            return
        n = net.sizes[v]
        part = slice(n // 2 if half == 1 else 0, n // 2 if half == 0 else n)
        dve.wait_ge(net.w_hi_ready, self.at(v + 1))
        if v >= RING:
            dve.wait_ge(net.unit_used, self.at(v - RING + 1))
        ins = dve.tensor_tensor(net.w_lo[:, v % RING, part], net.raw[:, v % RING, part],
                                net.w_hi[:, v % RING, part].bitcast(F32), ALU.subtract)
        if half != 0:
            ins.then_inc(net.w_lo_ready, 1)

    def unit(self, x_hi, x_lo, k0, nk, width, banks, start, stop, pieces=1, quarter=None, ahead=0,
             tile_done=None):
        net, u, pe = self.net, self.u + ahead, self.eng
        n = nk * pieces * width
        assert self.it is not None or net.sizes[u] == n, (u, net.sizes[u], n)
        hi = net.w_hi[:, u % RING, 0:n].rearrange("p (k c n) -> p k c n", k=nk, c=pieces)
        lo = net.w_lo[:, u % RING, 0:n].rearrange("p (k c n) -> p k c n", k=nk, c=pieces)
        if not quarter:
            pe.wait_ge(net.w_lo_ready, self.at(u + 1))
        for tt in range(TT) if quarter is None else [quarter // 2]:
            for k in range(nk) if quarter is None else range(quarter % 2 * nk // 2, (quarter % 2 + 1) * nk // 2):
                first, last = start and k == 0, stop and k == nk - 1
                xh = x_hi[:, k0 + k, tt * P:(tt + 1) * P]
                xl = x_lo[:, k0 + k, tt * P:(tt + 1) * P]
                for c in range(pieces):
                    out = banks[tt][c][:, 0:width]
                    pe.matmul(out, xh, hi[:, k, c, :], start=first, stop=False)
                for c in range(pieces):
                    pe.matmul(banks[tt][c][:, 0:width], xh, lo[:, k, c, :], start=False, stop=False)
                for c in range(pieces):
                    mm = pe.matmul(banks[tt][c][:, 0:width], xl, hi[:, k, c, :], start=False, stop=last)
            if tile_done is not None and tt == 0 and k == nk - 1:
                mm.then_inc(tile_done.sem, 1)
        if quarter in (None, 3):
            mm.then_inc(net.unit_used, 1)
            self.u += 1

    def first_units(self, pre, banks):
        net = self.net
        for tt in range(TT):
            for h in range(2):
                self.eng.wait_ge(*pre.lo(pre.groups.index((tt, h)) + 1))
                for q in range(2):
                    self.unit(net.x_hi, net.x_lo, 4 * h, 4, 512, banks, h == 0, h == 1, quarter=2 * tt + q,
                              ahead=h if tt == 0 else 0)



class Pre:

    def __init__(self, net, name, g, before, x=None, x_hi=None, x_lo=None):
        self.net, self.g = net, g
        self.x_ready, self.x_step, self.x_by = before
        if self.x_by == "tokens":
            self.groups = [(0, 0), (0, 1), (1, 0), (1, 1)]
        else:
            self.groups = [(0, 0), (1, 0), (0, 1), (1, 1)]
        self.turned = net.shared_sem("pre_turned", 4)
        self.gained = net.shared_sem("pre_gained", 4)
        self.hi = net.shared_sem("pre_x_hi", 4)
        self.lo = net.shared_sem("pre_x_lo", 4)
        self.r_ready = net.shared_sem("pre_r", 1)
        self.x = net.x if x is None else x
        self.x_hi = net.x_hi if x_hi is None else x_hi
        self.x_lo = net.x_lo if x_lo is None else x_lo
        self.banks = [net.G[0], net.G[1], net.M[0], net.M[1]]

    def part(self, m, n):
        tt, h = self.groups[n]
        return m[:, 4 * h:4 * h + 4, tt * P:(tt + 1) * P]

    def pe(self, pe):
        for n, (tt, h) in enumerate(self.groups):
            if self.x_step:
                pe.wait_ge(*self.x_ready(self.x_step * (n // 2 + 1)))
            for k in range(4):
                mm = pe.transpose(self.banks[n][:, k * P:(k + 1) * P],
                                  self.x[:, tt, (4 * h + k) * P:(4 * h + k + 1) * P], self.net.ident[:, :])
            mm.then_inc(self.turned.sem, 1)

    def act(self, w):
        for n in range(4):
            w.eng.wait_ge(*self.gained(n + 1))
            w.eng.activation(self.part(self.x_hi, n), self.y(n), ACT.Copy).then_inc(self.hi.sem, 1)

    def y(self, n):
        return self.net.tmp[:, n % 2, :].rearrange("p (k t) -> p k t", k=4)

    def dve(self, w):
        dve = w.eng

        def lo(n):
            dve.wait_ge(*self.hi(n + 1))
            dve.tensor_tensor(self.part(self.x_lo, n), self.y(n), self.part(self.x_hi, n).bitcast(F32),
                              ALU.subtract).then_inc(self.lo.sem, 1)
        for n, (tt, h) in enumerate(self.groups):
            dve.wait_ge(*self.turned(n + 1))
            if n >= 2:
                dve.wait_ge(*self.lo(n - 1))
            dve.tensor_tensor(self.y(n), self.banks[n][:, :].rearrange("p (k t) -> p k t", k=4),
                              self.g[:, 4 * h:4 * h + 4].unsqueeze(2).to_broadcast([P, 4, P]), ALU.mult)\
               .then_inc(self.gained.sem, 1)
            dve.wait_ge(*self.gained(n + 1))
            if n:
                lo(n - 1)
        lo(3)
        dve.wait_ge(*self.lo(4))

    def act_r(self, w, r=None):
        act, net = w.eng, self.net
        for tt in range(TT):
            w.chain(act.activation(net.scratch[:, :], self.x[:, tt, :], ACT.Square,
                                   accum_out=net.ss[:, tt:tt + 1]))
        w.chain(act.activation(net.ss[:, :], net.ss[:, :], ACT.Ln, scale=1.0 / D, bias=EPS))
        if r is not None:
            act.activation(r[:, :], net.ss[:, :], ACT.Exp, scale=-0.5).then_inc(self.r_ready.sem, 1)
            act.wait_ge(*self.r_ready(1))
            return
        w.chain(act.activation(net.r[:, :], net.ss[:, :], ACT.Exp, scale=-0.5))
        act.activation(net.nr[:, :], net.r[:, :], ACT.Copy, scale=-1.0).then_inc(self.r_ready.sem, 1)



class Post:
    def __init__(self, net, name, g_row, scale, brow_free):
        self.net, self.g_row, self.scale, self.brow_free = net, g_row, scale, brow_free
        self.loaded = net.shared_sem("post_brow", 16)
        self.tile_done = net.shared_sem("post_tile", 1)
        self.squared = net.shared_sem("post_squares", 2)
        self.summed = net.shared_sem("post_sums", 2)
        self.r_ready = net.shared_sem("post_r", 2)
        self.x_ready = net.shared_sem("post_x", 2)

    def pool(self, pool):
        if self.brow_free is not None:
            pool.wait_ge(*self.brow_free(2))
        pool.dma_start(self.net.brow[:, :], self.g_row.partition_broadcast(P)).then_inc(self.loaded.sem, 16)

    def act(self, w):
        act, net = w.eng, self.net
        for tt in range(TT):
            if tt == 0:
                act.wait_ge(*self.tile_done(1))
            else:
                act.wait_ge(net.unit_used, w.at(w.u - LEAD))
                w.chain.sync()
            for c in range(2):
                ins = act.activation(net.scratch[:, c * 512:(c + 1) * 512], net.A[2 * tt + c][:, :],
                                     ACT.Square, accum_out=net.ss4[:, tt, c:c + 1])
                if c == 0:
                    w.chain.mark(ins)
            ins.then_inc(self.squared.sem, 1)
            act.wait_ge(*self.summed(tt + 1))
            ss = net.post_ss[:, tt:tt + 1]
            w.chain(act.activation(ss, ss, ACT.Ln, scale=1.0 / D, bias=EPS))
            act.activation(net.post_r[:, tt:tt + 1], ss, ACT.Exp, scale=-0.5).then_inc(self.r_ready.sem, 1)

    def dve(self, w):
        dve, net = w.eng, self.net
        for tt in range(TT):
            dve.wait_ge(*self.squared(tt + 1))
            dve.tensor_tensor(net.post_ss[:, tt:tt + 1], net.ss4[:, tt, 0:1], net.ss4[:, tt, 1:2], ALU.add)\
               .then_inc(self.summed.sem, 1)
            dve.wait_ge(*self.r_ready(tt + 1))
            if tt == 0:
                dve.wait_ge(*self.loaded(16))
            for c in range(2):
                cols = slice(c * 512, (c + 1) * 512)
                w.chain(dve.scalar_tensor_tensor(out=net.tmp[:, c, :], in0=net.A[2 * tt + c][:, :],
                                                 scalar=net.post_r[:, tt:tt + 1], in1=net.brow[:, cols],
                                                 op0=ALU.mult, op1=ALU.mult))
                ins = dve.scalar_tensor_tensor(out=net.x[:, tt, cols], in0=net.tmp[:, c, :],
                                               scalar=self.scale, in1=net.x[:, tt, cols],
                                               op0=ALU.mult, op1=ALU.add)
                if c == 1:
                    ins.then_inc(self.x_ready.sem, 1)
                else:
                    w.chain.mark(ins)
        dve.wait_ge(*self.x_ready(2))



class Ffn:
    def __init__(self, net, name, w_gu, w_dn, pre_g, post_row, before, brow_free, last):
        self.net, self.w_gu, self.w_dn = net, w_gu, w_dn
        self.steps = w_dn.shape[0] // 256
        self.loops = (self.steps - 2) // 2 - last
        self.after = range(2 + 2 * self.loops, self.steps)
        self.pre = Pre(net, name, pre_g, before)
        self.post = Post(net, name, post_row, 0.5, brow_free)
        self.x_ready = self.post.x_ready
        self.clamped = net.shared_sem("ffn_gate", self.steps)
        self.gated = net.shared_sem("ffn_sigmoid", self.steps)
        self.hidden = net.shared_sem("ffn_hidden", self.steps)
        self.h_turned = net.shared_sem("ffn_h_turned", self.steps)
        self.h_hi = net.shared_sem("ffn_h_hi", self.steps)
        self.h_lo = net.shared_sem("ffn_h_lo", self.steps)
        net.sizes += [4 * 512] * (3 * self.steps)

    def tensors(self, net):
        self.z = net.sb("ffn_z", [P, TT, 256])
        self.e = net.sb("ffn_e", [P, TT, 256])
        self.gs = net.sb("ffn_gs", [P, TT, 256])
        self.h = net.sb("ffn_h", [P, TT, 256])
        self.hT_hi = net.sb("ffn_hT_hi", [P, 2, T], F32R)
        self.hT_lo = net.sb("ffn_hT_lo", [P, 2, T], F32R)

    def pool(self, pool):
        self.post.pool(pool)

    def sp(self, w):
        half = self.w_gu.shape[1] // 2

        def gate_up(j):
            for kh in range(2):
                src = self.w_gu[kh * 512:(kh + 1) * 512, :].rearrange("(k p) (g n) -> p k g n", p=P, g=2)
                w.load([4, 2, 256], src[:, :, :, bass.ds(j * 256, 256)])

        def down(j):
            src = self.w_dn[bass.ds(j * 256, 256), :].rearrange("(k p) n -> p k n", p=P)
            w.load([2, D], src)

        gate_up(0)
        gate_up(1)
        down(0)
        with w.eng.Fori(0, self.loops) as it:
            w.enter(it)
            for i in range(2):
                gate_up(it * 2 + (2 + i))
                down(it * 2 + (1 + i))
            w.leave(self.loops)
        for j in self.after:
            gate_up(j)
            down(j - 1)
        down(self.steps - 1)

    def banks(self, j):
        return self.net.A[0:2] if isinstance(j, int) and j == 0 else self.net.G

    def gate_up(self, w, j):
        w.eng.wait_ge(*self.hidden(j))
        for kh in range(2):
            self.gate_up_half(w, kh)

    def gate_up_half(self, w, kh):
        net = self.net
        w.unit(net.x_hi, net.x_lo, 4 * kh, 4, 512, [[net.G[0]], [net.G[1]]], kh == 0, kh == 1)

    def turn(self, w, j):
        net, pe = self.net, w.eng
        pe.wait_ge(*self.hidden(j + 1))
        if not isinstance(j, int) or j:
            pe.wait_ge(*self.h_lo(j))
        for kk in range(2):
            for tt in range(TT):
                mm = pe.transpose(net.M[0][:, kk * T + tt * P:kk * T + (tt + 1) * P],
                                  self.h[:, tt, kk * P:(kk + 1) * P], net.ident[:, :])
        mm.then_inc(self.h_turned.sem, 1)

    def down(self, w, j, last=False):
        net = self.net
        w.eng.wait_ge(*self.h_lo(j + 1))
        w.unit(self.hT_hi, self.hT_lo, 0, 2, 512, [net.A[0:2], net.A[2:4]], False, last, pieces=2,
               tile_done=self.post.tile_done if last else None)

    def pe(self, w):
        net, pe = self.net, w.eng
        self.pre.pe(pe)
        w.first_units(self.pre, [[net.A[0]], [net.A[1]]])
        self.gate_up_half(w, 0)
        self.turn(w, 0)
        self.gate_up_half(w, 1)
        for bank in net.A:
            pe.matmul(bank[:, :], net.zeros[:, 0:P], net.zeros[:, :], start=True, stop=False)
        self.down(w, 0)
        self.turn(w, 1)
        with pe.Fori(0, self.loops) as it:
            w.enter(it)
            for i in range(2):
                j = it * 2 + (2 + i)
                self.gate_up(w, j)
                self.down(w, it * 2 + (1 + i))
                self.turn(w, j)
            w.leave(self.loops)
        for j in self.after:
            self.gate_up(w, j)
            self.down(w, j - 1)
            self.turn(w, j)
        self.down(w, self.steps - 1, True)

    def sigmoid(self, w, j):
        act = w.eng
        act.wait_ge(*self.clamped(j + 1))
        w.chain(act.activation(self.e[:, :, :], self.z[:, :, :], ACT.Exp, scale=-1.0))
        w.chain(act.activation(self.e[:, :, :], self.e[:, :, :], ACT.Ln, bias=1.0))
        act.activation(self.e[:, :, :], self.e[:, :, :], ACT.Exp, scale=-1.0).then_inc(self.gated.sem, 1)

    def hid_hi(self, w, j):
        act = w.eng
        act.wait_ge(*self.h_turned(j + 1))
        act.activation(self.hT_hi[:, :, :], self.net.M[0][:, :], ACT.Copy).then_inc(self.h_hi.sem, 1)

    def act(self, w):
        act = w.eng
        self.pre.act(w)
        w.split_hi()
        self.pre.act_r(w)
        w.split_hi()
        act.wait_ge(*self.pre.r_ready(1))
        self.sigmoid(w, 0)

        def step(j, before):
            w.split_hi()
            self.hid_hi(w, before)
            w.split_hi()
            self.sigmoid(w, j)
            w.split_hi()
        step(1, 0)
        with act.Fori(0, self.loops) as it:
            w.enter(it, per=4)
            for i in range(2):
                step(it * 2 + (2 + i), it * 2 + (1 + i))
            w.leave(self.loops)
        for j in self.after:
            step(j, j - 1)
        self.hid_hi(w, self.steps - 1)
        w.split_hi()
        self.post.act(w)

    def make_hidden(self, w, j):
        net, dve = self.net, w.eng
        dve.wait_ge(net.unit_used, w.at(w.u - LEAD))
        for tt in range(TT):
            ins = dve.tensor_scalar(self.z[:, tt, :], self.banks(j)[tt][:, 0:256], net.r[:, tt:tt + 1], CLAMP,
                                    ALU.mult, ALU.max)
        ins.then_inc(self.clamped.sem, 1)
        dve.wait_ge(*self.gated(j + 1))
        w.chain(dve.tensor_tensor(self.gs[:, :, :], self.z[:, :, :], self.e[:, :, :], ALU.mult))
        for tt in range(TT):
            ins = dve.scalar_tensor_tensor(out=self.h[:, tt, :], in0=self.banks(j)[tt][:, 256:512],
                                           scalar=net.r[:, tt:tt + 1], in1=self.gs[:, tt, :],
                                           op0=ALU.mult, op1=ALU.mult)
        ins.then_inc(self.hidden.sem, 1)

    def hid_lo(self, w, j):
        dve = w.eng
        dve.wait_ge(*self.h_hi(j + 1))
        dve.tensor_tensor(self.hT_lo[:, :, :], self.net.M[0][:, :], self.hT_hi[:, :, :].bitcast(F32),
                          ALU.subtract).then_inc(self.h_lo.sem, 1)

    def dve(self, w):
        dve = w.eng
        self.pre.dve(w)
        w.split_lo()
        w.split_lo()
        dve.wait_ge(*self.pre.r_ready(1))
        self.make_hidden(w, 0)

        def step(j, before):
            w.split_lo()
            self.hid_lo(w, before)
            w.split_lo()
            self.make_hidden(w, j)
            if not isinstance(j, int) or j < self.steps - 1:
                w.split_lo()
        step(1, 0)
        with dve.Fori(0, self.loops) as it:
            w.enter(it, per=2)
            for i in range(2):
                step(it * 2 + (2 + i), it * 2 + (1 + i))
            w.leave(self.loops)
        for j in self.after:
            step(j, j - 1)
        self.hid_lo(w, self.steps - 1)
        w.split_lo()
        w.split_lo()
        self.post.dve(w)



HD = 64
HEADS_A, HEADS_M, HEADS_B = 8, 4, 4
DK_B = 32
RANK = 16
LEVELS = [64, 32, 16, 8, 4, 2, 1]
CLAMP = -43.0

CHUNKS = {"b": (2048, 512), "gb": (2560, 256), "rb": (2816, 16), "m": (2832, 512), "qa": (0, 512), "ka": (512, 512),
          "va": (1024, 512), "ga": (1536, 512)}


class Block:

    def __init__(self, net, name, l, dram, gain, before):
        self.net, self.l, self.x_before, self.name = net, l, (before[0] if l else None), name
        self.w_in, self.w_mem, self.w_out = dram["w_in"][l], dram["w_mem_kv"][l], dram["w_out"][l]
        self.mem_dram = dram["mem"][0].rearrange("(t p) d -> p t d", p=P)
        self.w_gate_up = dram["w_gate_up"][l]
        self.g_gla_row = dram["g_gla_out"][l:l + 1, :]
        self.mem_g = net.vectors("g_mem", l)
        self.x_g = net.vectors("g_pre", l)
        self.before = before
        self.head_g = {y: net.vectors(f"g_{k}", l, HD)
                       for y, k in (("qa", "q_moba"), ("ka", "k_moba"), ("qm", "q_mem"), ("mk", "k_mem"))}
        self.b_gate = net.vectors("b_gate_up", l)
        plan = """
            mempre
            mem 0 [ | xpre | | rms]
            mem 1 [ | | | evac:mem]
            rb 0 [norm1:mk | | | evac:rb]
            b 0 [turn:rb | norm2:mk | z | decay turn:mk]
            b 1 [ | kexp | | evac:b]
            gb 0 [turn:qkb | spread | | evac:gb]
            m 0 [gate1:b | level:0:0 | level:0:1 | level:0:2 gate2:b]
            m 1 [level:1:0 | glav:0 level:1:1 | level:1:2 | evac:m level:2:0]
            qa 0 [glav:1 norm1:qm | level:2:1 | level:2:2 norm2:qm | level:3:0 gate1:m]
            qa 1 [level:3:1 glav:2 | turn:qm level:3:2 | gate2:m glav:3 | evac:qa gcopy]
            ka 0 [norm1:qa score:8 | norm1:gla score:9 | norm2:qa | pturn:8]
            ka 1 [turn:qa0 pv:8 | norm2:gla pturn:9 score:10 | turn:qa1 | evac:ka pv:9]
            va 0 [gfin norm1:ka | pturn:10 score:11 | norm2:ka pv:10 | pturn:11]
            va 1 [turn:ka0 pv:11 | turn:ka1 | join:1 jgate:1 | evac:va score:0]
            ga 0 [score:1 cturn:2 | pturn:0 | cturn:3 score:2 pv:0 | pturn:1]
            ga 1 [score:3 pv:1 | pturn:2 | score:4 pv:2 | evac:ga pturn:3]"""
        steps = []
        for line in plan.split("\n"):
            if "[" not in line:
                steps += line.split()
                continue
            chunk, half = line.split("[")[0].split()
            for q, after in enumerate(line.split("[")[1].rstrip("]").split("|")):
                after = after.split()
                steps.append(f"unit:{chunk}:{half}:{q}")
                if after and after[0].startswith("evac"):
                    steps.append(after.pop(0))
                steps += [("hi:0", "hi:1", "lo:0", "lo:1")[q]] + after
        steps += "out:0:1:0 hi:0 gate1:a pv:3 score:5 out:0:1:1 hi:1 pturn:4 join:2 gate_ln " \
                 "out:0:1:2 lo:0 score:6 pv:4 gate_exp out:0:1:3 lo:1 pturn:5 out:1:1:0 hi:0 gate2:a jgate:2 " \
                 "pv:5 hi:1 cturn:0 out:1:1:1 lo:0 pturn:6 score:7 out:0:0:0 lo:1 pv:6 pturn:7 out:0:0:2 pv:7 " \
                 "join:3 jgate:3 cturn:1 out:1:1:2 out:1:1:3 " \
                 "out:0:0:1 hi:0 hi:1 out:0:0:3 lo:0 lo:1 add:0 " \
                 "out:1:0:0 hi:0 out:1:0:1 hi:1 out:1:0:2 lo:0 out:1:0:3 lo:1 add:1".split()
        self.steps = [tuple(x.split(":")) for x in steps]
        self.norms = [x[1] for x in self.steps if x[0] == "norm1"]
        self.evacs = [x[1] for x in self.steps if x[0] == "evac"]
        self.gates = [x[1] for x in self.steps if x[0] == "gate1"]
        self.items = [int(x[1]) for x in self.steps if x[0] == "score"]
        self.misc = [x for x in self.steps if x[0] in ("turn", "z", "pturn", "cturn")]
        self.cturns = [x for x in self.steps if x[0] == "cturn"]
        self.g_uses = [x for x in self.steps if x[0] in ("level", "score")]
        s = lambda n, total: net.shared_sem(f"block_{n}", total)
        self.mem_loaded, self.small_loaded = s("mem_loaded", 16), s("small_loaded", 32)
        self.evacuated = s("evacuated", 2 * len(self.evacs))
        self.sumsq = s("sumsq", len(self.norms))
        self.rhead = s("rhead", len(self.norms))
        self.normed = s("normed", len(self.norms))
        self.misc_done = s("misc_done", len(self.misc))
        self.misc_free = s("misc_free", len(self.misc))
        self.score_done = s("score_done", len(self.g_uses))
        self.levels_in = s("levels_in", 3 * HEADS_B)
        self.maxed = s("maxed", len(self.items))
        self.probs = s("probs", len(self.items))
        self.soft = s("soft", 1)
        self.b_diff = s("b_diff", 1)
        self.b_exp = s("b_exp", 1)
        self.b_qk = s("b_qk", 1)
        self.pv_done = s("pv_done", 4)
        self.o_free = s("o_free", 4)
        self.clamped = s("clamped", len(self.gates))
        self.sigm = s("sigm", len(self.gates))
        self.cat_part = s("cat_part", 4)
        self.cat_lo = s("cat_lo", 4)
        self.x_ready = s("x", 2)
        self.u0 = len(net.sizes)
        for x in self.steps:
            if x[0] == "unit" and x[3] == "0":
                net.sizes.append(KT * CHUNKS[x[1]][1] if x[1] in ("gb", "rb") else 4 * 512)
            elif x[0] == "out" and x[3] == "0":
                net.sizes.append(4 * 512)
        self.u_out = len(net.sizes) - 4

    def tensors(self, net):
        self.y = {c: net.sb(f"y_{c}", [P, TT, w]) for c, w in
                  (("mem", 512), ("b", 512), ("gb", 256), ("rb", 16), ("m", 512), ("qa", 512),
                   ("ka", 512), ("va", 512))}
        self.y["ga"] = self.y["qa"]
        self.gate = net.sb("gate", [P, TT, D])
        self.cat = net.sb("cat", [P, TT, D])
        self.qaT, self.kaT = net.sb("qaT", [P, 4, T]), net.sb("kaT", [P, 4, T])
        self.qmT, self.kmT = net.sb("qmT", [P, 2, T]), net.sb("kmT", [P, 2, T])
        self.qbT, self.kbT = net.sb("qbT", [P, T]), net.sb("kbT", [P, T])
        self.rbT = net.sb("rbT", [RANK, T])
        self.w_gate = net.sb("w_gate", [RANK, P])
        self.g_gla = net.sb("g_gla", [P, HD])
        self.zb, self.soft_t = net.sb("zb", [P, T]), net.sb("soft_t", [P, T])
        self.decay = net.sb("decay", [P, T])
        self.ones = net.sb("ones_row", [P, T])
        self.att = net.sb("att", [P, 2, 3, P])
        self.Pb = net.sb("Pb", [P, 3, 512])
        self.PT = net.sb("PT", [P, 2, 512])
        self.ssh = net.sb("ssh", [P, 5, TT * 8])
        self.r_mem = net.sb("r_mem", [P, TT])
        self.mx, self.nm = net.sb("mx", [P, 12, 2]), net.sb("nm", [P, 12, 2])
        self.rs, self.rr = net.sb("rs", [P, 2, 12]), net.sb("rr", [P, 2, 12])
        with ExitStack() as alias:
            keep, net.ctx = net.ctx, alias
            self.mem_hi = net.sb("mem_hi", [P, KT, T], F32R)
            self.mem_lo = net.sb("mem_lo", [P, KT, T], F32R)
            net.ctx = keep
        self.QE = net.sb("QE", [P, 8, T])
        self.KE = net.sb("KE", [P, 8, T])
        self.src = {"mk": (self.y["mem"][:, :, 0:256], 4), "qm": (self.y["m"][:, :, 0:256], 4),
                    "qa": (self.y["qa"][:, :, :], 8), "ka": (self.y["ka"][:, :, :], 8),
                    "gla": (self.cat[:, :, 512:768], 4)}
        self.gate_src = {"b": (self.y["gb"][:, :, :], self.gate[:, :, 512:768]),
                         "m": (self.y["m"][:, :, 256:512], self.gate[:, :, 768:1024]),
                         "a": (self.y["ga"][:, :, :], self.gate[:, :, 0:512])}
        n = self.name
        self.mempre = Pre(net, f"{n}_mem", self.mem_g, (self.mem_loaded, 0, "columns"), self.cat, self.mem_hi, self.mem_lo)
        self.xpre = Pre(net, n, self.x_g, self.before)
        self.catT_hi = [net.x_hi, net.x_hi, self.mem_hi, self.mem_hi]
        self.catT_lo = [net.x_lo, net.x_lo, self.mem_lo, self.mem_lo]

    def misc_no(self, step):
        return self.misc.index(step)

    def g_no(self, use):
        return self.g_uses.index(use)

    def item_no(self, n):
        return self.items.index(n)

    def pool(self, pool):
        net = self.net
        if self.x_before is not None:
            pool.wait_ge(*self.prev.misc_done(len(self.misc)))
        pool.dma_start(self.cat[:, :, :], self.mem_dram).then_inc(self.mem_loaded.sem, 16)
        if self.x_before is not None:
            pool.wait_ge(*self.prev.cat_part(4))
        pool.dma_start(self.w_gate[:, :], self.w_gate_up).then_inc(self.small_loaded.sem, 16)
        pool.dma_start(self.g_gla[:, :], self.g_gla_row.partition_broadcast(P)).then_inc(self.small_loaded.sem, 16)

    def sp(self, w):
        def cols(m, rows, at, width):
            return m[rows[0]:rows[1], at:at + width].rearrange("(k p) n -> p k n", p=P)
        for step in self.steps:
            if step[0] not in ("unit", "out") or step[3] != "0":
                continue
            h = int(step[2])
            if step[0] == "out":
                w.load([4, 512], cols(self.w_out, (512 * h, 512 * h + 512), 512 * int(step[1]), 512))
            elif step[1] == "mem":
                w.load([4, 512], cols(self.w_mem, (512 * h, 512 * h + 512), 0, 512))
            elif step[1] in ("gb", "rb"):
                at, width = CHUNKS[step[1]]
                w.load([KT, width], cols(self.w_in, (0, D), at, width))
            else:
                w.load([4, 512], cols(self.w_in, (512 * h, 512 * h + 512), *CHUNKS[step[1]]))

    def pe(self, w):
        net, pe = self.net, w.eng
        ident = net.ident

        def take_misc(step):
            n = self.misc_no(step)
            if n >= 2 and self.misc[n - 2][0] == "cturn":
                pe.wait_ge(*self.cat_lo(self.cturns.index(self.misc[n - 2]) + 1))
            elif n >= 2:
                pe.wait_ge(*self.misc_free(n - 1))
            return net.M[n % 2]

        def take_g(use):
            n = self.g_no(use)
            if n >= 2:
                before = self.g_uses[n - 2]
                if before[0] == "level":
                    pe.wait_ge(*self.levels_in(self.level_no(before)))
                elif int(before[1]) >= HEADS_A:
                    pe.wait_ge(*self.probs(self.item_no(int(before[1])) + 1))
                else:
                    pe.wait_ge(*self.maxed(self.item_no(int(before[1])) + 1))
            return net.G[n % 2]

        for step in self.steps:
            kind = step[0]
            if kind == "mempre":
                if self.x_before is not None:
                    pe.wait_ge(*self.prev.cat_lo(4))
                pe.wait_ge(*self.mem_loaded(16))
                self.mempre.pe(pe)
            elif kind == "xpre":
                pe.wait_ge(*self.mempre.gained(4))
                self.xpre.pe(pe)
            elif kind == "unit":
                c, h, q = step[1], int(step[2]), int(step[3])
                i = 2 * self.evacs.index(c)
                if h == 0 and q % 2 == 0:
                    if i + q // 2 > 2:
                        pe.wait_ge(*self.evacuated(i + q // 2 - 2))
                    elif i + q == 0 and self.x_before is not None:
                        pe.wait_ge(*self.x_before(1))
                banks = [[net.A[i % 3]], [net.A[(i + 1) % 3]]]
                if c == "mem":
                    pe.wait_ge(*self.mempre.lo(self.mempre.groups.index((q // 2, h)) + 1))
                    w.unit(self.mem_hi, self.mem_lo, 4 * h, 4, 512, banks, h == 0, h == 1, quarter=q)
                elif c in ("gb", "rb"):
                    if c == "rb" and q == 0:
                        pe.wait_ge(*self.xpre.lo(4))
                    w.unit(net.x_hi, net.x_lo, 0, KT, CHUNKS[c][1], banks, True, True, quarter=q)
                else:
                    w.unit(net.x_hi, net.x_lo, 4 * h, 4, 512, banks, h == 0, h == 1, quarter=q)
            elif kind == "turn":
                y = step[1]
                bank = take_misc(step)
                if y == "qkb":
                    pe.wait_ge(*self.evacuated(2 * self.evacs.index("b") + 2))
                    parts = [self.y["b"][:, :, 0:P], self.y["b"][:, :, P:2 * P]]
                elif y == "rb":
                    pe.wait_ge(*self.evacuated(2 * self.evacs.index("rb") + 2))
                    parts = [self.y["rb"][:, :, :]]
                else:
                    src = self.src[y[0:2]][0]
                    pe.wait_ge(*self.normed(self.norms.index(y[0:2]) + 1))
                    first = 2 * int(y[2]) if len(y) == 3 else 0
                    parts = [src[:, :, (first + q) * P:(first + q + 1) * P] for q in range(2)]
                for q, part in enumerate(parts):
                    rows = part.shape[2]
                    for tt in range(TT):
                        mm = pe.transpose(bank[0:rows, q * T + tt * P:q * T + (tt + 1) * P],
                                          part[:, tt, :], ident[:, :])
                mm.then_inc(self.misc_done.sem, 1)
            elif kind == "z":
                bank = take_misc(step)
                pe.wait_ge(*self.misc_free(self.misc_no(("turn", "rb")) + 1))
                pe.wait_ge(*self.small_loaded(32))
                pe.matmul(bank[:, 0:T], self.w_gate[:, :], self.rbT[:, :], start=True, stop=True)\
                  .then_inc(self.misc_done.sem, 1)
            elif kind == "level":
                h = int(step[1])
                rows = slice(DK_B * h, DK_B * (h + 1))
                part = int(step[2])
                pe.wait_ge(*self.b_qk(1))
                bank = take_g(step)
                if part < 2:
                    for n, lev in enumerate((range(0, 4), range(4, 7))[part]):
                        s = LEVELS[lev]
                        for t in range(TT):
                            right = self.QE[rows, 1 + lev, t * P:(t + 1) * P]\
                                .rearrange("p (b h r) -> p b h r", h=2, r=s)[:, :, 1, :]
                            mm = pe.matmul(bank[:, n * P + t * 64:n * P + (t + 1) * 64],
                                           self.KE[rows, 1 + lev, t * P:(t + 1) * P], right,
                                           start=True, stop=True, tile_position=(DK_B * h, 0))
                    if part == 1:
                        mm = pe.matmul(bank[:, 3 * P:4 * P], self.KE[rows, 0, 0:P],
                                       self.QE[rows, 0, P:2 * P], start=True, stop=True,
                                       tile_position=(DK_B * h, 0))
                else:
                    for t in range(TT):
                        tok = slice(t * P, (t + 1) * P)
                        mm = pe.matmul(bank[:, tok], self.kbT[rows, tok], self.qbT[rows, tok],
                                       start=True, stop=True, tile_position=(DK_B * h, 0))
                mm.then_inc(self.score_done.sem, 1)
            elif kind == "glav":
                h = int(step[1])
                pe.wait_ge(*self.levels_in(3 * (h + 1)))
                v = self.y["b"]
                cols = slice(256 + HD * h, 256 + HD * (h + 1))
                a = self.att[:, h % 2]
                O = net.A[3]
                pe.matmul(O[:, HD * h:HD * (h + 1)], a[:, 0, :], v[:, 0, cols], start=True, stop=True)
                o1 = O[:, T + HD * h:T + HD * (h + 1)]
                pe.matmul(o1, a[:, 2, :], v[:, 0, cols], start=True, stop=False)
                mm = pe.matmul(o1, a[:, 1, :], v[:, 1, cols], start=False, stop=True)
                if h == 3:
                    mm.then_inc(self.pv_done.sem, 1)
            elif kind == "score":
                n = int(step[1])
                bank = take_g(step)
                if n < HEADS_A:
                    pe.wait_ge(*self.misc_free(self.misc_no(("turn", "qa1")) + 1))
                    pe.wait_ge(*self.misc_free(self.misc_no(("turn", "ka1")) + 1))
                    rows, pair = slice(HD * (n % 2), HD * (n % 2 + 1)), n // 2
                    q, k = self.qaT[rows, pair, :], self.kaT[rows, pair, :]
                    spans = [(0, P), (P, T)]
                else:
                    pe.wait_ge(*self.misc_free(self.misc_no(("turn", "qm")) + 1))
                    h = n - HEADS_A
                    rows, pair = slice(HD * (h % 2), HD * (h % 2 + 1)), h // 2
                    q, k = self.qmT[rows, pair, :], self.kmT[rows, pair, :]
                    spans = [(0, T), (T, T)]
                for tt, (at, keys) in enumerate(spans):
                    mm = pe.matmul(bank[:, at:at + keys], q[:, tt * P:(tt + 1) * P], k[:, 0:keys],
                                   start=True, stop=True, tile_position=(rows.start, 0))
                mm.then_inc(self.score_done.sem, 1)
            elif kind == "pturn":
                n = int(step[1])
                bank = take_misc(step)
                i = self.item_no(n)
                pe.wait_ge(*self.probs(i + 1))
                for b in range(3 if n < HEADS_A else 4):
                    mm = pe.transpose(bank[:, b * P:(b + 1) * P], self.Pb[:, i % 3, b * P:(b + 1) * P],
                                      ident[:, :])
                mm.then_inc(self.misc_done.sem, 1)
            elif kind == "pv":
                n = int(step[1])
                i = self.item_no(n)
                pe.wait_ge(*self.misc_free(self.misc_no(("pturn", step[1])) + 1))
                g = i // 4 + 1
                if i % 4 == 0:
                    pe.wait_ge(*self.o_free(g))
                pt = self.PT[:, i % 2, :]
                O = net.A[3]
                at = HD * (i % 4)
                if n < HEADS_A:
                    pe.wait_ge(*self.evacuated(2 * self.evacs.index("va") + 2))
                    v, cols = self.y["va"], slice(HD * n, HD * (n + 1))
                    blocks = [[0], [1, 2]]
                else:
                    v, cols = self.y["mem"], slice(256 + HD * (n - HEADS_A), 256 + HD * (n - HEADS_A + 1))
                    blocks = [[0, 1], [2, 3]]
                for tt in range(TT):
                    for kt, b in enumerate(blocks[tt]):
                        mm = pe.matmul(O[:, tt * T + at:tt * T + at + HD], pt[:, b * P:(b + 1) * P],
                                       v[:, kt, cols], start=(kt == 0), stop=(b == blocks[tt][-1]))
                if i % 4 == 3:
                    mm.then_inc(self.pv_done.sem, 1)
            elif kind == "cturn":
                grp = int(step[1])
                bank = take_misc(step)
                pe.wait_ge(*self.cat_part(self.cturns.index(step) + 1))
                for kk in range(2):
                    for tt in range(TT):
                        k = 2 * grp + kk
                        mm = pe.transpose(bank[:, kk * T + tt * P:kk * T + (tt + 1) * P],
                                          self.cat[:, tt, k * P:(k + 1) * P], ident[:, :])
                mm.then_inc(self.misc_done.sem, 1)
            elif kind == "out":
                c, h, q = (int(x) for x in step[1:4])
                if h == 1:
                    pe.wait_ge(*self.cat_lo(2))
                    if q == 0:
                        pe.wait_ge(*self.evacuated(2 * len(self.evacs)))
                    if c == 1 and q == 2:
                        pe.wait_ge(*self.o_free(4))
                else:
                    pe.wait_ge(*self.cat_lo(3 if q % 2 == 0 and c == 0 else 4))
                w.unit(self.catT_hi[2 * h], self.catT_lo[2 * h], 4 * h, 4, 512, [[net.A[2 * c]], [net.A[2 * c + 1]]],
                       h == 1, h == 0, quarter=q, ahead=int(step in (("out", "0", "0", "0"), ("out", "0", "0", "2"))))

    def level_no(self, use):
        return [u for u in self.g_uses if u[0] == "level"].index(use) + 1

    def act(self, w):
        net, act = self.net, w.eng
        for step in self.steps:
            kind = step[0]
            if kind == "mempre":
                self.mempre.act(w)
            elif kind == "xpre":
                self.xpre.act(w)
            elif kind == "rms":
                self.mempre.act_r(w, self.r_mem)
                self.xpre.act_r(w)
            elif kind == "hi":
                w.split_hi(int(step[1]))
            elif kind == "evac":
                c = step[1]
                i = 2 * self.evacs.index(c)
                act.wait_ge(net.unit_used, self.unit_end(c))
                if c == "mem":
                    act.wait_ge(*self.xpre.r_ready(1))
                elif c == "rb":
                    act.wait_ge(*self.xpre.r_ready(1))
                width = self.y[c].shape[2]
                r = self.r_mem if c == "mem" else net.r
                for tt in range(TT):
                    act.activation(self.y[c][:, tt, :], net.A[(i + tt) % 3][:, 0:width], ACT.Copy,
                                   scale=r[:, tt:tt + 1]).then_inc(self.evacuated.sem, 1)
            elif kind == "norm1":
                i = self.norms.index(step[1])
                n = TT * self.src[step[1]][1]
                act.wait_ge(*self.sumsq(i + 1))
                w.chain(act.activation(self.ssh[:, i, 0:n], self.ssh[:, i, 0:n], ACT.Ln,
                                       scale=1.0 / HD, bias=EPS))
                act.activation(self.ssh[:, i, 0:n], self.ssh[:, i, 0:n], ACT.Exp, scale=-0.5)\
                   .then_inc(self.rhead.sem, 1)
            elif kind in ("turn", "z", "pturn", "cturn"):
                m = self.misc_no(step)
                bank = net.M[m % 2]
                act.wait_ge(*self.misc_done(m + 1))
                if kind == "cturn":
                    g = int(step[1])
                    act.activation(self.catT_hi[g][:, 2 * g:2 * g + 2, :], bank[:, :], ACT.Copy)\
                       .then_inc(self.misc_free.sem, 1)
                    continue
                if kind == "pturn":
                    n = int(step[1])
                    width = (3 if n < HEADS_A else 4) * P
                    ins = act.activation(self.PT[:, self.item_no(n) % 2, 0:width], bank[:, 0:width], ACT.Copy)
                elif kind == "z":
                    ins = act.activation(self.zb[:, :], bank[:, 0:T], ACT.Identity, bias=self.b_gate)
                elif step[1] == "qkb":
                    w.chain.mark(act.activation(self.qbT[:, :], bank[:, 0:T], ACT.Copy, scale=DK_B ** -0.5))
                    ins = act.activation(self.kbT[:, :], bank[:, T:2 * T], ACT.Copy)
                elif step[1] == "rb":
                    ins = act.activation(self.rbT[:, :], bank[0:RANK, 0:T], ACT.Copy)
                else:
                    y = step[1]
                    dst = {"qa": self.qaT, "ka": self.kaT, "qm": self.qmT, "mk": self.kmT}[y[0:2]]
                    first = 2 * int(y[2]) if len(y) == 3 else 0
                    ins = act.activation(dst[:, first:first + 2, :], bank[:, :], ACT.Copy,
                                         scale=self.head_g[y[0:2]])
                ins.then_inc(self.misc_free.sem, 1)
            elif kind == "decay":
                act.wait_ge(*self.misc_free(self.misc_no(("z",)) + 1))
                w.chain(act.activation(self.soft_t[:, :], self.zb[:, :], ACT.Abs))
                w.chain(act.activation(self.soft_t[:, :], self.soft_t[:, :], ACT.Exp, scale=-1.0))
                act.activation(self.soft_t[:, :], self.soft_t[:, :], ACT.Ln, bias=1.0).then_inc(self.soft.sem, 1)
            elif kind == "kexp":
                act.wait_ge(*self.b_diff(1))
                w.chain(act.activation(self.KE[:, :, :], self.KE[:, :, :], ACT.Abs))
                act.activation(self.KE[:, :, :], self.KE[:, :, :], ACT.Exp, scale=-1.0 / 16.0)\
                   .then_inc(self.b_exp.sem, 1)
            elif kind == "gate1":
                i = self.gates.index(step[1])
                g = self.gate_src[step[1]][1]
                act.wait_ge(*self.clamped(i + 1))
                w.chain.mark(act.activation(g, g, ACT.Exp, scale=-1.0))
                if step[1] != "a":
                    w.chain.sync()
                    w.chain(act.activation(g, g, ACT.Ln, bias=1.0))
                    act.activation(g, g, ACT.Exp, scale=-1.0).then_inc(self.sigm.sem, 1)
            elif kind in ("gate_ln", "gate_exp"):
                g = self.gate_src["a"][1]
                w.chain.sync()
                if kind == "gate_ln":
                    w.chain.mark(act.activation(g, g, ACT.Ln, bias=1.0))
                else:
                    act.activation(g, g, ACT.Exp, scale=-1.0).then_inc(self.sigm.sem, 1)
            elif kind == "score":
                n = int(step[1])
                i = self.item_no(n)
                act.wait_ge(*self.maxed(i + 1))
                for tt in range(TT):
                    if n < HEADS_A:
                        span = slice(0, P) if tt == 0 else slice(P, P + T)
                        src = self.Pb[:, i % 3, span]
                    else:
                        span = slice(tt * T, (tt + 1) * T)
                        src = net.G[self.g_no(step) % 2][:, span]
                    ins = act.activation(self.Pb[:, i % 3, span], src, ACT.Exp, scale=HD ** -0.5,
                                         bias=self.nm[:, i, tt:tt + 1], accum_out=self.rs[:, tt, i:i + 1])
                    if tt == 0:
                        w.chain.mark(ins)
                ins.then_inc(self.probs.sem, 1)

    def unit_end(self, c):
        n = self.u0
        for step in self.steps:
            if step[0] == "unit" and step[3] == "3":
                n += 1
                if step[1] == c and (step[2] == "1" or c in ("gb", "rb")):
                    return n

    def dve(self, w):
        net, dve = self.net, w.eng
        w.chain.mark(dve.memset(self.ones[:, :], 1.0))
        w.chain(dve.memset(self.att[:, :, :, :], 0.0))
        for step in self.steps:
            kind = step[0]
            if kind == "mempre":
                self.mempre.dve(w)
            elif kind == "xpre":
                self.xpre.dve(w)
            elif kind == "lo":
                w.split_lo(int(step[1]))
            elif kind == "norm1":
                y = step[1]
                i = self.norms.index(y)
                src, heads = self.src[y]
                n = TT * heads
                if y != "gla":
                    c = {"mk": "mem", "qm": "m"}.get(y, y)
                    dve.wait_ge(*self.evacuated(2 * self.evacs.index(c) + 2))
                else:
                    w.chain.sync()
                sq = net.tmp[:, :, 0:heads * HD]
                w.chain(dve.tensor_tensor(sq, src, src, ALU.mult))
                dve.tensor_reduce(self.ssh[:, i, 0:n].rearrange("p (t h) -> p t h", t=TT),
                                  sq.rearrange("p t (h d) -> p t h d", d=HD), AX.X, ALU.add)\
                   .then_inc(self.sumsq.sem, 1)
            elif kind == "norm2":
                y = step[1]
                i = self.norms.index(y)
                src, heads = self.src[y]
                dve.wait_ge(*self.rhead(i + 1))
                for tt in range(TT):
                    s = src[:, tt, :].rearrange("p (h d) -> p h d", d=HD)
                    r = self.ssh[:, i, tt * heads:(tt + 1) * heads].unsqueeze(2).to_broadcast([P, heads, HD])
                    ins = dve.tensor_tensor(s, s, r, ALU.mult)
                    if tt == 0:
                        w.chain.mark(ins)
                ins.then_inc(self.normed.sem, 1)
            elif kind == "decay":
                dve.wait_ge(net.consts, net.masks_at)
                dve.wait_ge(*self.soft(1))
                w.chain(dve.scalar_tensor_tensor(out=self.soft_t[:, :], in0=self.zb[:, :], scalar=0.0,
                                                 in1=self.soft_t[:, :], op0=ALU.min, op1=ALU.subtract))
                w.chain(dve.tensor_tensor_scan(self.decay[:, :], self.ones[:, :], self.soft_t[:, :], 0.0,
                                               ALU.mult, ALU.add))
                for lev, s in enumerate([P] + LEVELS):
                    b = self.decay[:, :].rearrange("p (n s) -> p n s", s=2 * s)
                    mid = b[:, :, s - 1:s].to_broadcast([P, T // (2 * s), 2 * s])
                    ins = dve.tensor_tensor(self.KE[:, lev, :].rearrange("p (n s) -> p n s", s=2 * s),
                                            b, mid, ALU.subtract)
                    if lev < len(LEVELS):
                        w.chain.mark(ins)
                ins.then_inc(self.b_diff.sem, 1)
            elif kind == "spread":
                dve.wait_ge(*self.b_exp(1))
                dve.wait_ge(*self.misc_free(self.misc_no(("turn", "qkb")) + 1))
                all_levels = [P, 8, T]
                w.chain(dve.tensor_tensor(self.QE[:, :, :], self.KE[:, :, :],
                                          self.qbT[:, :].unsqueeze(1).to_broadcast(all_levels), ALU.mult))
                dve.tensor_tensor(self.KE[:, :, :], self.KE[:, :, :],
                                  self.kbT[:, :].unsqueeze(1).to_broadcast(all_levels), ALU.mult)\
                   .then_inc(self.b_qk.sem, 1)
            elif kind == "gate1":
                y, g = self.gate_src[step[1]]
                c = {"b": "gb", "m": "m", "a": "ga"}[step[1]]
                dve.wait_ge(*self.evacuated(2 * self.evacs.index(c) + 2))
                dve.tensor_scalar(g, y, CLAMP, None, ALU.max).then_inc(self.clamped.sem, 1)
            elif kind == "gate2":
                y, g = self.gate_src[step[1]]
                dve.wait_ge(*self.sigm(self.gates.index(step[1]) + 1))
                w.chain(dve.tensor_tensor(g, g, y, ALU.mult))
            elif kind == "level":
                a = self.att[:, int(step[1]) % 2, 0:2, :].rearrange("p t i -> p (t i)")
                part = int(step[2])
                n = self.g_no(step)
                bank = net.G[n % 2]
                dve.wait_ge(*self.score_done(n + 1))
                if part < 2:
                    for k, lev in enumerate((range(0, 4), range(4, 7))[part]):
                        s = LEVELS[lev]
                        right = a.rearrange("p (b h r) -> p b h r", h=2, r=s)[:, :, 1, :]
                        ins = dve.copy_predicated(
                            right, net.level_u8[:, lev, :].rearrange("p (b r) -> p b r", r=s),
                            bank[:, k * P:(k + 1) * P].rearrange("p (b r) -> p b r", r=s))
                        if lev < 6 and not (part == 0 and k == 3):
                            w.chain(ins)
                    if part == 1:
                        w.chain(ins)
                        ins = dve.tensor_copy(self.att[:, int(step[1]) % 2, 2, :], bank[:, 3 * P:4 * P])
                else:
                    ins = dve.copy_predicated(a, net.diag_u8[:, :], bank[:, 0:T])
                ins.then_inc(self.levels_in.sem, 1)
                dve.wait_ge(*self.levels_in(self.level_no(step)))
            elif kind == "gcopy":
                dve.wait_ge(*self.pv_done(1))
                dve.tensor_copy(self.cat[:, :, 512:768], net.A[3][:, :].rearrange("p (t n) -> p t n", t=TT))\
                   .then_inc(self.o_free.sem, 1)
                dve.wait_ge(*self.o_free(1))
            elif kind == "gfin":
                dve.wait_ge(*self.normed(self.norms.index("gla") + 1))
                for tt in range(TT):
                    o = self.cat[:, tt, 512:768].rearrange("p (h d) -> p h d", d=HD)
                    w.chain.mark(dve.tensor_tensor(
                        o, o, self.g_gla[:, :].unsqueeze(1).to_broadcast([P, HEADS_B, HD]), ALU.mult))
                w.chain.sync()
                dve.tensor_tensor(self.cat[:, :, 512:768], self.cat[:, :, 512:768],
                                  self.gate[:, :, 512:768], ALU.mult).then_inc(self.cat_part.sem, 1)
            elif kind == "score":
                n = int(step[1])
                i = self.item_no(n)
                g = self.g_no(step)
                bank = net.G[g % 2]
                dve.wait_ge(*self.score_done(g + 1))
                if n < HEADS_A:
                    logits = self.Pb[:, i % 3, 0:P + T]
                    slope = 2.0 ** (-8.0 * (n + 1) / HEADS_A)
                    w.chain(dve.scalar_tensor_tensor(out=logits, in0=net.neg_dist[:, :],
                                                     scalar=slope * HD ** 0.5, in1=bank[:, 0:P + T],
                                                     op0=ALU.mult, op1=ALU.add))
                    for tt, span in enumerate((slice(0, P), slice(P, P + T))):
                        w.chain.mark(dve.tensor_reduce(self.mx[:, i, tt:tt + 1], logits[:, span], AX.X, ALU.max))
                else:
                    w.chain.mark(dve.tensor_reduce(self.mx[:, i, :],
                                                   bank[:, :].rearrange("p (t n) -> p t n", t=TT), AX.X, ALU.max))
                w.chain.sync()
                dve.tensor_scalar(self.nm[:, i, :], self.mx[:, i, :], -(HD ** -0.5), None, ALU.mult)\
                   .then_inc(self.maxed.sem, 1)
            elif kind == "join":
                g = int(step[1])
                i0 = 4 * (g - 1)
                n0 = self.items[i0]
                at = HD * n0 if n0 < HEADS_A else 768
                dve.wait_ge(*self.pv_done(g + 1))
                dve.wait_ge(*self.probs(i0 + 4))
                w.chain(dve.reciprocal(self.rr[:, :, i0:i0 + 4], self.rs[:, :, i0:i0 + 4]))
                for tt in range(TT):
                    ins = dve.tensor_tensor(
                        self.cat[:, tt, at:at + 4 * HD].rearrange("p (h d) -> p h d", d=HD),
                        net.A[3][:, tt * T:(tt + 1) * T].rearrange("p (h d) -> p h d", d=HD),
                        self.rr[:, tt, i0:i0 + 4].unsqueeze(2).to_broadcast([P, 4, HD]), ALU.mult)
                    if tt == 0:
                        w.chain.mark(ins)
                ins.then_inc(self.o_free.sem, 1)
                dve.wait_ge(*self.o_free(g + 1))
            elif kind == "jgate":
                g = int(step[1])
                n0 = self.items[4 * (g - 1)]
                at = HD * n0 if n0 < HEADS_A else 768
                w.chain.sync()
                dve.tensor_tensor(self.cat[:, :, at:at + 4 * HD], self.cat[:, :, at:at + 4 * HD],
                                  self.gate[:, :, at:at + 4 * HD], ALU.mult).then_inc(self.cat_part.sem, 1)
            elif kind == "cturn":
                g = int(step[1])
                m = self.misc_no(step)
                dve.wait_ge(*self.misc_free(m + 1))
                dve.tensor_tensor(self.catT_lo[g][:, 2 * g:2 * g + 2, :], net.M[m % 2][:, :],
                                  self.catT_hi[g][:, 2 * g:2 * g + 2, :].bitcast(F32), ALU.subtract)\
                   .then_inc(self.cat_lo.sem, 1)
            elif kind == "add":
                c = int(step[1])
                dve.wait_ge(net.unit_used, self.u_out + 3 + c)
                for tt in range(TT):
                    cols = net.x[:, tt, c * 512:(c + 1) * 512]
                    ins = dve.tensor_tensor(cols, net.A[2 * c + tt][:, :], cols, ALU.add)
                    if tt == 0:
                        w.chain.mark(ins)
                ins.then_inc(self.x_ready.sem, 1)



class Conv:
    def __init__(self, net, name, dram, gain, before, brow_free):
        self.net = net
        s = lambda n: net.shared_sem(f"{name}_{n}")
        self.w_in, self.w_out = dram["sc_w_in_2"][0], dram["sc_w_out_2"][0]
        g = dram["norm_g_2"][0]
        self.pre = Pre(net, name, gain(g[2]), before)
        self.post = Post(net, name, g[3], 1.0, brow_free)
        self.x_ready = self.post.x_ready
        taps = dram["sc_conv_w_2"][0]
        self.width = taps.shape[0]
        self.taps = net.columns(taps.rearrange("j (k p) -> (j k) p", p=P))
        self.c_out, self.cv, self.b_out = s("c_out"), s("cv"), s("b_out")
        self.cv_turned, self.b_turned = s("cv_turned"), s("b_turned")
        self.tapped = s("tapped")
        self.y, self.y_hi_ready, self.y_lo_ready = s("y"), s("y_hi"), s("y_lo")
        self.u0 = len(net.sizes)
        net.sizes += [4 * 512] * 16
        steps = "unit:c:0:0 unit:c:0:1 c:0 unit:v:0:0 unit:v:0:1 cv:0 unit:b:0:0 turncv:0 unit:b:0:1 b:0 " \
                "unit:c:1:0 turnb:0 mul:0 unit:c:1:1 c:1 unit:v:1:0 unit:v:1:1 cv:1 unit:b:1:0 turncv:1 " \
                "unit:b:1:1 b:1 turnb:1 mul:1 out"
        self.steps = [tuple(x.split(":")) for x in steps.split()]
        self.chunks = [("c", 0), ("v", 0), ("b", 0), ("c", 1), ("v", 1), ("b", 1)]

    def tensors(self, net):
        self.c = net.sb("sc_c", [P, TT, 512])
        self.b = net.sb("sc_b", [P, TT, 512])
        self.cvs = net.sb("sc_cv", [P, TT, 512])
        self.t = net.sb("sc_t", [P, 4, T])
        self.y_hi = net.sb("sc_y_hi", [P, KT, T], F32R)
        self.y_lo = net.sb("sc_y_lo", [P, KT, T], F32R)

    def pool(self, pool):
        self.post.pool(pool)

    def sp(self, w):
        for what, half in self.chunks:
            at = {"b": 0, "c": D, "v": 2 * D}[what] + 512 * half
            for h in range(2):
                w.load([4, 512], self.w_in[512 * h:512 * h + 512, at:at + 512].rearrange("(k p) n -> p k n", p=P))
        for h in range(4):
            w.load([2, D], self.w_out[256 * h:256 * h + 256, :].rearrange("(k p) n -> p k n", p=P))

    def banks(self, n):
        A = self.net.A
        return (A[0], A[1]) if n % 2 == 0 else (A[2], A[3])

    def pe(self, w):
        net, pe = self.net, w.eng
        self.pre.pe(pe)
        for step in self.steps:
            kind = step[0]
            if kind == "unit":
                n = self.chunks.index((step[1], int(step[2])))
                h = int(step[3])
                if n == 0:
                    if h == 0:
                        w.first_units(self.pre, [[bank] for bank in self.banks(0)])
                    continue
                if n >= 2 and h == 0:
                    what, half = self.chunks[n - 2]
                    sem, per = {"c": (self.c_out, 1), "v": (self.cv, 1), "b": (self.b_out, 1)}[what]
                    pe.wait_ge(*sem(half + 1))
                b0, b1 = self.banks(n)
                w.unit(net.x_hi, net.x_lo, 4 * h, 4, 512, [[b0], [b1]], h == 0, h == 1)
            elif kind in ("turncv", "turnb"):
                half = int(step[1])
                src, banks, sem, ready = (self.cvs, net.G, self.cv_turned, self.cv) if kind == "turncv" \
                    else (self.b, net.M, self.b_turned, self.b_out)
                pe.wait_ge(*ready(half + 1))
                if half:
                    pe.wait_ge(*self.y(2))
                else:
                    pe.wait_ge(*self.pre.lo(4))
                for pair in range(2):
                    for kk in range(2):
                        for tt in range(TT):
                            k = 2 * pair + kk
                            mm = pe.transpose(banks[pair][:, kk * T + tt * P:kk * T + (tt + 1) * P],
                                              src[:, tt, k * P:(k + 1) * P], net.ident[:, :])
                    mm.then_inc(sem.sem, 1)
            elif kind == "out":
                pe.wait_ge(*self.cv(2))
                pe.wait_ge(*self.b_out(2))
                for h in range(4):
                    pe.wait_ge(*self.y_lo_ready(h + 1))
                    w.unit(self.y_hi, self.y_lo, 2 * h, 2, 512, [net.A[0:2], net.A[2:4]], h == 0, h == 3,
                           pieces=2, tile_done=self.post.tile_done if h == 3 else None)

    def act(self, w):
        net, act = self.net, w.eng
        self.pre.act(w)
        self.pre.act_r(w)
        act.wait_ge(*self.pre.r_ready(1))
        for step in self.steps:
            kind = step[0]
            if kind == "unit":
                w.split_hi()
            elif kind in ("c", "b"):
                half = int(step[1])
                n = self.chunks.index((kind, half))
                act.wait_ge(net.unit_used, self.u0 + 2 * (n + 1))
                if kind == "c" and half:
                    act.wait_ge(*self.cv(1))
                if kind == "b" and half:
                    act.wait_ge(*self.b_turned(2))
                for tt in range(TT):
                    ins = act.activation((self.c if kind == "c" else self.b)[:, tt, :],
                                         self.banks(n)[tt][:, :], ACT.Copy, scale=net.r[:, tt:tt + 1])
                ins.then_inc((self.c_out if kind == "c" else self.b_out).sem, 1)
            elif kind == "turncv":
                half = int(step[1])
                for pair in range(2):
                    act.wait_ge(*self.cv_turned(2 * half + pair + 1))
                    if half:
                        act.wait_ge(*self.y_lo_ready(pair + 1))
                    for kk in range(2):
                        k = 4 * half + 2 * pair + kk
                        at = (self.width - 1) * KT + k
                        ins = act.activation(self.t[:, 2 * pair + kk, :],
                                             net.G[pair][:, kk * T:(kk + 1) * T], ACT.Copy,
                                             scale=self.taps[:, at:at + 1])
                    ins.then_inc(self.tapped.sem, 1)
            elif kind == "mul":
                half = int(step[1])
                for pair in range(2):
                    n = 2 * half + pair
                    act.wait_ge(*self.y(n + 1))
                    act.activation(self.y_hi[:, 2 * n:2 * n + 2, :], self.t[:, 2 * pair:2 * pair + 2, :],
                                   ACT.Copy).then_inc(self.y_hi_ready.sem, 1)
            elif kind == "out":
                for _ in range(4):
                    w.split_hi()
        self.post.act(w)

    def dve(self, w):
        net, dve = self.net, w.eng
        self.pre.dve(w)
        for step in self.steps:
            kind = step[0]
            if kind == "unit":
                w.split_lo()
            elif kind == "cv":
                half = int(step[1])
                n = self.chunks.index(("v", half))
                dve.wait_ge(net.unit_used, self.u0 + 2 * (n + 1))
                dve.wait_ge(*self.c_out(half + 1))
                if half:
                    dve.wait_ge(*self.cv_turned(2))
                for tt in range(TT):
                    ins = dve.scalar_tensor_tensor(out=self.cvs[:, tt, :], in0=self.banks(n)[tt][:, :],
                                                   scalar=net.r[:, tt:tt + 1], in1=self.c[:, tt, :],
                                                   op0=ALU.mult, op1=ALU.mult)
                    if tt == 0:
                        w.chain.mark(ins)
                ins.then_inc(self.cv.sem, 1)
            elif kind == "turncv":
                half = int(step[1])
                for pair in range(2):
                    dve.wait_ge(*self.tapped(2 * half + pair + 1))
                    for back in range(1, self.width):
                        for kk in range(2):
                            k = 4 * half + 2 * pair + kk
                            at = (self.width - 1 - back) * KT + k
                            row = self.t[:, 2 * pair + kk, back:T]
                            w.chain.mark(dve.scalar_tensor_tensor(
                                out=row, in0=net.G[pair][:, kk * T:(kk + 1) * T - back],
                                scalar=self.taps[:, at:at + 1], in1=row, op0=ALU.mult, op1=ALU.add))
                        w.chain.sync()
            elif kind == "mul":
                half = int(step[1])
                for pair in range(2):
                    n = 2 * half + pair
                    t = self.t[:, 2 * pair:2 * pair + 2, :].rearrange("p k t -> p (k t)")
                    dve.wait_ge(*self.b_turned(n + 1))
                    dve.tensor_tensor(t, t, net.M[pair][:, :], ALU.mult).then_inc(self.y.sem, 1)
                for pair in range(2):
                    n = 2 * half + pair
                    dve.wait_ge(*self.y_hi_ready(n + 1))
                    dve.tensor_tensor(self.y_lo[:, 2 * n:2 * n + 2, :], self.t[:, 2 * pair:2 * pair + 2, :],
                                      self.y_hi[:, 2 * n:2 * n + 2, :].bitcast(F32), ALU.subtract)\
                       .then_inc(self.y_lo_ready.sem, 1)
            elif kind == "out":
                for _ in range(4):
                    w.split_lo()
        self.post.dve(w)



GH, GV = 8, 16
NQ = 4


class Gdn:

    def __init__(self, net, name, dram, gain, before, brow_free):
        self.net, self.name = net, name
        s = lambda n: net.shared_sem(f"{name}_{n}")
        self.w_in, self.w_out = dram["gdn_w_in_2"][0], dram["gdn_w_out_2"][0]
        g = dram["norm_g_2"][1]
        self.pre = Pre(net, name, gain(g[2]), before)
        self.post = Post(net, name, g[3], 1.0, brow_free)
        self.x_ready = self.post.x_ready
        taps = dram["gdn_conv_w_2"][0]
        self.width, self.ctiles = taps.shape[0], taps.shape[1] // P
        self.taps = net.columns(taps.rearrange("j (k p) -> (j k) p", p=P), side=1)
        self.rows_dram = (dram["gdn_a_log_2"], dram["gdn_dt_bias_2"], dram["gdn_norm_w_2"])
        self.small_loaded = s("small_loaded")
        self.evacuated = s("evacuated")
        self.ba = {x: s(f"ba_{x}") for x in ("act", "dve", "pe")}
        self.ones_set = s("ones_set")
        self.a3_pe = s("a3_written")
        self.a3_act = s("a3_read_act")
        self.a3_dve = s("a3_read_dve")
        self.tapped = s("tapped")
        self.clamped, self.sigm = s("clamped"), s("sigm")
        self.silued = s("silued")
        self.squared = s("squared")
        self.rsq = s("rsq")
        self.l2 = s("l2")
        self.c_pe = [s(f"core_pe{i}") for i in range(2)]
        self.c_act = [s(f"core_act{i}") for i in range(2)]
        self.c_dve = [s(f"core_dve{i}") for i in range(2)]
        self.c_pool = [s(f"core_pool{i}") for i in range(2)]
        self.o_sq, self.o_r, self.o_ready = s("o_sq"), s("o_r"), s("o_ready")
        self.z_clamped, self.z_sigm = s("z_clamped"), s("z_sigm")
        self.o_turned, self.o_hi_ready, self.o_lo_ready = s("o_turned"), s("o_hi"), s("o_lo")
        self.u0 = len(net.sizes)
        self.chunks = ["ba", "q0", "k0", "v0", "v1", "q1", "k1", "v2", "v3", "z0", "z1", "z2", "z3"]
        for c in self.chunks:
            net.sizes += [KT * 32] if c == "ba" else [4 * 512] * 2
        net.sizes += [4 * 512] * 8
        self.steps = [tuple(x.split(":")) for x in self.schedule()]
        self.evacs = [x[1] for x in self.steps if x[0] == "evac"]
        self.silus = [x[1] for x in self.steps if x[0] == "silu" and x[2] == "0"]
        self.norms = [x for x in self.steps if x[0] == "norm"]
        self.l2s = [x[1] for x in self.steps if x[0] == "l2"]
        self.a3 = [x for x in self.steps if x[0] in ("conv", "norm", "kn", "vt", "ba")]
        self.a3 = [x for x in self.a3 if x[0] != "ba" or x[1] in "12"]

    def schedule(self):
        steps, cores = [], [[], [[]] * 3]
        conv = [c for c in self.chunks if c[0] in "qkv"]
        z = [c for c in self.chunks if c[0] == "z"]

        def add_core(i):
            pieces = ["k0", "", "k1"] + [f"{ab}{lev}" for lev in range(5, -1, -1) for ab in "xt"] + \
                     [f"p{n}" for n in range(5)]
            for one in range(2):
                cores[one] += [[f"core:{2 * i + one}:{piece}"] if piece else [] for piece in pieces]

        def core():
            for one in range(2):
                if cores[one]:
                    steps.extend(cores[one].pop(0))

        def quarter(unit, extras):
            steps.append(unit)
            if extras and extras[0].startswith("evac"):
                steps.append(extras.pop(0))
            if any(cores[0] + cores[1]):
                core()
            steps.extend(extras)

        for q in range(NQ):
            quarter(f"unit:ba:0:{q}", ["evac:ba"] if q == 3 else [])
        started_by = ["k0", "v1", "v2", "v3"]
        for n, c in enumerate(self.chunks[1:]):
            slots = [[] for _ in range(2 * NQ)]
            one = conv[n - 1] if 1 <= n <= len(conv) else None
            two = conv[n - 2] if 2 <= n <= len(conv) + 1 else None
            if n == 0:
                slots[3], slots[7] = ["ba:0", "ba:1"], ["ba:2", "ba:3"]
            if two:
                slots[0] = [f"silu:{two}:2"]
                if two[0] == "v":
                    slots[1], slots[2] = [f"vt:{two}:0"], [f"vt:{two}:1"]
                else:
                    slots[1:4] = [f"l2:{two}"], [f"norm:{two}:0"], [f"norm:{two}:1"]
                    slots[4] += [f"kn:{two}"] if two[0] == "k" else []
            if one:
                slots[4] += [f"conv:{one}:0"]
                slots[5] += [f"conv:{one}:1"]
                slots[6] += [f"silu:{one}:0"]
                slots[7] += [f"silu:{one}:1"]
            if c in z[2:]:
                slots[0] += [f"z2:{z[z.index(c) - 2]}:2"]
            if c in z[1:]:
                i = z.index(c) - 1
                slots[3:6] = [f"z1:z{i}:0"], [f"z1:z{i}:1"], [f"z1:z{i}:2"]
                if i < 2:
                    slots[6:8] = [f"z2:z{i}:0"], [f"z2:z{i}:1"]
            slots[7].insert(0, f"evac:{c}")
            for slot, extras in enumerate(slots):
                quarter(f"unit:{c}:{slot // NQ}:{slot % NQ}", extras)
                if two in started_by and slot == 6:
                    add_core(started_by.index(two))
        for n in range(4):
            steps.append(f"ot:{n}")
            if n > 0:
                core()
        last_z = ["z2:z2:0", "z2:z2:1", "z2:z2:2", "z1:z3:0", "z1:z3:1", "z1:z3:2"]
        last_o = [("core:7:p1", "z2:z3:0"), ("core:7:p4", "z2:z3:1"), ("core:7:p4", "z2:z3:2")]
        third = ["ot:4", "ot:5"]
        for slot in range(6 * NQ):
            if slot == 4 * NQ:
                while third:
                    while any(cores[0]):
                        core()
                    steps.append(third.pop(0))
            quarter(f"out:{slot // NQ}:{slot % NQ}", [last_z.pop(0)] if last_z else [])
            if not last_z and last_o and last_o[0][0] in steps:
                steps.append(last_o.pop(0)[1])
            if third and "core:6:p4" in steps:
                steps.append(third.pop(0))
        while any(cores[0] + cores[1]):
            core()
        steps += [x for _, x in last_o] + ["ot:6", "ot:7"]
        for slot in range(2 * NQ):
            quarter(f"out:{6 + slot // NQ}:{slot % NQ}", [])
        return steps

    def tensors(self, net):
        self.v = net.sb("gd_v", [P, TT, GV * P])
        self.u = net.sb("gd_u", [P, 2, TT, 512])
        self.t = net.sb("gd_t", [P, 4, T])
        self.sg = net.sb("gd_sg", [P, 4, T])
        self.yba = net.sb("gd_ba", [P, TT, 32])
        self.a_row, self.dt_row = net.sb("gd_a", [P, GV]), net.sb("gd_dt", [P, GV])
        self.n_row = net.sb("gd_n", [P, P])
        self.beta, self.g = net.sb("gd_beta", [P, TT, GV]), net.sb("gd_g", [P, TT, GV])
        self.tb = net.sb("gd_tb", [P, TT, GV])
        self.G, self.eG, self.neG = (net.sb(f"gd_{n}", [P, TT, GV]) for n in ("G", "eG", "neG"))
        self.tail = net.sb("gd_tail", [P, GV])
        self.GT = net.sb("gd_GT", [GV, T])
        self.ones = net.sb("gd_ones", [P, P])
        self.tri = net.sb("gd_tri", [P, P])
        self.strict = net.sb("gd_strict", [P, P])
        self.before = net.sb("gd_before", [P, P])
        self.ss16 = net.sb("gd_ss", [P, TT * 4])
        with ExitStack() as alias:
            keep, net.ctx = net.ctx, alias
            o_hi, o_lo = (net.sb(f"gd_o_{n}", [P, GV // 2, T], F32R) for n in ("hi", "lo"))
            net.ctx = keep
        self.qT, self.kT = net.sb("gd_qT", [P, GH, T]), net.sb("gd_kT", [P, GH, T])
        self.kn = net.sb("gd_kn", [P, GH, P])
        self.E, self.MT, self.Tm, self.U, self.X, self.QK = (
            [net.sb(f"gd_{n}{i}", [P, 4, P]) for i in range(2)] for n in ("E", "MT", "T", "U", "X", "QK"))
        self.o_hi, self.o_lo = [net.x_hi, o_hi], [net.x_lo, o_lo]
        self.ot_banks = [net.A[(2 * len(self.evacs)) % 3], net.A[3], net.G[0], net.M[0]]
        self.ML = self.E
        self.vn = self.X
        self.S = self.MT
        self.qs = self.Tm

    def pool(self, pool):
        net = self.net
        self.post.pool(pool)
        for dst, src in zip((self.a_row, self.dt_row, self.n_row), self.rows_dram):
            pool.dma_start(dst[:, :], src.partition_broadcast(P) if len(src.shape) == 1
                           else src[0].partition_broadcast(P)).then_inc(self.small_loaded.sem, 16)
        for step in self.steps:
            if step[0] != "core" or step[2] not in ("k1", "x5", "x4", "x3", "x2", "x1"):
                continue
            g, x = int(step[1]), step[2]
            i = g % 2
            if x == "k1":
                lev = 5
                pool.wait_ge(*self.C("dve", g)(3))
            else:
                lev = int(x[1]) - 1
                pool.wait_ge(*self.C("pe", g)(3 + 2 * (4 - lev)))
            pool.tensor_tensor(self.ML[i][:, :, :], self.MT[i][:, :, :],
                               net.level_f[:, lev, :].unsqueeze(1).to_broadcast([P, 4, P]), ALU.mult)\
                .then_inc(self.c_pool[i].sem, 1)

    def C(self, engine, g):
        sem, per = {"pe": (self.c_pe, 19), "act": (self.c_act, 12), "dve": (self.c_dve, 13),
                    "pool": (self.c_pool, 6)}[engine]
        return lambda n: sem[g % 2](per * (g // 2) + n)

    def sp(self, w):
        starts = {"q": 0, "k": D, "v": 2 * D, "z": 4 * D}
        for c in self.chunks:
            if c == "ba":
                w.load([KT, 32], self.w_in[:, 6 * D:6 * D + 32].rearrange("(k p) n -> p k n", p=P))
                continue
            at = starts[c[0]] + 512 * int(c[1])
            for h in range(2):
                w.load([4, 512], self.w_in[512 * h:512 * h + 512, at:at + 512].rearrange("(k p) n -> p k n", p=P))
        for h in range(8):
            w.load([2, D], self.w_out[256 * h:256 * h + 256, :].rearrange("(k p) n -> p k n", p=P))

    def a3_take(self, eng, step):
        n = self.a3.index(step)
        if n:
            kinds = ["dve" if x[0] == "conv" else "act" for x in self.a3[:n]]
            sem = self.a3_dve if kinds[-1] == "dve" else self.a3_act
            eng.wait_ge(*sem(kinds.count(kinds[-1])))
        return self.net.A[3]

    def a3_ready(self, eng, step):
        eng.wait_ge(*self.a3_pe(self.a3.index(step) + 1))

    def pe(self, w):
        net, pe = self.net, w.eng
        ident = net.ident
        self.pre.pe(pe)
        for step in self.steps:
            kind = step[0]
            if kind == "unit":
                c, h, q = step[1], int(step[2]), int(step[3])
                n = self.evacs.index(c)
                i = 2 * n
                if q % 2 == 0 and h == 0 and i + q // 2 > 2:
                    pe.wait_ge(*self.evacuated(i + q // 2 - 2))
                if n == 0:
                    pe.wait_ge(*self.pre.lo(self.pre.groups.index((q // 2, q % 2)) + 1))
                banks = [[net.A[i % 3]], [net.A[(i + 1) % 3]]]
                if c == "ba":
                    w.unit(net.x_hi, net.x_lo, 0, KT, 32, banks, True, True, quarter=q)
                else:
                    w.unit(net.x_hi, net.x_lo, 4 * h, 4, 512, banks, h == 0, h == 1, quarter=q)
            elif kind == "ba":
                if step[1] == "1":
                    bank = self.a3_take(pe, step)
                    pe.wait_ge(*self.ba["dve"](2))
                    pe.wait_ge(*self.ones_set(2))
                    for t in range(TT):
                        mm = pe.matmul(bank[:, t * GV:(t + 1) * GV], self.tri[:, :], self.g[:, t, :],
                                       start=True, stop=True)
                    mm.then_inc(self.a3_pe.sem, 1)
                elif step[1] == "2":
                    bank = self.a3_take(pe, step)
                    for t in range(TT):
                        pe.transpose(bank[0:GV, t * P:(t + 1) * P], self.G[:, t, :], ident[:, :])
                    pe.matmul(bank[:, T:T + GV], ident[:, P - 1:P].to_broadcast([P, P]), self.G[:, 0, :],
                              start=True, stop=True).then_inc(self.a3_pe.sem, 1)
            elif kind == "conv":
                c, part = step[1], int(step[2])
                bank = self.a3_take(pe, step)
                pe.wait_ge(*self.evacuated(2 * self.evacs.index(c) + 2))
                u = self.u[:, self.evacs.index(c) % 2]
                for kk in range(2):
                    for tt in range(TT):
                        k = 2 * part + kk
                        mm = pe.transpose(bank[:, kk * T + tt * P:kk * T + (tt + 1) * P],
                                          u[:, tt, k * P:(k + 1) * P], ident[:, :])
                mm.then_inc(self.a3_pe.sem, 1)
            elif kind == "norm":
                c, part = step[1], int(step[2])
                bank = self.a3_take(pe, step)
                pe.wait_ge(*self.squared(self.l2s.index(c) + 1))
                pe.matmul(bank[:, :], self.ones[:, :],
                          self.sg[:, 2 * part:2 * part + 2, :].rearrange("p k t -> p (k t)"),
                          start=True, stop=True).then_inc(self.a3_pe.sem, 1)
            elif kind == "kn":
                c = step[1]
                bank = self.a3_take(pe, step)
                pe.wait_ge(*self.l2(self.norms.index(("norm", c, "1")) + 1))
                for k in range(4):
                    mm = pe.transpose(bank[:, k * P:(k + 1) * P], self.kT[:, 4 * int(c[1]) + k, 0:P],
                                      ident[:, :])
                mm.then_inc(self.a3_pe.sem, 1)
            elif kind == "vt":
                c, t = step[1], int(step[2])
                bank = self.a3_take(pe, step)
                pe.wait_ge(*self.silued(self.silus.index(c) + 1))
                for k in range(4):
                    mm = pe.transpose(bank[:, k * P:(k + 1) * P], self.t[:, k, t * P:(t + 1) * P], ident[:, :])
                mm.then_inc(self.a3_pe.sem, 1)
            elif kind == "core":
                self.core_pe(pe, int(step[1]), step[2])
            elif kind == "ot":
                n = int(step[1])
                bank = self.ot_banks[n % 2 + 2 * (n >= 4)]
                pe.wait_ge(*self.o_ready(n // 2 + 1))
                if n == 0:
                    pe.wait_ge(*self.evacuated(2 * len(self.evacs) - 2))
                    pe.wait_ge(*self.a3_act(self.act_reads(self.a3[-1])))
                if n == 4:
                    pe.wait_ge(*self.C("act", 6)(12))
                    pe.wait_ge(*self.C("dve", 6)(13))
                if n >= 2:
                    pe.wait_ge(*self.o_lo_ready(n - 1))
                for kk in range(2):
                    for tt in range(TT):
                        k = 2 * n + kk
                        mm = pe.transpose(bank[:, kk * T + tt * P:kk * T + (tt + 1) * P],
                                          self.v[:, tt, k * P:(k + 1) * P], ident[:, :])
                mm.then_inc(self.o_turned.sem, 1)
            elif kind == "out":
                h, q = int(step[1]), int(step[2])
                if q == 0:
                    pe.wait_ge(*self.o_lo_ready(h + 1 if h else 4))
                    if h == 0:
                        pe.wait_ge(*self.evacuated(2 * len(self.evacs)))
                w.unit(self.o_hi[h // 4], self.o_lo[h // 4], 2 * (h % 4), 2, 512, [net.A[0:2], net.A[2:4]],
                       h == 0, h == 7, pieces=2, quarter=q,
                       tile_done=self.post.tile_done if (h, q) == (7, 1) else None)

    def core_pe(self, pe, g, x):
        net = self.net
        i = g % 2
        bg, bm = net.G[i], net.M[i]
        act, dve, pool = (self.C(n, g) for n in ("act", "dve", "pool"))
        tile = lambda t: slice(t * P, (t + 1) * P)
        four = [(j, t, 2 * j + t) for j in range(2) for t in range(TT)]
        kT, qT = self.kT[:, g, :], self.qT[:, g, :]
        if x == "k0":
            pe.wait_ge(*self.l2(self.norms.index(("norm", f"k{g // 4}", "1")) + 1))
            if g == 0 or g == 1:
                pe.wait_ge(*self.ba["act"](3))
            if g >= 2:
                prev_act, prev_dve = self.C("act", g - 2), self.C("dve", g - 2)
                pe.wait_ge(*prev_act(12))
                pe.wait_ge(*prev_dve(13))
            for t in range(TT):
                pe.matmul(bg[:, tile(t)], kT[:, tile(t)], kT[:, tile(t)], start=True, stop=True)
                pe.matmul(bg[:, tile(2 + t)], kT[:, tile(t)], qT[:, tile(t)], start=True, stop=True)
            for j, t, n in four:
                h = 2 * g + j
                mm = pe.matmul(bm[:, tile(n)], net.ident[0:GV, h:h + 1].to_broadcast([GV, P]),
                               self.GT[:, tile(t)], start=True, stop=True)
        elif x == "k1":
            pe.wait_ge(*dve(4))
            for n in range(4):
                mm = pe.transpose(bm[:, tile(n)], self.U[i][:, n, :], net.ident[:, :])
        elif x[0] == "x":
            lev = int(x[1])
            pe.wait_ge(*pool(1 + 5 - lev))
            if lev == 5:
                pe.wait_ge(*act(2))
            else:
                pe.wait_ge(*dve(5 + 4 - lev))
            for n in range(4):
                mm = pe.matmul(bg[:, n * P:(n + 1) * P], self.ML[i][:, n, :], self.Tm[i][:, n, :],
                               start=True, stop=True)
        elif x[0] == "t":
            lev = int(x[1])
            s = LEVELS[lev]
            pe.wait_ge(*act(3 + 5 - lev))
            for n in range(4):
                if lev:
                    left = self.X[i][:, n, :].rearrange("p (b h r) -> p b h r", h=2, r=s)[:, :, 0, :]
                    pe.matmul(bm[:, n * 64:(n + 1) * 64], self.U[i][:, n, :], left, start=True, stop=True)
                right = self.U[i][:, n, :].rearrange("p (b h r) -> p b h r", h=2, r=s)[:, :, 1, :]
                mm = pe.matmul(bm[:, T + n * 64:T + (n + 1) * 64], self.X[i][:, n, :], right,
                               start=True, stop=True)
        elif x == "p0":
            pe.wait_ge(*dve(10))
            pe.wait_ge(*self.a3_act(self.vt_read(g)))
            for j in range(2):
                h = 2 * g + j
                mm = pe.matmul(bg[:, tile(j)], self.U[i][:, 2 * j, :], self.v[:, 0, h * P:(h + 1) * P],
                               start=True, stop=True)
        elif x == "p1":
            pe.wait_ge(*act(9))
            pe.wait_ge(*dve(11))
            for j in range(2):
                pe.matmul(bm[:, tile(j)], self.QK[i][:, 2 * j, :], self.vn[i][:, j, :], start=True, stop=True)
                mm = pe.matmul(bm[:, tile(2 + j)], self.kn[:, g, :], self.S[i][:, 2 + j, :],
                               start=True, stop=True)
        elif x == "p2":
            pe.wait_ge(*act(10))
            S = self.S[i][:, 0:2, :].rearrange("p j e -> p (j e)")
            pe.matmul(bg[:, 0:T], kT[:, tile(1)], S, start=True, stop=True)
            mm = pe.matmul(bg[:, T:2 * T], qT[:, tile(1)], S, start=True, stop=True)
        elif x == "p3":
            pe.wait_ge(*dve(12))
            for j in range(2):
                mm = pe.matmul(bm[:, tile(j)], self.U[i][:, 2 * j + 1, :], self.S[i][:, 2 + j, :],
                               start=True, stop=True)
        elif x == "p4":
            pe.wait_ge(*act(12))
            for j in range(2):
                mm = pe.matmul(bm[:, tile(2 + j)], self.QK[i][:, 2 * j + 1, :], self.vn[i][:, 2 + j, :],
                               start=True, stop=True)
        mm.then_inc(self.c_pe[i].sem, 1)

    def vt_read(self, g):
        step = ("vt", f"v{g // 2}", "1")
        n = self.a3.index(step)
        return len([x for x in self.a3[:n + 1] if x[0] != "conv"])

    def act(self, w):
        net, act = self.net, w.eng
        self.pre.act(w)
        self.pre.act_r(w)
        act.wait_ge(*self.pre.r_ready(1))
        for step in self.steps:
            kind = step[0]
            if kind in ("unit", "out"):
                if int(step[-1]) < 2:
                    w.split_hi(int(step[-1]))
            elif kind == "evac":
                c = step[1]
                n = self.evacs.index(c)
                act.wait_ge(net.unit_used, self.u0 + 2 * n + 1)
                if c == "ba":
                    dst = self.yba
                else:
                    dst = self.u[:, n % 2]
                    if c[0] == "z" and int(c[1]) >= 2:
                        act.wait_ge(*self.o_ready(int(c[1]) - 1))
                for tt in range(TT):
                    act.activation(dst[:, tt, :], net.A[(2 * n + tt) % 3][:, 0:dst.shape[2]], ACT.Copy,
                                   scale=net.r[:, tt:tt + 1]).then_inc(self.evacuated.sem, 1)
            elif kind == "ba":
                sem = self.ba["act"]
                if step[1] == "0":
                    act.wait_ge(*self.ba["dve"](1))
                    act.wait_ge(*self.small_loaded(48))
                    w.chain(act.activation(self.beta[:, :, :], self.beta[:, :, :], ACT.Exp, scale=-1.0))
                    w.chain(act.activation(self.beta[:, :, :], self.beta[:, :, :], ACT.Ln, bias=1.0))
                    w.chain(act.activation(self.beta[:, :, :], self.beta[:, :, :], ACT.Exp, scale=-1.0))
                    w.chain(act.activation(self.tb[:, :, :], self.g[:, :, :], ACT.Abs))
                    w.chain(act.activation(self.tb[:, :, :], self.tb[:, :, :], ACT.Exp, scale=-1.0))
                    w.chain.mark(act.activation(self.tb[:, :, :], self.tb[:, :, :], ACT.Ln, bias=1.0))
                    act.activation(self.a_row[:, :], self.a_row[:, :], ACT.Exp).then_inc(sem.sem, 1)
                elif step[1] == "1":
                    self.a3_ready(act, step)
                    act.activation(self.G[:, :, :], net.A[3][:, 0:TT * GV].rearrange("p (t h) -> p t h", t=TT),
                                   ACT.Copy).then_inc(self.a3_act.sem, 1)
                    act.wait_ge(*self.a3_act(1))
                    w.chain(act.activation(self.eG[:, :, :], self.G[:, :, :], ACT.Exp))
                    act.activation(self.neG[:, :, :], self.eG[:, :, :], ACT.Copy, scale=-1.0).then_inc(sem.sem, 1)
                elif step[1] == "2":
                    self.a3_ready(act, step)
                    w.chain.mark(act.activation(self.GT[:, :], net.A[3][0:GV, 0:T], ACT.Copy))
                    act.activation(self.tail[:, :], net.A[3][:, T:T + GV], ACT.Copy).then_inc(self.a3_act.sem, 1)
                elif step[1] == "3":
                    act.wait_ge(*self.ba["dve"](3))
                    act.activation(self.tail[:, :], self.tail[:, :], ACT.Exp).then_inc(sem.sem, 1)
            elif kind == "conv":
                c, part = step[1], int(step[2])
                self.a3_ready(act, step)
                n = self.silus.index(c)
                if n and part == 0:
                    before = self.silus[n - 1]
                    if before[0] == "v":
                        act.wait_ge(*self.a3_act(self.act_reads(("vt", before, "1"))))
                    else:
                        act.wait_ge(*self.l2(self.norms.index(("norm", before, "1")) + 1))
                for kk in range(2):
                    at = (self.width - 1) * self.ctiles + self.ctile(c) + 2 * part + kk
                    ins = act.activation(self.t[:, 2 * part + kk, :], net.A[3][:, kk * T:(kk + 1) * T],
                                         ACT.Copy, scale=self.taps[:, at:at + 1])
                ins.then_inc(self.tapped.sem, 1)
            elif kind == "silu":
                if step[2] == "0":
                    act.wait_ge(*self.clamped(self.silus.index(step[1]) + 1))
                    w.chain(act.activation(self.sg[:, :, :], self.sg[:, :, :], ACT.Exp, scale=-1.0))
                    w.chain.mark(act.activation(self.sg[:, :, :], self.sg[:, :, :], ACT.Ln, bias=1.0))
                elif step[2] == "1":
                    w.chain.sync()
                    act.activation(self.sg[:, :, :], self.sg[:, :, :], ACT.Exp, scale=-1.0)\
                       .then_inc(self.sigm.sem, 1)
            elif kind == "l2":
                act.wait_ge(*self.silued(self.silus.index(step[1]) + 1))
                act.activation(self.sg[:, :, :], self.t[:, :, :], ACT.Square).then_inc(self.squared.sem, 1)
            elif kind == "norm":
                self.a3_ready(act, step)
                half = self.sg[:, 2 * int(step[2]):2 * int(step[2]) + 2, :].rearrange("p k t -> p (k t)")
                act.activation(half, net.A[3][:, :], ACT.Ln, bias=EPS).then_inc(self.a3_act.sem, 1)
                act.wait_ge(*self.a3_act(self.act_reads(step)))
                act.activation(half, half, ACT.Exp, scale=-0.5).then_inc(self.rsq.sem, 1)
            elif kind == "kn":
                self.a3_ready(act, step)
                first = 4 * int(step[1][1])
                act.activation(self.kn[:, first:first + 4, :], net.A[3][:, :], ACT.Copy).then_inc(self.a3_act.sem, 1)
            elif kind == "vt":
                self.a3_ready(act, step)
                first = 512 * int(step[1][1])
                act.activation(self.v[:, int(step[2]), first:first + 512], net.A[3][:, :], ACT.Copy)\
                   .then_inc(self.a3_act.sem, 1)
            elif kind == "core":
                self.core_act(w, int(step[1]), step[2])
            elif kind == "z1":
                i = int(step[1][1])
                z = self.sg[:, :, :].rearrange("p (t k) n -> p t (k n)", t=TT)
                if step[2] == "0":
                    act.wait_ge(*self.z_clamped(i + 1))
                    w.chain(act.activation(z, z, ACT.Exp, scale=-1.0))
                    w.chain.mark(act.activation(z, z, ACT.Ln, bias=1.0))
                elif step[2] == "1":
                    w.chain.sync()
                    act.activation(z, z, ACT.Exp, scale=-1.0).then_inc(self.z_sigm.sem, 1)
            elif kind == "z2" and step[2] != "2":
                i, tt = int(step[1][1]), int(step[2])
                act.wait_ge(*self.o_sq(2 * i + tt + 1))
                ss = self.ss16[:, 4 * tt:4 * tt + 4]
                w.chain(act.activation(ss, ss, ACT.Ln, scale=1.0 / P, bias=EPS))
                act.activation(ss, ss, ACT.Exp, scale=-0.5).then_inc(self.o_r.sem, 1)
            elif kind == "ot":
                n = int(step[1])
                act.wait_ge(*self.o_turned(n + 1))
                at = 2 * (n % 4)
                act.activation(self.o_hi[n // 4][:, at:at + 2, :], self.ot_banks[n % 2 + 2 * (n >= 4)][:, :], ACT.Copy)\
                   .then_inc(self.o_hi_ready.sem, 1)
        self.post.act(w)

    def act_reads(self, step):
        n = self.a3.index(step)
        return len([x for x in self.a3[:n + 1] if x[0] != "conv"])

    def ctile(self, c):
        return {"q": 0, "k": GH, "v": 2 * GH}[c[0]] + 4 * int(c[1])

    def core_act(self, w, g, x):
        net, act = self.net, w.eng
        i = g % 2
        bg, bm = net.G[i], net.M[i]
        pe, dve = self.C("pe", g), self.C("dve", g)
        own = self.C("act", g)
        heads = slice(2 * g * P, (2 * g + 2) * P)
        tile = lambda t: slice(t * P, (t + 1) * P)
        if x == "k0":
            act.wait_ge(*dve(1))
            ins = act.activation(self.E[i][:, :, :], self.E[i][:, :, :], ACT.Exp)
        elif x == "k1":
            act.wait_ge(*pe(2))
            ins = act.activation(self.Tm[i][:, :, :], bm[:, :], ACT.Copy)
        elif x[0] == "x":
            act.wait_ge(*pe(3 + 2 * (5 - int(x[1]))))
            ins = act.activation(self.X[i][:, :, :], bg[:, :], ACT.Copy)
        elif x == "p0":
            act.wait_ge(*pe(15))
            for j in range(2):
                h = 2 * g + j
                ins = act.activation(self.vn[i][:, j, :], bg[:, tile(j)], ACT.Copy,
                                     scale=self.beta[:, 0, h:h + 1])
        elif x == "p1":
            act.wait_ge(*pe(16))
            w.chain.mark(act.activation(self.v[:, 0, heads], bm[:, 0:T], ACT.Copy))
            ins = act.activation(self.S[i][:, 0:2, :], bm[:, T:2 * T], ACT.Copy)
        elif x == "p2":
            act.wait_ge(*pe(17))
            act.wait_ge(*dve(12))
            for j in range(2):
                h = 2 * g + j
                ins = act.activation(self.qs[i][:, j, :], bg[:, tile(2 + j)], ACT.Copy,
                                     scale=self.eG[:, 1, h:h + 1])
        elif x == "p3":
            act.wait_ge(*pe(18))
            for j in range(2):
                h = 2 * g + j
                ins = act.activation(self.vn[i][:, 2 + j, :], bm[:, tile(j)], ACT.Copy,
                                     scale=self.beta[:, 1, h:h + 1])
        else:
            return
        ins.then_inc(self.c_act[i].sem, 1)

    def dve(self, w):
        net, dve = self.net, w.eng
        w.chain(dve.memset(self.ones[:, :], 1.0))
        dve.wait_ge(net.consts, net.masks_at)
        dve.tensor_reduce(self.strict[:, :], net.level_f[:, :, :].rearrange("p l c -> p c l"), AX.X, ALU.add)\
           .then_inc(self.ones_set.sem, 1)
        dve.wait_ge(*self.ones_set(1))
        dve.tensor_tensor(self.tri[:, :], self.strict[:, :], net.ident[:, :], ALU.add).then_inc(self.ones_set.sem, 1)
        dve.wait_ge(*self.ones_set(2))
        w.chain(dve.tensor_scalar(self.before[:, :], self.tri[:, :], 1.0, 1e30, ALU.subtract, ALU.mult))
        self.pre.dve(w)
        for step in self.steps:
            kind = step[0]
            if kind in ("unit", "out"):
                if int(step[-1]) >= 2:
                    w.split_lo(int(step[-1]) - 2)
            elif kind == "ba":
                sem = self.ba["dve"]
                if step[1] == "0":
                    dve.wait_ge(*self.evacuated(2))
                    dve.wait_ge(*self.small_loaded(48))
                    w.chain.mark(dve.tensor_scalar(self.beta[:, :, :], self.yba[:, :, 0:GV], CLAMP, None, ALU.max))
                    dve.tensor_tensor(self.g[:, :, :], self.yba[:, :, GV:2 * GV],
                                      self.dt_row[:, :].unsqueeze(1).to_broadcast([P, TT, GV]), ALU.add)\
                       .then_inc(sem.sem, 1)
                    dve.wait_ge(*self.ba["act"](1))
                    w.chain(dve.scalar_tensor_tensor(out=self.tb[:, :, :], in0=self.g[:, :, :], scalar=0.0,
                                                     in1=self.tb[:, :, :], op0=ALU.max, op1=ALU.add))
                    for t in range(TT):
                        ins = dve.scalar_tensor_tensor(out=self.g[:, t, :], in0=self.tb[:, t, :], scalar=-1.0,
                                                       in1=self.a_row[:, :], op0=ALU.mult, op1=ALU.mult)
                        if t == 0:
                            w.chain.mark(ins)
                    ins.then_inc(sem.sem, 1)
                elif step[1] == "2":
                    dve.wait_ge(*self.a3_act(self.act_reads(step)))
                    dve.tensor_tensor(self.tail[:, :], self.tail[:, :], self.G[:, 0, :], ALU.subtract)\
                       .then_inc(sem.sem, 1)
            elif kind == "conv":
                c, part = step[1], int(step[2])
                n = 2 * self.silus.index(c) + part
                dve.wait_ge(*self.tapped(n + 1))
                for back in range(1, self.width):
                    for kk in range(2):
                        at = (self.width - 1 - back) * self.ctiles + self.ctile(c) + 2 * part + kk
                        row = self.t[:, 2 * part + kk, back:T]
                        ins = dve.scalar_tensor_tensor(out=row, in0=net.A[3][:, kk * T:(kk + 1) * T - back],
                                                       scalar=self.taps[:, at:at + 1], in1=row,
                                                       op0=ALU.mult, op1=ALU.add)
                        if back == self.width - 1 and kk == 1:
                            ins.then_inc(self.a3_dve.sem, 1)
                        else:
                            w.chain.mark(ins)
                    if back < self.width - 1:
                        w.chain.sync()
                dve.wait_ge(*self.a3_dve(n + 1))
            elif kind == "silu":
                n = self.silus.index(step[1])
                if step[2] == "0":
                    if n and self.silus[n - 1][0] != "v":
                        dve.wait_ge(*self.l2(self.norms.index(("norm", self.silus[n - 1], "1")) + 1))
                    dve.tensor_scalar(self.sg[:, :, :], self.t[:, :, :], CLAMP, None, ALU.max)\
                       .then_inc(self.clamped.sem, 1)
                elif step[2] == "2":
                    dve.wait_ge(*self.sigm(n + 1))
                    dve.tensor_tensor(self.t[:, :, :], self.t[:, :, :], self.sg[:, :, :], ALU.mult)\
                       .then_inc(self.silued.sem, 1)
            elif kind == "norm":
                c, part = step[1], int(step[2])
                dve.wait_ge(*self.rsq(self.norms.index(step) + 1))
                half = slice(2 * part, 2 * part + 2)
                first = 4 * int(c[1]) + 2 * part
                dst = (self.qT if c[0] == "q" else self.kT)[:, first:first + 2, :].rearrange("p k t -> p (k t)")
                dve.scalar_tensor_tensor(out=dst, in0=self.t[:, half, :].rearrange("p k t -> p (k t)"),
                                         scalar=P ** -0.5 if c[0] == "q" else 1.0,
                                         in1=self.sg[:, half, :].rearrange("p k t -> p (k t)"),
                                         op0=ALU.mult, op1=ALU.mult).then_inc(self.l2.sem, 1)
            elif kind == "core":
                self.core_dve(w, int(step[1]), step[2])
            elif kind == "z1":
                i = int(step[1][1])
                n = self.evacs.index(step[1])
                z = self.sg[:, :, :].rearrange("p (t k) n -> p t (k n)", t=TT)
                u = self.u[:, n % 2]
                if step[2] == "0":
                    dve.wait_ge(*self.evacuated(2 * n + 2))
                    dve.wait_ge(*self.silued(len(self.silus)))
                    dve.tensor_scalar(z, u, CLAMP, None, ALU.max).then_inc(self.z_clamped.sem, 1)
                elif step[2] == "2":
                    dve.wait_ge(*self.z_sigm(i + 1))
                    w.chain(dve.tensor_tensor(u, u, z, ALU.mult))
                    uh = u.rearrange("p t (h e) -> p (t h) e", e=P)
                    w.chain.mark(dve.tensor_tensor(uh, uh, self.n_row[:, :].unsqueeze(1)
                                                   .to_broadcast([P, TT * 4, P]), ALU.mult))
            elif kind == "z2":
                i = int(step[1][1])
                n = self.evacs.index(step[1])
                u = self.u[:, n % 2]
                o = self.v[:, :, 512 * i:512 * (i + 1)]
                tt = int(step[2])
                w.chain.sync()
                if tt < 2:
                    for g in (2 * i, 2 * i + 1):
                        dve.wait_ge(*self.C("act", g)(10))
                        if tt:
                            dve.wait_ge(*self.C("dve", g)(13))
                    w.chain(dve.tensor_tensor(net.tmp[:, tt, :], o[:, tt, :], o[:, tt, :], ALU.mult))
                    dve.tensor_reduce(self.ss16[:, 4 * tt:4 * tt + 4],
                                      net.tmp[:, tt, :].rearrange("p (h e) -> p h e", e=P), AX.X, ALU.add)\
                       .then_inc(self.o_sq.sem, 1)
                else:
                    dve.wait_ge(*self.o_r(2 * i + 2))
                    for tt in range(TT):
                        for h in range(4):
                            cols = slice(h * P, (h + 1) * P)
                            ins = dve.scalar_tensor_tensor(out=o[:, tt, cols], in0=o[:, tt, cols],
                                                           scalar=self.ss16[:, 4 * tt + h:4 * tt + h + 1],
                                                           in1=u[:, tt, cols], op0=ALU.mult, op1=ALU.mult)
                            if tt * h < 3:
                                w.chain.mark(ins)
                    ins.then_inc(self.o_ready.sem, 1)
                    dve.wait_ge(*self.o_ready(i + 1))
            elif kind == "ot":
                n = int(step[1])
                dve.wait_ge(*self.o_hi_ready(n + 1))
                at = slice(2 * (n % 4), 2 * (n % 4) + 2)
                dve.tensor_tensor(self.o_lo[n // 4][:, at, :], self.ot_banks[n % 2 + 2 * (n >= 4)][:, :],
                                  self.o_hi[n // 4][:, at, :].bitcast(F32), ALU.subtract)\
                   .then_inc(self.o_lo_ready.sem, 1)
        self.post.dve(w)

    def core_dve(self, w, g, x):
        net, dve = self.net, w.eng
        i = g % 2
        bg, bm = net.G[i], net.M[i]
        pe, act, pool, own = (self.C(n, g) for n in ("pe", "act", "pool", "dve"))
        sem = self.c_dve[i]
        tile = lambda t: slice(t * P, (t + 1) * P)
        four = [(2 * g + j, t, 2 * j + t) for j in range(2) for t in range(TT)]
        if x == "k0":
            dve.wait_ge(*pe(1))
            if g >= 2:
                dve.wait_ge(*self.C("pool", g - 2)(6))
                dve.wait_ge(*self.C("pe", g - 2)(19))
            for h, t, n in four:
                ins = dve.scalar_tensor_tensor(out=self.E[i][:, n, :], in0=bm[:, tile(n)],
                                               scalar=self.G[:, t, h:h + 1], in1=self.before[:, :],
                                               op0=ALU.subtract, op1=ALU.min)
            ins.then_inc(sem.sem, 1)
            dve.wait_ge(*act(1))
            for h, t, n in four:
                ins = dve.scalar_tensor_tensor(out=self.MT[i][:, n, :], in0=bg[:, tile(t)],
                                               scalar=self.beta[:, t, h:h + 1], in1=self.E[i][:, n, :],
                                               op0=ALU.mult, op1=ALU.mult)
                if n < 3:
                    w.chain.mark(ins)
            ins.then_inc(sem.sem, 1)
            for j in range(2):
                ins = dve.tensor_tensor(self.QK[i][:, 2 * j:2 * j + 2, :], self.E[i][:, 2 * j:2 * j + 2, :],
                                        bg[:, T:2 * T].rearrange("p (t c) -> p t c", t=TT), ALU.mult)
                if j == 0:
                    w.chain.mark(ins)
            ins.then_inc(sem.sem, 1)
        elif x == "k1":
            dve.wait_ge(*own(2))
            w.chain(dve.tensor_tensor(self.U[i][:, :, :], self.MT[i][:, :, :],
                                      net.level_f[:, 6, :].unsqueeze(1).to_broadcast([P, 4, P]), ALU.mult))
            dve.tensor_tensor(self.U[i][:, :, :], net.ident[:, :].unsqueeze(1).to_broadcast([P, 4, P]),
                              self.U[i][:, :, :], ALU.subtract).then_inc(sem.sem, 1)
        elif x[0] == "t":
            lev = int(x[1])
            s = LEVELS[lev]
            dve.wait_ge(*pe(4 + 2 * (5 - lev)))

            def take(m, right, at):
                half = m[:, :, :].rearrange("p n c -> p (n c)")\
                    .rearrange("p (b h r) -> p b h r", h=2, r=s)[:, :, right, :]
                part = bm[:, at:at + T].rearrange("p (b r) -> p b r", r=s)
                return dve.tensor_tensor(half, half, part, ALU.subtract)
            dve.wait_ge(*own(4 + 5 - lev))
            if lev:
                w.chain.mark(take(self.Tm[i], 0, 0))
            take(self.U[i], 1, T).then_inc(sem.sem, 1)
        elif x == "p0":
            dve.wait_ge(*act(9))
            for j in range(2):
                h = 2 * g + j
                ins = dve.tensor_scalar(self.S[i][:, 2 + j, :], self.vn[i][:, j, :], self.tail[:, h:h + 1],
                                        None, ALU.mult)
                if j == 0:
                    w.chain.mark(ins)
            ins.then_inc(sem.sem, 1)
        elif x == "p2":
            dve.wait_ge(*pe(17))
            for j in range(2):
                h = 2 * g + j
                ins = dve.scalar_tensor_tensor(out=self.S[i][:, 2 + j, :], in0=bg[:, tile(j)],
                                               scalar=self.neG[:, 1, h:h + 1],
                                               in1=self.v[:, 1, h * P:(h + 1) * P], op0=ALU.mult, op1=ALU.add)
                if j == 0:
                    w.chain.mark(ins)
            ins.then_inc(sem.sem, 1)
        elif x == "p4":
            dve.wait_ge(*pe(19))
            dve.wait_ge(*act(11))
            dve.tensor_tensor(self.v[:, 1, 2 * g * P:(2 * g + 2) * P],
                              self.qs[i][:, 0:2, :].rearrange("p j e -> p (j e)"), bm[:, T:2 * T], ALU.add)\
               .then_inc(sem.sem, 1)


def program(nc, dram, out, only=None):
    with ExitStack() as ctx:
        net = Net(nc, ctx, dram)
        x_in, out_t = dram["x"][0].rearrange("(t p) d -> p t d", p=P), out[0].rearrange("(t p) d -> p t d", p=P)
        phases, before, brow_free = [], (net.x_in, 16, "columns"), None

        def gain(ap):
            return net.columns(ap.rearrange("(k p) -> k p", p=P))

        plan = only or ["block0", "block1", "ffn00", "conv", "ffn01", "ffn10", "gdn", "ffn11"]
        for what in plan:
            phase_ctx = ExitStack()
            if what.startswith("ffn"):
                i, s = int(what[3]), int(what[4])
                g = dram["norm_g_2"][i]
                ph = Ffn(net, what, dram["ffn_w_gate_up_2"][i, s], dram["ffn_w_down_2"][i, s],
                         gain(g[4 * s]), g[4 * s + 1], before, brow_free, what == plan[-1])
                brow_free = ph.x_ready
            elif what.startswith("block"):
                ph = Block(net, what, int(what[5]), dram, gain, before)
                ph.prev = phases[-1] if phases else None
                if not phases:
                    ph.x_before = None
            elif what == "conv":
                ph = Conv(net, what, dram, gain, before, brow_free)
                brow_free = ph.x_ready
            else:
                ph = Gdn(net, what, dram, gain, before, brow_free)
                brow_free = ph.x_ready
            with phase_ctx:
                net.ctx, net.prefix = phase_ctx, f"{what}_"
                ph.tensors(net)
            net.ctx = ctx
            before = (ph.x_ready, 1, "columns" if what.startswith("block") else "tokens")
            phases.append(ph)

        block = ctx.enter_context(nc.Block())

        @block.sync
        def _(sp):
            w = Walk(net, sp)
            sp.dma_start(net.x[:, :, 0:512], x_in[:, :, 0:512]).then_inc(net.x_in.sem, 16)
            sp.wait_ge(*net.x_in(16))
            sp.dma_start(net.x[:, :, 512:D], x_in[:, :, 512:D]).then_inc(net.x_in.sem, 16)
            for ph in phases:
                ph.sp(w)
            for c in range(2):
                sp.wait_ge(*before[0](c + 1))
                half = (slice(None), c) if before[2] == "tokens" else \
                    (slice(None), slice(None), slice(c * 512, (c + 1) * 512))
                sp.dma_start(out_t[half], net.x[half]).then_inc(net.out_done, 16)
            sp.wait_ge(net.out_done, 32)

        @block.gpsimd
        def _(pool):
            c = Chain(pool, net.consts)
            c(pool.memset(net.ident[:, :], 0.0))
            c(pool.affine_select(out=net.ident[:, :], in_=net.ident[:, :], compare_op=ALU.not_equal,
                                 fill=1.0, base=0, pattern=[[-1, P]], channel_multiplier=1))
            c(pool.memset(net.zeros[:, :], 0.0))
            early = [ph for ph in phases[:1] if isinstance(ph, Block)]
            for ph in early:
                ph.pool(pool)
            c(pool.memset(net.level_f[:, :, :], 0.0))
            for lev, s in enumerate(LEVELS):
                right = net.level_f[:, lev, :].rearrange("p (b h r) -> p b h r", h=2, r=s)[:, :, 1, :]
                c(pool.memset(right, 1.0))
                c(pool.affine_select(out=right, in_=right, compare_op=ALU.is_ge, fill=0.0, base=0,
                                     pattern=[[-2 * s, P // (2 * s)], [0, s]], channel_multiplier=1))
                c(pool.affine_select(out=right, in_=right, compare_op=ALU.is_ge, fill=0.0, base=s - 1,
                                     pattern=[[2 * s, P // (2 * s)], [0, s]], channel_multiplier=-1))
                for t in range(TT):
                    c.mark(pool.tensor_copy(
                        net.level_u8[:, lev, t * 64:(t + 1) * 64].rearrange("p (b r) -> p b r", r=s), right))
            for t in range(TT):
                c.mark(pool.tensor_copy(net.diag_u8[:, t * P:(t + 1) * P], net.ident[:, :]))
            c.mark(pool.iota(net.neg_dist[:, 0:P], [[1, P]], base=0, channel_multiplier=-1,
                             allow_small_or_imprecise_dtypes=True))
            c(pool.iota(net.neg_dist[:, P:P + T], [[1, T]], base=-P, channel_multiplier=-1,
                        allow_small_or_imprecise_dtypes=True))
            c.mark(pool.affine_select(out=net.neg_dist[:, 0:P], in_=net.neg_dist[:, 0:P],
                                      compare_op=ALU.is_ge, fill=-1e30, base=0, pattern=[[-1, P]],
                                      channel_multiplier=1))
            c(pool.affine_select(out=net.neg_dist[:, P:P + T], in_=net.neg_dist[:, P:P + T],
                                 compare_op=ALU.is_ge, fill=-1e30, base=P, pattern=[[-1, T]],
                                 channel_multiplier=1))
            net.masks_at = c.n
            for ph in phases[len(early):]:
                ph.pool(pool)

        @block.scalar
        def _(act):
            w = Walk(net, act, net.act_chain)
            act.preload_act_table_set("natural_log_exp_and_others")
            act.wait_ge(net.rows_clear, 1)
            for dst, src in net.row_loads:
                act.dma_start(dst, src).then_inc(net.params, 16)
            for _ in range(LEAD):
                w.split_hi()
            act.wait_ge(net.rows_turned, 1)
            act.activation(net.cols[:, :, :], net.M[1][:, 0:2 * P], ACT.Copy).then_inc(net.cols_ready, 1)
            act.wait_ge(net.cols_ready, 1)
            for ph in phases:
                ph.act(w)

        @block.vector
        def _(dve):
            w = Walk(net, dve, net.dve_chain)
            dve.memset(net.rows[:, :, :], 0.0).then_inc(net.rows_clear, 1)
            for _ in range(LEAD):
                w.split_lo()
            dve.wait_ge(net.cols_ready, 1)
            for ph in phases:
                ph.dve(w)

        @block.tensor
        def _(pe):
            w = Walk(net, pe)
            pe.wait_ge(net.consts, 3)
            pe.wait_ge(net.rows_clear, 1)
            pe.wait_ge(net.params, 16 * len(net.row_loads))
            for side in range(2):
                mm = pe.transpose(net.M[1][:, side * P:(side + 1) * P], net.rows[:, side, :], net.ident[:, :])
            mm.then_inc(net.rows_turned, 1)
            pe.wait_ge(net.cols_ready, 1)
            for ph in phases:
                ph.pe(w)


INPUTS = ["x", "mem", "g_pre", "w_in", "g_q_moba", "g_k_moba", "w_gate_up", "b_gate_up", "g_gla_out",
          "g_mem", "w_mem_kv", "g_q_mem", "g_k_mem", "w_out", "norm_g_2", "ffn_w_gate_up_2",
          "ffn_w_down_2", "sc_w_in_2", "sc_conv_w_2", "sc_w_out_2", "gdn_w_in_2", "gdn_conv_w_2",
          "gdn_a_log_2", "gdn_dt_bias_2", "gdn_norm_w_2", "gdn_w_out_2"]


def kernel(**inputs):
    import concourse.bacc as bacc
    from concourse.bass_utils import run_bass_kernel_spmd

    nc = bacc.Bacc("TRN2", target_bir_lowering=False, num_devices=1)
    arrays, dram = {}, {}
    for name in INPUTS:
        arrays[f"in_{name}"] = np.ascontiguousarray(inputs[name])
        dram[name] = nc.dram_tensor(f"in_{name}", arrays[f"in_{name}"].shape, F32, kind="ExternalInput").ap()
    out = nc.dram_tensor("out", (1, T, D), F32, kind="ExternalOutput").ap()
    program(nc, dram, out)
    return run_bass_kernel_spmd(nc, [arrays], core_ids=[0]).results[0]["out"]
```
